# Optimizing a Trainium2 kernel written in Bass

```python
import math
import jax, jax.numpy as jnp
from jax import lax
import numpy as np

D_MODEL = 1024
BATCH = 1
SEQ = 512
DEPTH = 1
DEC_BATCH = 8
DEC_SEQ = 4
PAST_LEN = 4096
PAGE_SIZE = 128

EPS = 1e-6
CONV_W = 4
RG_WIDTH = D_MODEL
RG_BLOCKS = 8
RG_BLOCK_W = RG_WIDTH // RG_BLOCKS
RG_C = 8.0
SSD_INNER = 2 * D_MODEL
SSD_HEADDIM = 64
SSD_HEADS = SSD_INNER // SSD_HEADDIM
SSD_GROUPS = 4
SSD_STATE = 128
SSD_GN = SSD_GROUPS * SSD_STATE
SSD_CONV_DIM = SSD_INNER + 2 * SSD_GN
SSD_CHUNK = 128
PEER_HEADS = 8
PEER_NKEYS = 128
PEER_EXPERTS = PEER_NKEYS * PEER_NKEYS
PEER_KEY_DIM = 256
PEER_HALF = PEER_KEY_DIM // 2
PEER_TOPK = 16
PEER_BLOCK = 128
IN_SIZES = (RG_WIDTH, RG_WIDTH, SSD_INNER, SSD_CONV_DIM, SSD_HEADS, 2 * D_MODEL)
IN_WIDTH = sum(IN_SIZES)
IN_SPLITS = [int(v) for v in np.cumsum(IN_SIZES)[:-1]]

kernel_name = 'hawk_ssd_peer_hybrid_step'

def rmsnorm(x, g):
    xf = x.astype(jnp.float32)
    y = xf * lax.rsqrt(jnp.mean(xf * xf, axis=-1, keepdims=True) + EPS) * g.astype(jnp.float32)
    return y.astype(x.dtype)

def causal_conv(u, buf, w, b):
    L = u.shape[1]
    padded = jnp.concatenate([buf.astype(u.dtype), u], axis=1)
    out = b.astype(u.dtype) + sum(padded[:, k:k + L] * w[k].astype(u.dtype) for k in range(CONV_W))
    return out, padded[:, L:]

def rg_lru(xc, h0, wa, ba, wx, bx, lam):
    B, L, _ = xc.shape
    xf = xc.astype(jnp.float32)
    xb = xf.reshape(B, L, RG_BLOCKS, RG_BLOCK_W)
    r = jax.nn.sigmoid(jnp.einsum('blhi,hij->blhj', xb, wa.astype(jnp.float32)).reshape(B, L, RG_WIDTH) + ba)
    i = jax.nn.sigmoid(jnp.einsum('blhi,hij->blhj', xb, wx.astype(jnp.float32)).reshape(B, L, RG_WIDTH) + bx)
    log_a = -RG_C * r * jax.nn.softplus(-lam.astype(jnp.float32))
    a = jnp.exp(log_a)
    bterm = jnp.sqrt(-jnp.expm1(2.0 * log_a)) * (i * xf)
    bterm = bterm.at[:, 0].add(a[:, 0] * h0.astype(jnp.float32))

    def combine(p, q):
        return p[0] * q[0], q[0] * p[1] + q[1]

    _, h = lax.associative_scan(combine, (a, bterm), axis=1)
    return h.astype(xc.dtype), h[:, -1]

def ssd_chunked(x, dt, A, Bm, Cm, h0):
    Bsz, L = x.shape[0], x.shape[1]
    Q = math.gcd(L, SSD_CHUNK)
    nc = L // Q
    G, R, P, N = SSD_GROUPS, SSD_HEADS // SSD_GROUPS, SSD_HEADDIM, SSD_STATE
    xs = x.astype(jnp.float32).reshape(Bsz, nc, Q, G, R, P)
    dts = dt.reshape(Bsz, nc, Q, G, R)
    Bs = Bm.astype(jnp.float32).reshape(Bsz, nc, Q, G, N)
    Cs = Cm.astype(jnp.float32).reshape(Bsz, nc, Q, G, N)
    acum = jnp.cumsum(dts * A.reshape(G, R), axis=2)
    seg = acum[:, :, :, None] - acum[:, :, None, :]
    mask = jnp.tril(jnp.ones((Q, Q), dtype=bool))[:, :, None, None]
    decay = jnp.exp(jnp.where(mask, seg, -jnp.inf))
    cb = jnp.einsum('bcign,bcjgn->bcijg', Cs, Bs)
    wgt = cb[..., None] * decay * dts[:, :, None]
    y_intra = jnp.einsum('bcijgr,bcjgrp->bcigrp', wgt, xs)
    last = acum[:, :, -1]
    to_end = jnp.exp(last[:, :, None] - acum) * dts
    S = jnp.einsum('bcjgrp,bcjgn->bcgrpn', to_end[..., None] * xs, Bs)
    chunk_decay = jnp.exp(last)

    def step(h, inp):
        s_c, d_c = inp
        return d_c[..., None, None] * h + s_c, h

    hT, h_starts = lax.scan(step, h0.astype(jnp.float32).reshape(Bsz, G, R, P, N),
                            (jnp.moveaxis(S, 1, 0), jnp.moveaxis(chunk_decay, 1, 0)))
    h_starts = jnp.moveaxis(h_starts, 0, 1)
    y_inter = jnp.einsum('bcign,bcgrpn->bcigrp', Cs, h_starts) * jnp.exp(acum)[..., None]
    y = (y_intra + y_inter).reshape(Bsz, L, SSD_HEADS, P)
    return y, hT.reshape(Bsz, SSD_HEADS, P, N)

def peer(h, w_q, sub_keys, u_emb, v_emb):
    shape = h.shape
    t = h.reshape(-1, D_MODEL)
    T = t.shape[0]
    blk = min(PEER_BLOCK, T)
    nb = -(-T // blk)
    t = jnp.pad(t, ((0, nb * blk - T), (0, 0))).reshape(nb, blk, D_MODEL)

    def block(tb):
        q = (tb @ w_q).reshape(blk, PEER_HEADS, 2, PEER_HALF)
        s = jnp.einsum('thsk,hsnk->thsn', q, sub_keys).astype(jnp.float32)
        sv, si = lax.top_k(s, PEER_TOPK)
        cand = sv[:, :, 0, :, None] + sv[:, :, 1, None, :]
        cand_idx = si[:, :, 0, :, None] * PEER_NKEYS + si[:, :, 1, None, :]
        fv, fi = lax.top_k(cand.reshape(blk, PEER_HEADS, PEER_TOPK * PEER_TOPK), PEER_TOPK)
        idx = jnp.take_along_axis(cand_idx.reshape(blk, PEER_HEADS, PEER_TOPK * PEER_TOPK), fi, axis=-1)
        g = jax.nn.softmax(fv, axis=-1)
        act = jax.nn.gelu(jnp.einsum('thkd,td->thk', u_emb[idx], tb).astype(jnp.float32))
        return jnp.einsum('thk,thkd->td', (g * act).astype(tb.dtype), v_emb[idx])

    out = lax.map(block, t).reshape(nb * blk, D_MODEL)[:T]
    return out.reshape(shape)

def trunk_layer(x, rg_h0, rg_buf, ssd_h0, ssd_buf,
                norm_mix, w_in, rg_conv_w, rg_conv_b, rg_wa, rg_ba, rg_wx, rg_bx, rg_lam, w_rg_out,
                ssd_conv_w, ssd_conv_b, ssd_dt_bias, ssd_a_log, ssd_d, ssd_norm, w_ssd_out, w_out,
                norm_ffn, peer_wq, peer_keys, peer_u, peer_v):
    Bsz, L = x.shape[0], x.shape[1]
    h = rmsnorm(x, norm_mix)
    proj = h @ w_in
    rg_x, rg_gate, ssd_z, ssd_xbc, ssd_dt, merge = jnp.split(proj, IN_SPLITS, axis=-1)
    rg_xc, new_rg_buf = causal_conv(rg_x, rg_buf, rg_conv_w, rg_conv_b)
    rg_y, new_rg_h = rg_lru(rg_xc, rg_h0, rg_wa, rg_ba, rg_wx, rg_bx, rg_lam)
    y_a = (rg_y * jax.nn.gelu(rg_gate)) @ w_rg_out
    xbc, new_ssd_buf = causal_conv(ssd_xbc, ssd_buf, ssd_conv_w, ssd_conv_b)
    xbc = jax.nn.silu(xbc)
    xs, bs, cs = jnp.split(xbc, [SSD_INNER, SSD_INNER + SSD_GN], axis=-1)
    xs = xs.reshape(Bsz, L, SSD_HEADS, SSD_HEADDIM)
    bs = bs.reshape(Bsz, L, SSD_GROUPS, SSD_STATE)
    cs = cs.reshape(Bsz, L, SSD_GROUPS, SSD_STATE)
    dt = jax.nn.softplus(ssd_dt.astype(jnp.float32) + ssd_dt_bias.astype(jnp.float32))
    A = -jnp.exp(ssd_a_log.astype(jnp.float32))
    y, new_ssd_h = ssd_chunked(xs, dt, A, bs, cs, ssd_h0)
    y = y + ssd_d.astype(jnp.float32)[:, None] * xs.astype(jnp.float32)
    y = y.reshape(Bsz, L, SSD_INNER) * jax.nn.silu(ssd_z.astype(jnp.float32))
    y_b = rmsnorm(y, ssd_norm).astype(x.dtype) @ w_ssd_out
    g_a, g_b = jnp.split(merge, 2, axis=-1)
    x = x + (jax.nn.sigmoid(g_a) * y_a + jax.nn.sigmoid(g_b) * y_b) @ w_out
    x = x + peer(rmsnorm(x, norm_ffn), peer_wq, peer_keys, peer_u, peer_v)
    return x, new_rg_h.astype(x.dtype), new_rg_buf, new_ssd_h.astype(x.dtype), new_ssd_buf

def setup_inputs(seed: int = 0) -> dict:
    key = jax.random.key(seed)
    ks = jax.random.split(key, 32)
    f32 = jnp.float32

    def nrm(k, shape, s):
        return jax.random.normal(k, shape, f32) * s

    Lz = DEPTH
    a8 = jax.random.uniform(ks[14], (Lz, RG_WIDTH), f32, minval=0.9, maxval=0.999)
    a = a8 ** (1.0 / RG_C)
    dt0 = jnp.exp(jax.random.uniform(ks[18], (Lz, SSD_HEADS), f32, minval=math.log(1e-3), maxval=math.log(1e-1)))
    return {
        'x_prompt': nrm(ks[0], (BATCH, SEQ, D_MODEL), 1.0),
        'x_sample': nrm(ks[1], (DEC_BATCH, DEC_SEQ, D_MODEL), 1.0),
        'state_rg_h': nrm(ks[2], (Lz, DEC_BATCH, RG_WIDTH), 0.5),
        'state_rg_conv': nrm(ks[3], (Lz, DEC_BATCH, CONV_W - 1, RG_WIDTH), 1.0),
        'state_ssd_h': nrm(ks[4], (Lz, DEC_BATCH, SSD_HEADS, SSD_HEADDIM, SSD_STATE), 0.1),
        'state_ssd_conv': nrm(ks[5], (Lz, DEC_BATCH, CONV_W - 1, SSD_CONV_DIM), 1.0),
        'norm_mix': 1.0 + nrm(ks[6], (Lz, D_MODEL), 0.02),
        'w_in': nrm(ks[7], (Lz, D_MODEL, IN_WIDTH), D_MODEL ** -0.5),
        'rg_conv_w': nrm(ks[8], (Lz, CONV_W, RG_WIDTH), CONV_W ** -0.5),
        'rg_conv_b': nrm(ks[9], (Lz, RG_WIDTH), 0.02),
        'rg_wa': nrm(ks[10], (Lz, RG_BLOCKS, RG_BLOCK_W, RG_BLOCK_W), RG_BLOCK_W ** -0.5),
        'rg_ba': nrm(ks[11], (Lz, RG_WIDTH), 0.02),
        'rg_wx': nrm(ks[12], (Lz, RG_BLOCKS, RG_BLOCK_W, RG_BLOCK_W), RG_BLOCK_W ** -0.5),
        'rg_bx': nrm(ks[13], (Lz, RG_WIDTH), 0.02),
        'rg_lam': jnp.log(a) - jnp.log1p(-a),
        'w_rg_out': nrm(ks[15], (Lz, RG_WIDTH, D_MODEL), RG_WIDTH ** -0.5),
        'ssd_conv_w': nrm(ks[16], (Lz, CONV_W, SSD_CONV_DIM), CONV_W ** -0.5),
        'ssd_conv_b': nrm(ks[17], (Lz, SSD_CONV_DIM), 0.02),
        'ssd_dt_bias': dt0 + jnp.log(-jnp.expm1(-dt0)),
        'ssd_a_log': jnp.log(jax.random.uniform(ks[19], (Lz, SSD_HEADS), f32, minval=1.0, maxval=16.0)),
        'ssd_d': 1.0 + nrm(ks[20], (Lz, SSD_HEADS), 0.02),
        'ssd_norm': 1.0 + nrm(ks[21], (Lz, SSD_INNER), 0.02),
        'w_ssd_out': nrm(ks[22], (Lz, SSD_INNER, D_MODEL), SSD_INNER ** -0.5),
        'w_out': nrm(ks[23], (Lz, D_MODEL, D_MODEL), D_MODEL ** -0.5),
        'norm_ffn': 1.0 + nrm(ks[24], (Lz, D_MODEL), 0.02),
        'peer_wq': nrm(ks[25], (Lz, D_MODEL, PEER_HEADS * PEER_KEY_DIM), D_MODEL ** -0.5),
        'peer_keys': nrm(ks[26], (Lz, PEER_HEADS, 2, PEER_NKEYS, PEER_HALF), PEER_HALF ** -0.5),
        'peer_u': nrm(ks[27], (Lz, PEER_EXPERTS, D_MODEL), D_MODEL ** -0.5),
        'peer_v': nrm(ks[28], (Lz, PEER_EXPERTS, D_MODEL), 0.3),
        'norm_final': 1.0 + nrm(ks[29], (D_MODEL,), 0.02),
    }

def reference(x_prompt, x_sample, state_rg_h, state_rg_conv, state_ssd_h, state_ssd_conv,
              norm_mix, w_in, rg_conv_w, rg_conv_b, rg_wa, rg_ba, rg_wx, rg_bx, rg_lam, w_rg_out,
              ssd_conv_w, ssd_conv_b, ssd_dt_bias, ssd_a_log, ssd_d, ssd_norm, w_ssd_out, w_out,
              norm_ffn, peer_wq, peer_keys, peer_u, peer_v, norm_final):
    yp, ys = x_prompt, x_sample
    dt_p = x_prompt.dtype
    p_rg_h, p_rg_c, p_ssd_h, p_ssd_c = [], [], [], []
    s_rg_h, s_rg_c, s_ssd_h, s_ssd_c = [], [], [], []
    for l in range(DEPTH):
        wl = (norm_mix[l], w_in[l], rg_conv_w[l], rg_conv_b[l], rg_wa[l], rg_ba[l], rg_wx[l], rg_bx[l],
              rg_lam[l], w_rg_out[l], ssd_conv_w[l], ssd_conv_b[l], ssd_dt_bias[l], ssd_a_log[l], ssd_d[l],
              ssd_norm[l], w_ssd_out[l], w_out[l], norm_ffn[l], peer_wq[l], peer_keys[l], peer_u[l], peer_v[l])
        yp, a1, a2, a3, a4 = trunk_layer(
            yp,
            jnp.zeros((BATCH, RG_WIDTH), dt_p),
            jnp.zeros((BATCH, CONV_W - 1, RG_WIDTH), dt_p),
            jnp.zeros((BATCH, SSD_HEADS, SSD_HEADDIM, SSD_STATE), dt_p),
            jnp.zeros((BATCH, CONV_W - 1, SSD_CONV_DIM), dt_p),
            *wl)
        ys, b1, b2, b3, b4 = trunk_layer(ys, state_rg_h[l], state_rg_conv[l], state_ssd_h[l], state_ssd_conv[l], *wl)
        p_rg_h.append(a1); p_rg_c.append(a2); p_ssd_h.append(a3); p_ssd_c.append(a4)
        s_rg_h.append(b1); s_rg_c.append(b2); s_ssd_h.append(b3); s_ssd_c.append(b4)
    y_prompt = rmsnorm(yp, norm_final)
    y_sample = rmsnorm(ys, norm_final)
    prompt_rg_h = jnp.stack(p_rg_h)
    prompt_rg_conv = jnp.stack(p_rg_c)
    prompt_ssd_h = jnp.stack(p_ssd_h)
    prompt_ssd_conv = jnp.stack(p_ssd_c)
    sample_rg_h = jnp.stack(s_rg_h)
    sample_rg_conv = jnp.stack(s_rg_c)
    sample_ssd_h = jnp.stack(s_ssd_h)
    sample_ssd_conv = jnp.stack(s_ssd_c)
    return (y_prompt, y_sample, prompt_rg_h, prompt_rg_conv, prompt_ssd_h, prompt_ssd_conv,
            sample_rg_h, sample_rg_conv, sample_ssd_h, sample_ssd_conv)


_drawn_inputs = setup_inputs


def setup_inputs(seed=0):
    import zlib

    import numpy as np

    out = dict(_drawn_inputs(seed))
    spreads = {}
    factors = {'rg_ba': 8.0,
     'rg_bx': 8.0,
     'ssd_d': 4.374,
     'ssd_norm': 3.362,
     'norm_ffn': 2.85,
     'norm_final': 2.92}
    for name, (base, spread) in spreads.items():
        noise = np.random.default_rng([zlib.crc32(name.encode()), seed]).standard_normal(out[name].shape)
        drawn = base * np.exp(spread * noise) if base else spread * noise
        out[name] = __import__('jax').numpy.asarray(drawn.astype(out[name].dtype))
    for name, factor in factors.items():
        out[name] = (out[name] * factor).astype(out[name].dtype)
    return out
```

```python
from contextlib import ExitStack

import numpy as np

import concourse.bass as bass
from concourse import mybir

F32 = mybir.dt.float32
U32 = mybir.dt.uint32
ALU = mybir.AluOpType
ACT = mybir.ActivationFunctionType
AX_X = mybir.AxisListType.X

P = 128
D_MODEL = 1024
SEQ = 512
DEC_B, DEC_L = 8, 4
DEC = DEC_B * DEC_L
TOK = SEQ + DEC
HALF = TOK // 2
EPS = 1e-6
CONV_W = 4
PAD = CONV_W - 1
KT = D_MODEL // P
INNER = 2 * D_MODEL
NH, HD, NG, NST = 32, 64, 4, 128
HPG = NH // NG
XB = INNER // P
CONVB = XB + 2 * NG
RGB = D_MODEL // P
CH = 128
NCH = SEQ // CH
TILES = NCH + 1
PH, NKEYS, TOPK = 8, 128, 16
HS = 2 * PH
EXPERTS = NKEYS * NKEYS
ROW = 2 * D_MODEL
NEG = -1e30
LOWEST = -3e38
GELU_C = 0.044715
GELU_S = float(np.sqrt(2.0 / np.pi))

RINGW = 4
U_XBC, U_Z, U_SO, U_GB, U_RG, U_GA, U_WO, U_WQ, UNITS = 0, 24, 40, 56, 64, 80, 96, 104, 120
O_XBC, O_Z, O_SO, O_GB, O_RG, O_GA, O_WO, O_WQ = 0, 24, 40, 48, 56, 72, 88, 96
SAMP0 = PAD + TOK
SEQW = PAD + DEC_L
CBW = SAMP0 + DEC_B * SEQW
CONVN = CBW - PAD

ITERS = NCH * 4 + 1
SLOTS = 2 * TOPK
RING = 8
GROUP = 4

_PARAMS = [("norm_mix", KT), ("norm_ffn", KT), ("ssd_norm", XB), ("ssd_d", XB), ("conv_w", CONVB * CONV_W),
           ("conv_b", CONVB), ("rg_conv_w", RGB * CONV_W), ("rg_conv_b", RGB), ("rg_ba", RGB), ("rg_bx", RGB),
           ("rg_lam", RGB), ("dt_bias", NH), ("a_log", NH)]
PCOL, NPAR = {}, 0
for _n, _w in _PARAMS:
    PCOL[_n] = (NPAR, _w)
    NPAR += _w
_CONSTS = [("ident", P), ("tri", P), ("mneg", P), ("ones", P), ("tri_s", DEC), ("mneg_s", DEC), ("blk_s", DEC),
           ("bcol", DEC_B), ("sel", DEC), ("iota", TOPK)]
CCOL, NCON = {}, 0
for _n, _w in _CONSTS:
    CCOL[_n] = (NCON, _w)
    NCON += _w


class Chain:

    def __init__(self, eng, sem):
        self.eng, self.sem, self.base, self.k, self.it, self.per = eng, sem, 0, 0, None, 0

    def value(self):
        if self.it is None:
            return self.base + self.k
        return self.it * self.per + (self.base + self.k)

    def step(self, ins):
        ins.then_inc(self.sem, 1)
        self.k += 1

    def wait(self):
        self.eng.wait_ge(self.sem, self.value())

    def link(self, ins):
        self.step(ins)
        self.wait()

    def enter(self, it, per):
        self.base += self.k
        self.k, self.it, self.per = 0, it, per

    def leave(self, n):
        assert self.k == self.per, f"steps in a pass: {self.k}, not {self.per}"
        self.base += n * self.per
        self.k, self.it = 0, None


def hybrid_layer(nc, a):
    with ExitStack() as ctx:
        def sb(name, shape, dt=F32):
            return ctx.enter_context(nc.sbuf_tensor("s_" + name, shape, dt))

        def sem(name):
            return ctx.enter_context(nc.semaphore(name))

        ps = ctx.enter_context(nc.psum_tensor("ps", [P, 8, 512], F32))

        WORK = 17472
        R1 = sb("r1", [P, 2 * KT * TOK])
        R2 = sb("r2", [P, CONVB * TOK])
        R3 = sb("r3", [P, RINGW * KT * P])
        R4 = sb("r4", [P, WORK])
        h0 = sb("h0", [P, 2, INNER])

        def view(region, at, *shape):
            v = region[:, at:at + int(np.prod(shape))]
            if len(shape) == 2:
                return v.rearrange("p (a b) -> p a b", b=shape[1])
            if len(shape) == 3:
                return v.rearrange("p (a b c) -> p a b c", b=shape[1], c=shape[2])
            return v

        def places(region, start, end, **shapes):
            out, at = {}, start
            for name, shape in shapes.items():
                out[name] = view(region, at, *shape)
                at += int(np.prod(shape))
            assert at <= end, (at, end)
            return out

        X = view(R1, 0, KT, TOK)
        HN = view(R1, KT * TOK, KT, TOK)
        wring = view(R3, 0, RINGW, KT, P)
        XBC = view(R2, 0, CONVB, TOK)
        M = XBC[:, XB:XB + KT, :]
        R = XBC[:, 0:KT, :]
        wax_all = view(R2, KT * TOK, RGB, 2, P)
        keys = view(R2, 2 * KT * TOK - HS * NKEYS, HS, NKEYS)
        X2T = view(R2, 0, TILES, D_MODEL)
        scs = R2[:, XB * TOK:XB * TOK + HS * NKEYS]
        rows = view(R2, XB * TOK + HS * NKEYS, 2, D_MODEL)
        w = places(R4, 0, WORK - 2 * TOK, sq=(KT, TOK), cb=(2, CBW), acc=(2, CBW), rs=(TOK,), gate=(2, TOK),
                   pool_t=(2, TOK), ssq=(TOK,), sp1=(168,), sp2=(168,), sp3=(168,), sp4=(168,), t=(2, TOK))
        sq, cb, acc, rs, gate, pool_t, ssq, tt = (w[k] for k in ("sq", "cb", "acc", "rs", "gate", "pool_t", "ssq", "t"))
        sp1, sp2, sp3, sp4 = (w[k] for k in ("sp1", "sp2", "sp3", "sp4"))
        x2b = view(R4, WORK - 2 * TOK, 2, TOK)
        w = places(R4, 0, KT * TOK, tr=(TOK,), ti=(TOK,), a=(TOK,), q=(TOK,), h=(TOK,), g=(TOK,), g2=(TOK,), g3=(TOK,))
        rg_tr, rg_ti, rg_a, rg_q, rg_h, rg_g, rg_g2, rg_g3 = w.values()
        w = places(R4, 0, WORK, st=(CONVB, CH), xdt=(INNER,), xs2=(INNER,), xd=(XB, CH), hT=(INNER,), bt=(NG * NST,),
                   cbs=(NG, CH), seg=(2, 512), dec=(2, 512), wgt=(2, 512), eas=(512,), yt=(512,), bm=(2, NG * NST))
        st, xdt, xs2, xd, hT, bt, cbs, seg, dec, wgt, eas, yt, bm = w.values()
        w = places(R4, 0, WORK - 2 * TOK, SC=(ITERS + 1, 512), H2T=(TILES, D_MODEL), tb=(D_MODEL,), diag=(4, P), eq=(2 * TOPK, TOPK))
        SC, H2T, tb, diag, tk_eq = w.values()
        h2s, qs = tb, x2b
        w = places(R4, WORK - 2 * TOK, WORK, s=(2, NKEYS), s2=(2, NKEYS), c=(TOPK * TOPK,), c2=(TOPK * TOPK,))
        tk_s, tk_s2, tk_c, tk_c2 = w.values()
        ring = [R1[:, i * ROW:(i + 1) * ROW] for i in range(4)] + [R3[:, i * ROW:(i + 1) * ROW] for i in range(2)] \
            + [h0[:, i, :] for i in range(2)]

        par, con = sb("par", [P, NPAR]), sb("con", [P, NCON])
        wdt = sb("wdt", [P, KT, NH])
        wax = sb("wax", [P, 2, 2, P])
        hist = sb("hist", [P, CONVB + RGB, DEC_B, PAD])
        rgh0 = sb("rgh0", [P, RGB, DEC_B])
        cst = sb("cst", [P, CONVB + RGB, (1 + DEC_B) * PAD])
        rgho = sb("rgho", [P, RGB, 1 + DEC_B])
        DT, DA = sb("DT", [P, TILES, NH]), sb("DA", [P, TILES, NH])
        half_b, ca, ea_log = sb("half_b", [P, 2 * RGB]), sb("ca", [P, RGB]), sb("ea_log", [P, NH])
        dtc, nac, el, ed = sb("dtc", [P, 2, NH]), sb("nac", [P, NH]), sb("el", [P, NH]), sb("ed", [P, NH])
        cdec, dam = sb("cdec", [P, DEC_B, NH]), sb("dam", [P, DEC_B, NH])
        epst = sb("epst", [P, 1])
        fss = sb("fss", [P, 2 * TILES])
        tk_v, tk_i, tk_if = sb("tk_v", [P, 2, TOPK]), sb("tk_i", [P, 2, TOPK], U32), sb("tk_if", [P, 2, TOPK])
        tk_fv, tk_fi = sb("tk_fv", [P, TOPK]), sb("tk_fi", [P, TOPK], U32)
        tk_ab, tk_abf = sb("tk_ab", [P, 2, TOPK], U32), sb("tk_abf", [P, 2, TOPK])
        tk_sel = sb("tk_sel", [P, 2, TOPK])
        tk_nm, tk_e, tk_sum, tk_r = sb("tk_nm", [P, 1]), sb("tk_e", [P, TOPK]), sb("tk_sum", [P, 1]), sb("tk_r", [P, 1])
        gidx, gw = sb("gidx", [P, 2, TOPK], U32), sb("gw", [P, 2, TOPK])
        act_z, slot_w = sb("act_z", [P, 2, TOPK]), sb("slot_w", [P, 2, TOPK])
        g1, g3, gth = sb("g1", [P, GROUP]), sb("g3", [P, GROUP]), sb("gth", [P, GROUP])

        def pc(name):
            o, n = PCOL[name]
            return par[:, o:o + n]

        def pcol(name, i, k=None):
            if k is None:
                return pc(name).unsqueeze(2)[:, i, :]
            return pc(name).rearrange("p (b k) -> p b k", k=CONV_W)[:, i, k:k + 1]

        def cc(name, n=P):
            o, m = CCOL[name]
            return con[0:n, o:o + m]

        ident, tri, ones = cc("ident"), cc("tri"), cc("ones")

        def halves(v):
            return v.rearrange("p (h t) -> p h t", h=2)

        def outb(p):
            return ps[:, 2 * p:2 * p + 2, 0:HALF]

        def bc(v, n):
            return v.unsqueeze(2).to_broadcast([v.shape[0], v.shape[1], n])

        def bc1(v, n):
            return v.unsqueeze(1).to_broadcast([v.shape[0], n, v.shape[1]])

        def seqs(v):
            return v[:, SAMP0:CBW].rearrange("p (b l) -> p b l", l=SEQW)

        ld_x, ld_c, ld_s, ld_late, ld_rows = sem("ld_x"), sem("ld_consts"), sem("ld_small"), sem("ld_late"), sem("ld_rows")
        w_full = [sem(f"w_full{i}") for i in range(RINGW)]
        unit_done = sem("unit_done")
        out_free = [sem("out_free0"), sem("out_free1")]
        dve_s, act_s, pool_s = sem("dve_steps"), sem("act_steps"), sem("pool_steps")
        sq_ready, stat_ready, root_ready, hn_ready = (sem(n) for n in ("sq_ready", "stat_ready", "root_ready", "hn_ready"))
        dt_mm, sp_in, sp_exp, dt_ready, set_ready = (sem(n) for n in ("dt_mm", "sp_in", "sp_exp", "dt_ready", "set_ready"))
        hist_in, conv_done, state_kept, xbc_ready = (sem(n) for n in ("hist_in", "conv_done", "state_kept", "xbc_ready"))
        st_ready, small_mm, small_sb, cb_mm, cb_sb = (sem(n) for n in ("st_ready", "small_mm", "small_sb", "cb_mm", "cb_sb"))
        tr_mm, tr_free_x, tr_free_b, ed_ready, xs2_ready = (
            sem(n) for n in ("tr_mm", "tr_free_x", "tr_free_b", "ed_ready", "xs2_ready"))
        ab_mm, seg_ready, dec_ready, wgt_ready, intra_mm = (
            sem(n) for n in ("ab_mm", "seg_ready", "dec_ready", "wgt_ready", "intra_mm"))
        inter_mm, eas_ready, y_done, s_mm, h_done, xd_ready = (
            sem(n) for n in ("inter_mm", "eas_ready", "y_done", "s_mm", "h_done", "xd_ready"))
        h0_in, h0_out = [sem("h0_in0"), sem("h0_in1")], [sem("h0_out0"), sem("h0_out1")]
        h0_dec, bm_ready, hT_out = sem("h0_decayed"), sem("bm_ready"), sem("hT_out")
        z_read, y_gated, ssq_ready, m_ready = (sem(n) for n in ("z_read", "y_gated", "ssq_ready", "m_ready"))
        wax_ready, ax_mm, rg_ri, rg_at, rg_arg, rg_root, g_in, g_u, g_th, r_ready = (
            sem(n) for n in ("wax_ready", "ax_mm", "rg_ri", "rg_at", "rg_arg", "rg_root", "g_in", "g_u", "g_th", "r_ready"))
        x2_ready, x2t_mm, x2t_ready, ss_ready, ss_root = (
            sem(n) for n in ("x2_ready", "x2t_mm", "x2t_ready", "ss_ready", "ss_root"))
        q_ready, sc_mm, sc_ready, sc_moved, h2t_ready, h2s_moved = (
            sem(n) for n in ("q_ready", "sc_mm", "sc_ready", "sc_moved", "h2t_ready", "h2s_moved"))
        fv_ready, ex_ready, idx_ready = sem("fv_ready"), sem("ex_ready"), sem("idx_ready")
        gath = [sem(f"gath{i}") for i in range(RING)]
        gl_in, gl_th, w_ready, diag_ready, slot_free, flushed = (
            sem(n) for n in ("gl_in", "gl_th", "w_ready", "diag_ready", "slot_free", "flushed"))
        fin_mm, fin_ready, stored = sem("fin_mm"), sem("fin_ready"), sem("stored")

        block = ctx.enter_context(nc.Block())

        @block.sync
        def _(sp):
            sp.dma_start(X, a["x"]).then_inc(ld_x, 16)
            sp.dma_start(con[:], a["consts"]).then_inc(ld_c, 16)
            sp.dma_start(par[:], a["params"]).then_inc(ld_c, 16)
            sp.dma_start(wdt[:], a["wdt"]).then_inc(ld_s, 16)
            for j in range(RINGW):
                sp.dma_start(wring[:, j], a["wstream"][j]).then_inc(w_full[j], 16)
            sp.dma_start(hist[:], a["hist"]).then_inc(ld_s, 16)
            sp.dma_start(rgh0[:], a["rgh0"]).then_inc(ld_s, 16)
            with sp.Fori(1, UNITS // RINGW) as i:
                for j in range(RINGW):
                    sp.wait_ge(unit_done, (i - 1) * RINGW + (j + 1))
                    sp.dma_start(wring[:, j], a["wstream"][i * RINGW + j]).then_inc(w_full[j], 16)
            sp.wait_ge(state_kept, CONVB + RGB)
            sp.wait_ge(r_ready, RGB)
            sp.dma_start(a["cst"], cst[:]).then_inc(stored, 16)
            sp.dma_start(a["rgho"], rgho[:]).then_inc(stored, 16)
            sp.wait_ge(sc_ready, HS)
            for q in range(4):
                sp.dma_start(SC[32 * q:32 * q + DEC, ITERS - 1, :],
                             scs[0:DEC, 512 * q:512 * (q + 1)]).then_inc(sc_moved, 16)
            sp.wait_ge(h2t_ready, 1)
            for q in range(4):
                sp.dma_start(H2T[32 * q:32 * q + DEC, TILES - 1, :], h2s[0:DEC, :]).then_inc(h2s_moved, 16)
            for i in range(TILES):
                sp.wait_ge(fin_ready, i + 1)
                if i < NCH:
                    sp.dma_start(a["y_prompt"][i * CH:(i + 1) * CH, :], X2T[:, i, :]).then_inc(stored, 16)
                else:
                    sp.dma_start(a["y_sample"], X2T[0:DEC, i, :]).then_inc(stored, 16)
            sp.wait_ge(stored, 16 * (2 + TILES))

        @block.tensor
        def _(pe):
            def unit(slot, p, rhs, fills, start=True, stop=True):
                pe.wait_ge(w_full[slot], fills * 16)
                for k in range(KT):
                    for h in range(2):
                        last = pe.matmul(ps[:, 2 * p + h, 0:HALF], wring[:, slot, k, :],
                                         rhs[:, k, h * HALF:(h + 1) * HALF],
                                         start=start and k == 0, stop=stop and k == KT - 1)
                last.then_inc(unit_done, 1)

            def plain_section(u0, o0, n_out, rhs):
                if o0 == 0:
                    for j in range(RINGW):
                        if j >= 2:
                            pe.wait_ge(out_free[j % 2], j // 2)
                        unit(j, j % 2, rhs, 1)
                with pe.Fori(1 if o0 == 0 else 0, n_out // RINGW) as i:
                    for j in range(RINGW):
                        pe.wait_ge(out_free[j % 2], i * 2 + (o0 + j) // 2)
                        unit(j, j % 2, rhs, i + (u0 // RINGW + 1))

            def stats(src, n):
                for k in range(n):
                    for h in range(2):
                        last = pe.matmul(ps[:, 4 + h, 0:HALF], ones, src[:, k, h * HALF:(h + 1) * HALF],
                                         start=k == 0, stop=k == n - 1)
                last.then_inc(stat_ready, 1)

            pe.wait_ge(ld_c, 32)
            pe.wait_ge(sq_ready, 1)
            stats(sq, KT)
            pe.wait_ge(hn_ready, 1)
            pe.wait_ge(ld_s, 16 * 3)
            for i in range(TILES):
                n = CH if i < NCH else DEC
                for k in range(KT):
                    last = pe.matmul(ps[0:n, 6, i * NH:(i + 1) * NH], HN[:, k, i * CH:i * CH + n], wdt[:, k, :],
                                     start=k == 0, stop=k == KT - 1)
            last.then_inc(dt_mm, 1)
            plain_section(U_XBC, O_XBC, CONVB, HN)

            pe.wait_ge(out_free[0], O_Z // 2)
            pe.wait_ge(out_free[1], O_Z // 2)
            pe.wait_ge(dt_ready, 1)
            pe.wait_ge(root_ready, 1)

            def pair_sums(v, k, at, m, sums):
                for o in range(2):
                    pe.matmul(ps[o * HD:(o + 1) * HD, 4, at:at + m],
                              v[:, 2 * k + o:2 * k + o + 1].to_broadcast([v.shape[0], HD]), sums, start=True, stop=True)

            def ssd_chunk(c, first):
                dac = dtc[:, 1, :]
                pe.wait_ge(st_ready, c + 1)
                if not first:
                    pe.wait_ge(ed_ready, c)
                    pe.wait_ge(small_sb, c)
                    pe.wait_ge(h_done, c * NG)
                pe.matmul(ps[:, 5, 0:NH], tri, dac, start=True, stop=True)
                pe.matmul(ps[:, 5, NH:2 * NH], ones, dac, start=True, stop=True).then_inc(small_mm, 1)
                for g in range(NG):
                    last = pe.matmul(ps[:, 7, g * CH:(g + 1) * CH], st[:, XB + g, :], st[:, XB + NG + g, :],
                                     start=True, stop=True)
                last.then_inc(cb_mm, 1)

                def acum_rows(hb):
                    if not (first and hb < 2):
                        pe.wait_ge(seg_ready, c * 8 + (hb - 1))
                    for k in range(4):
                        h = 4 * hb + k
                        last = pe.matmul(ps[:, hb % 2, k * CH:(k + 1) * CH], dac[:, h:h + 1].to_broadcast([P, P]),
                                         tri, start=True, stop=True)
                    last.then_inc(ab_mm, 1)

                def transposes(b):
                    if b >= 2:
                        pe.wait_ge(tr_free_x, c * 4 + (b - 1))
                    elif not first and b == 0:
                        pe.wait_ge(tr_free_b, c)
                    elif not first:
                        pe.wait_ge(y_done, c * NG)
                    for k in range(4):
                        last = pe.transpose(ps[:, 6 if b % 2 == 0 else 3, k * CH:(k + 1) * CH], st[:, 4 * b + k, :], ident)
                    last.then_inc(tr_mm, 1)

                def inter(g):
                    if g == 0:
                        pe.wait_ge(tr_free_x, c * 4 + 4)
                    if not (first and g == 0):
                        pe.wait_ge(y_done, c * NG + g)
                        pe.wait_ge(eas_ready, c * NG + g)
                        pe.wait_ge(h_done, c * NG)
                    for k in range(4):
                        pair_sums(dac, 4 * g + k, k * CH, CH, tri)
                    for k in range(4):
                        pr = 4 * g + k
                        last = pe.matmul(ps[:, 3, k * CH:(k + 1) * CH], hT[:, pr * P:(pr + 1) * P],
                                         st[:, XB + NG + g, :], start=True, stop=True)
                    last.then_inc(inter_mm, 1)

                def intra(hb):
                    pe.wait_ge(wgt_ready, c * 8 + (hb + 1))
                    if hb % 2 == 0 and not (first and hb == 0):
                        pe.wait_ge(y_done, c * NG + hb // 2)
                    for k in range(4):
                        h = 4 * hb + k
                        o, pr = (h % 2) * HD, (h % HPG) // 2
                        last = pe.matmul(ps[o:o + HD, 2, pr * CH:(pr + 1) * CH], xdt[:, h * HD:(h + 1) * HD],
                                         wgt[:, hb % 2, k * CH:(k + 1) * CH], start=True, stop=True)
                    last.then_inc(intra_mm, 1)

                acum_rows(0)
                transposes(0)
                transposes(1)
                acum_rows(1)
                transposes(2)
                transposes(3)
                transposes(4)
                inter(0)
                for g in range(NG):
                    intra(2 * g)
                    if g + 1 < NG:
                        acum_rows(2 * g + 2)
                    intra(2 * g + 1)
                    if g + 1 < NG:
                        acum_rows(2 * g + 3)
                    if g == 0:
                        pe.wait_ge(xs2_ready, c + 1)
                        pe.wait_ge(tr_free_b, c + 1)
                        pe.wait_ge(cb_sb, c + 1)
                    else:
                        pe.wait_ge(h_done, c * NG + g)
                    pe.matmul(ps[:, 7, :], bt[:, g * NST:(g + 1) * NST], xs2[:, g * 512:(g + 1) * 512],
                              start=True, stop=True).then_inc(s_mm, 1)
                    if g + 1 < NG:
                        inter(g + 1)

            ssd_chunk(0, True)
            with pe.Fori(1, NCH) as c:
                ssd_chunk(c, False)

            n = DEC
            dac = dtc[0:n, 1, :]
            tri_s, blk_s = cc("tri_s", n), cc("blk_s", n)
            pe.wait_ge(st_ready, NCH + 1)
            pe.wait_ge(ed_ready, NCH)
            pe.wait_ge(h_done, NCH * NG)
            pe.wait_ge(seg_ready, NCH * 8)
            pe.wait_ge(y_done, NCH * NG)
            pe.wait_ge(eas_ready, NCH * NG)
            pe.wait_ge(tr_free_b, NCH)
            pe.matmul(ps[0:n, 5, 0:NH], tri_s, dac, start=True, stop=True)
            pe.matmul(ps[0:n, 5, NH:2 * NH], blk_s, dac, start=True, stop=True)
            pe.matmul(ps[:, 5, 2 * NH:(2 + DEC_B) * NH], ones[0:n, :], dam[0:n].rearrange("p b h -> p (b h)"),
                      start=True, stop=True).then_inc(small_mm, 1)
            for g in range(NG):
                last = pe.matmul(ps[0:n, 7, g * n:(g + 1) * n], st[:, XB + g, 0:n], st[:, XB + NG + g, 0:n],
                                 start=True, stop=True)
            last.then_inc(cb_mm, 1)
            for hb in range(2):
                for k in range(16):
                    h = 16 * hb + k
                    last = pe.matmul(ps[0:n, hb, k * n:(k + 1) * n], dac[:, h:h + 1].to_broadcast([n, n]), tri_s,
                                     start=True, stop=True)
                last.then_inc(ab_mm, 1)
            for b in range(5):
                if b >= 2:
                    pe.wait_ge(tr_free_x, NCH * 4 + b - 1)
                for k in range(4):
                    last = pe.transpose(ps[0:n, 6 if b % 2 == 0 else 3, k * P:(k + 1) * P], st[:, 4 * b + k, 0:n], ident)
                last.then_inc(tr_mm, 1)
            for k in range(XB):
                pair_sums(dac, k, k * n, n, tri_s)
            for hb in range(2):
                pe.wait_ge(wgt_ready, NCH * 8 + hb + 1)
                for k in range(16):
                    h = 16 * hb + k
                    o = (h % 2) * HD
                    last = pe.matmul(ps[o:o + HD, 2, (h // 2) * n:(h // 2 + 1) * n], xdt[0:n, h * HD:(h + 1) * HD],
                                     wgt[0:n, hb, k * n:(k + 1) * n], start=True, stop=True)
                last.then_inc(intra_mm, 1)
            pe.wait_ge(tr_free_x, (NCH + 1) * 4)
            pe.wait_ge(tr_free_b, NCH + 1)
            pe.wait_ge(cb_sb, NCH + 1)
            pe.wait_ge(ed_ready, NCH + 1)
            pe.wait_ge(small_sb, NCH + 1)
            pe.wait_ge(eas_ready, NCH * NG + 1)
            pe.wait_ge(xs2_ready, NCH + 1)
            inter_out = ps[:, 3, :].rearrange("p (k b l) -> p k b l", b=DEC_B, l=DEC_L)
            with pe.Fori(0, DEC_B // 2) as i:
                for j in range(2):
                    pe.wait_ge(h0_in[j], i * 16 + 16)
                    for k in range(XB):
                        last = pe.matmul(inter_out[:, k, i * 2 + j, :], h0[:, j, k * P:(k + 1) * P],
                                         st[:, XB + NG + k // 4, 0:n].rearrange("p (b l) -> p b l", l=DEC_L)[:, i * 2 + j, :],
                                         start=True, stop=True)
                    last.then_inc(inter_mm, 1)
                    pe.wait_ge(bm_ready, i * 2 + (j + 1))
                    pe.wait_ge(h_done, i * 2 + (NCH * NG + j))
                    for g in range(NG):
                        last = pe.matmul(ps[:, 4 + g, :], bm[0:n, j, g * NST:(g + 1) * NST],
                                         xs2[0:n, g * 512:(g + 1) * 512], start=True, stop=True)
                    last.then_inc(s_mm, 1)
            pe.wait_ge(h_done, NCH * NG + DEC_B)
            pe.wait_ge(y_done, NCH * NG + 1)
            pe.wait_ge(seg_ready, NCH * 8 + 2)

            plain_section(U_Z, O_Z, XB, HN)
            pe.wait_ge(ssq_ready, XB)
            stats(ssq.unsqueeze(1), 1)
            pe.wait_ge(y_gated, XB)
            with pe.Fori(0, KT // 2) as i:
                for j in range(2):
                    pe.wait_ge(out_free[j], i + O_SO // 2)
                    for kk in range(2):
                        unit(2 * j + kk, j, XBC[:, KT * kk:KT * (kk + 1), :], i + (U_SO // RINGW + 1),
                             start=kk == 0, stop=kk == 1)
            plain_section(U_GB, O_GB, KT, HN)
            pe.wait_ge(root_ready, 2)

            def rg_products(i, j, first=False):
                for kk in range(2):
                    pe.wait_ge(out_free[kk], i * 2 + (O_RG // 2 + j))
                    unit(2 * j + kk, kk, HN, i + (U_RG // RINGW + 1))
                pe.wait_ge(wax_ready, i * 2 + (j + 1))
                pe.wait_ge(conv_done, i * 2 + (CONVB + j + 1))
                if not first:
                    pe.wait_ge(rg_ri, i * 4 + 2 * j)
                for m in range(2):
                    for h in range(2):
                        last = pe.matmul(ps[:, 4 + 2 * m + h, 0:HALF], wax[:, j, m, :],
                                         acc[:, j, h * HALF:(h + 1) * HALF], start=True, stop=True)
                last.then_inc(ax_mm, 1)

            rg_products(0, 0, True)
            rg_products(0, 1)
            with pe.Fori(1, RGB // 2) as i:
                for j in range(2):
                    rg_products(i, j)
            pe.wait_ge(r_ready, RGB)
            with pe.Fori(0, KT // 2) as i:
                for j in range(2):
                    for kk in range(2):
                        pe.wait_ge(out_free[kk], i * 2 + (O_GA // 2 + j))
                        unit(2 * j + kk, kk, HN if kk == 0 else R, i + (U_GA // RINGW + 1))
            pe.wait_ge(m_ready, 2 * KT)
            pe.wait_ge(rg_ri, 2 * RGB)

            def turn(b):
                p = b % 2
                pe.wait_ge(x2_ready, b + 1)
                if b >= 2:
                    pe.wait_ge(x2t_ready, 2 * b - 2)
                for i in range(NCH):
                    pe.transpose(ps[:, 4 + p, i * CH:(i + 1) * CH], x2b[:, p, i * CH:(i + 1) * CH], ident)
                pe.transpose(ps[0:DEC, 6 + p, 0:P], x2b[:, p, SEQ:TOK], ident).then_inc(x2t_mm, 1)

            for b in range(KT):
                pe.wait_ge(out_free[b % 2], (O_WO + b) // 2)
                unit(b % RINGW, b % 2, M, b // RINGW + U_WO // RINGW + 1)
                if b >= 1:
                    turn(b - 1)
            turn(KT - 1)
            pe.wait_ge(sq_ready, 2)
            pe.wait_ge(x2t_ready, 2 * KT)
            stats(sq, KT)
            pe.wait_ge(hn_ready, 2)
            pe.wait_ge(ld_late, 32)

            def scores(q, p, first=False):
                pe.wait_ge(q_ready, q + 1)
                if not first:
                    pe.wait_ge(sc_ready, q - 1)
                for i in range(NCH):
                    pe.matmul(ps[:, 4 + p, i * CH:(i + 1) * CH], qs[:, p, i * CH:(i + 1) * CH], keys[:, q, :],
                              start=True, stop=True)
                pe.matmul(ps[0:DEC, 6 + p, 0:NKEYS], qs[:, p, SEQ:TOK], keys[:, q, :],
                          start=True, stop=True).then_inc(sc_mm, 1)

            def query(i, j, first=False):
                if not first:
                    pe.wait_ge(q_ready, i * RINGW + (j - 1))
                unit(j, j % 2, HN, i + (U_WQ // RINGW + 1))

            pe.wait_ge(out_free[0], O_WQ // 2)
            pe.wait_ge(out_free[1], O_WQ // 2)
            query(0, 0, True)
            query(0, 1, True)
            scores(0, 0, True)
            query(0, 2)
            scores(1, 1, True)
            query(0, 3)
            scores(2, 0)
            with pe.Fori(1, HS // RINGW) as i:
                for j in range(RINGW):
                    query(i, j)
                    scores(i * RINGW + (j - 1), (j - 1) % 2)
            scores(HS - 1, 1)

            def experts(it):
                if isinstance(it, int):
                    pe.wait_ge(q_ready, HS)
                else:
                    pe.wait_ge(flushed, it)
                for s in range(SLOTS):
                    pe.wait_ge(diag_ready, it * SLOTS + (s + 1))
                    for h in range(2):
                        last = pe.matmul(ps[:, h, :], diag[:, s % 4, :],
                                         ring[s % RING][:, D_MODEL + 512 * h:D_MODEL + 512 * (h + 1)],
                                         start=s == 0, stop=s == SLOTS - 1)
                    last.then_inc(slot_free, 1)

            experts(0)
            with pe.Fori(1, ITERS) as it:
                experts(it)
            pe.wait_ge(flushed, ITERS)
            for h in range(2):
                last = pe.matmul(ps[0:DEC, 2 + h, :], cc("sel"), X2T[:, TILES - 1, 512 * h:512 * (h + 1)],
                                 start=True, stop=True)
            last.then_inc(fin_mm, 1)

        @block.scalar
        def _(act):
            ch = Chain(act, act_s)

            def root(src, dst, scale, done):
                act.activation(dst, src, ACT.Sqrt, bias=epst[:, 0:1], scale=scale).then_inc(done, 1)

            for j in range(2):
                act.dma_start(h0[:, j, :], a["sample_h_in"][j]).then_inc(h0_in[j], 16)
            act.wait_ge(ld_x, 16)
            act.activation(sq, X, ACT.Square).then_inc(sq_ready, 1)
            act.wait_ge(set_ready, 1)
            act.wait_ge(stat_ready, 1)
            root(ps[:, 4:6, 0:HALF], halves(rs), 1.0 / D_MODEL, root_ready)
            act.wait_ge(ld_c, 32)
            act.activation(ea_log[:], pc("a_log"), ACT.Exp).then_inc(sp_exp, 1)
            act.wait_ge(sp_in, 1)
            act.activation(sp2, sp3, ACT.Exp).then_inc(sp_exp, 1)

            def to_conv(n, p, u, banks, frees, first=False):
                act.wait_ge(unit_done, u)
                if not first:
                    act.wait_ge(conv_done, n - 1)
                    act.wait_ge(state_kept, n - 1)
                ch.step(act.activation(halves(cb[:, p, PAD:PAD + TOK]), outb(banks), ACT.Copy))
                act.activation(seqs(cb[:, p, :])[:, :, PAD:SEQW],
                               ps[:, 2 * banks + 1, SEQ - HALF:HALF].rearrange("p (b l) -> p b l", l=DEC_L),
                               ACT.Copy).then_inc(out_free[frees], 1)

            def silu_out(n, p):
                act.wait_ge(conv_done, n + 1)
                act.activation(XBC[:, n, :], acc[:, p, 0:TOK], ACT.Silu).then_inc(xbc_ready, 1)

            to_conv(0, 0, 1, 0, 0, True)
            to_conv(1, 1, 2, 1, 1, True)
            silu_out(0, 0)
            with act.Fori(1, CONVB // 2) as i:
                for j in range(2):
                    to_conv(i * 2 + j, j, i * 2 + (j + 1), j, j)
                    silu_out(i * 2 + (j - 1), (j - 1) % 2)
            silu_out(CONVB - 1, 1)

            def ssd_chunk(c, first):
                act.wait_ge(st_ready, c + 1)
                act.wait_ge(cb_mm, c + 1)
                if not first:
                    act.wait_ge(wgt_ready, c * 8)
                act.activation(cbs, ps[:, 7, :].rearrange("p (g t) -> p g t", t=CH), ACT.Copy).then_inc(cb_sb, 1)
                act.wait_ge(small_sb, c + 1)
                if not first:
                    act.wait_ge(xs2_ready, c)
                    act.wait_ge(h_done, c * NG)
                ch.step(act.activation(cdec[:, 0, :], ps[:, 5, NH:2 * NH], ACT.Exp))
                act.activation(ed[:], el[:], ACT.Exp).then_inc(ed_ready, 1)

                def decays(hb):
                    act.wait_ge(seg_ready, c * 8 + (hb + 1))
                    if not (first and hb < 2):
                        act.wait_ge(wgt_ready, c * 8 + (hb - 1))
                    for k in range(4):
                        last = act.activation(dec[:, hb % 2, k * CH:(k + 1) * CH], seg[:, hb % 2, k * CH:(k + 1) * CH],
                                              ACT.Exp, bias=nac[:, 4 * hb + k:4 * hb + k + 1])
                    last.then_inc(dec_ready, 1)

                decays(0)
                act.wait_ge(tr_mm, c * 5 + 5)
                if not first:
                    act.wait_ge(s_mm, c * NG)
                act.activation(bt, ps[:, 6, :], ACT.Copy).then_inc(tr_free_b, 1)
                for g in range(NG):
                    if g:
                        decays(2 * g)
                    act.wait_ge(inter_mm, c * NG + (g + 1))
                    if not (first and g == 0):
                        act.wait_ge(y_done, c * NG + g)
                    act.activation(eas, ps[:, 4, :], ACT.Exp).then_inc(eas_ready, 1)
                    decays(2 * g + 1)

            ssd_chunk(0, True)
            with act.Fori(1, NCH) as c:
                ssd_chunk(c, False)
            act.wait_ge(h_done, NCH * NG)
            act.dma_start(a["prompt_h"], hT).then_inc(hT_out, 16)
            n = DEC
            act.wait_ge(cb_mm, NCH + 1)
            act.wait_ge(wgt_ready, NCH * 8)
            act.activation(cbs[0:n, 0, 0:NG * n], ps[0:n, 7, 0:NG * n], ACT.Copy).then_inc(cb_sb, 1)
            act.wait_ge(small_sb, NCH + 1)
            act.wait_ge(xs2_ready, NCH)
            ch.step(act.activation(cdec[:], ps[:, 5, 2 * NH:(2 + DEC_B) * NH].rearrange("p (b h) -> p b h", h=NH), ACT.Exp))
            act.activation(ed[0:n, :], el[0:n, :], ACT.Exp).then_inc(ed_ready, 1)
            for hb in range(2):
                act.wait_ge(seg_ready, NCH * 8 + hb + 1)
                act.activation(dec[0:n, hb, :], seg[0:n, hb, :], ACT.Exp).then_inc(dec_ready, 1)
            act.wait_ge(tr_mm, NCH * 5 + 5)
            act.wait_ge(s_mm, NCH * NG)
            act.activation(bt[0:n, :], ps[0:n, 6, :], ACT.Copy).then_inc(tr_free_b, 1)
            act.wait_ge(intra_mm, NCH * 8 + 2)
            act.wait_ge(y_done, NCH * NG)
            act.activation(eas, ps[:, 4, :], ACT.Exp).then_inc(eas_ready, 1)

            def swap_state(b, j, fills, load=True):
                act.wait_ge(h_done, b + (NCH * NG + 1))
                act.dma_start(a["sample_h_out"][b], h0[:, j, :]).then_inc(h0_out[j], 16)
                if load:
                    act.wait_ge(h0_out[j], fills * 16)
                    act.dma_start(h0[:, j, :], a["sample_h_in"][b + 2]).then_inc(h0_in[j], 16)

            with act.Fori(0, DEC_B // 2 - 1) as i:
                for j in range(2):
                    swap_state(i * 2 + j, j, i + 1)
            for j in range(2):
                swap_state(DEC_B - 2 + j, j, 0, False)

            act.wait_ge(y_done, NCH * NG + 1)
            act.wait_ge(hT_out, 16)

            def z_block(b, j, first=False):
                act.wait_ge(unit_done, b + (U_Z + 1))
                if not first:
                    act.wait_ge(z_read, b - 1)
                    act.wait_ge(y_gated, b - 1)
                act.activation(halves(gate[:, j, :]), outb(j), ACT.Silu).then_inc(out_free[j], 1)

            z_block(0, 0, True)
            z_block(1, 1, True)
            with act.Fori(1, XB // 2) as i:
                for j in range(2):
                    z_block(i * 2 + j, j)
            act.wait_ge(stat_ready, 2)
            root(ps[:, 4:6, 0:HALF], halves(rs), 1.0 / INNER, root_ready)

            def b_gate(b, j, first=False):
                act.wait_ge(unit_done, b + (U_GB + 1))
                if first:
                    act.wait_ge(y_gated, XB)
                    act.wait_ge(z_read, XB)
                else:
                    act.wait_ge(m_ready, b - 1)
                act.activation(halves(gate[:, j, :]), outb(j), ACT.Tanh, scale=0.5).then_inc(out_free[j], 1)

            b_gate(0, 0, True)
            b_gate(1, 1, True)
            with act.Fori(1, KT // 2) as i:
                for j in range(2):
                    b_gate(i * 2 + j, j)

            act.wait_ge(unit_done, U_GB)
            act.dma_start(wax_all, a["wax"]).then_inc(ld_late, 16)
            act.dma_start(keys, a["keys"]).then_inc(ld_late, 16)

            def rg_block(b, j, first=False):
                to_conv(b + CONVB, j, b * 2 + (U_RG + 1), 0, 0)
                act.wait_ge(unit_done, b * 2 + (U_RG + 2))
                if not first:
                    act.wait_ge(r_ready, b)
                act.activation(halves(rg_g), outb(1), ACT.Copy).then_inc(out_free[1], 1)
                act.wait_ge(out_free[1], b + (O_RG // 2 + 1))
                act.activation(rg_g2, rg_g, ACT.Square).then_inc(g_in, 1)
                act.wait_ge(ax_mm, b + 1)
                act.activation(halves(rg_tr), ps[:, 4:6, 0:HALF], ACT.Tanh, scale=0.5,
                               bias=half_b[:].unsqueeze(2)[:, b, :]).then_inc(rg_ri, 1)
                act.activation(halves(rg_ti), ps[:, 6:8, 0:HALF], ACT.Tanh, scale=0.5,
                               bias=half_b[:, RGB:2 * RGB].unsqueeze(2)[:, b, :]).then_inc(rg_ri, 1)
                cab = ca[:].unsqueeze(2)[:, b, :]
                act.wait_ge(rg_ri, b * 2 + 2)
                ch.step(act.activation(rg_a, rg_tr, ACT.Exp, scale=cab, bias=cab))
                act.activation(rg_q, rg_tr, ACT.Tanh, scale=cab, bias=cab).then_inc(rg_at, 1)
                act.wait_ge(g_u, b + 1)
                act.activation(rg_g2, rg_g3, ACT.Tanh, scale=GELU_S).then_inc(g_th, 1)
                act.wait_ge(rg_arg, b + 1)
                act.activation(rg_q, tt[:, 0, :], ACT.Sqrt, scale=-0.25).then_inc(rg_root, 1)

            rg_block(0, 0, True)
            rg_block(1, 1)
            with act.Fori(1, RGB // 2) as i:
                for j in range(2):
                    rg_block(i * 2 + j, j)

            with act.Fori(0, KT) as b:
                act.wait_ge(unit_done, b * 2 + (U_GA + 1))
                act.wait_ge(m_ready, b + KT)
                act.activation(halves(gate[:, 0, :]), outb(0), ACT.Tanh, scale=0.5).then_inc(out_free[0], 1)

            act.wait_ge(set_ready, 3)
            for b in range(KT):
                p = b % 2
                act.wait_ge(x2_ready, b + 1)
                act.activation(X[:, b, :], x2b[:, p, :], ACT.Copy).then_inc(out_free[p], 1)
                act.wait_ge(x2t_mm, b + 1)
                act.activation(X2T[:, 0:NCH, b * P:(b + 1) * P], ps[:, 4 + p, :].rearrange("p (t d) -> p t d", d=P),
                               ACT.Copy).then_inc(x2t_ready, 1)
                act.activation(X2T[0:DEC, NCH, b * P:(b + 1) * P], ps[0:DEC, 6 + p, 0:P], ACT.Copy).then_inc(x2t_ready, 1)
            act.dma_start(rows, a["rows"]).then_inc(ld_rows, 16)
            act.wait_ge(out_free[1], O_WQ // 2)
            act.activation(sq, X, ACT.Square).then_inc(sq_ready, 1)
            act.wait_ge(stat_ready, 3)
            root(ps[:, 4:6, 0:HALF], halves(rs), 1.0 / D_MODEL, root_ready)

            def token_norms(base):
                for i in range(TILES):
                    m = CH if i < NCH else DEC
                    if base and i == NCH:
                        act.wait_ge(flushed, ITERS + 1)
                    act.activation(tb[0:m, :], X2T[0:m, i, :], ACT.Square, accum_out=fss[0:m, i:i + 1]).then_inc(ss_ready, 1)
                    act.wait_ge(ss_ready, base + i + 1)
                root(fss[:, 0:TILES], fss[:, TILES:2 * TILES], 1.0 / D_MODEL, ss_root)

            act.wait_ge(x2t_ready, 2 * KT)
            token_norms(0)

            act.wait_ge(hn_ready, 2)
            act.wait_ge(set_ready, 3)
            SCv = SC[:, 0:NCH * 4, :].rearrange("p (t r) (k n) -> p t (r k) n", r=4, n=NKEYS)
            scsv = scs.rearrange("p (q n) -> p q n", n=NKEYS)

            def keep_query(q, p, first=False):
                act.wait_ge(unit_done, q + (U_WQ + 1))
                if not first:
                    act.wait_ge(sc_mm, q - 1)
                act.activation(halves(qs[:, p, :]), outb(p), ACT.Copy).then_inc(q_ready, 1)

            def keep_scores(q, p):
                act.wait_ge(sc_mm, q + 1)
                for i in range(NCH):
                    ch.step(act.activation(SC[:, i * 4:(i + 1) * 4, :].rearrange("p r (k n) -> p (r k) n", n=NKEYS)[:, q, :],
                                           ps[:, 4 + p, i * NKEYS:(i + 1) * NKEYS], ACT.Copy))
                act.activation(scsv[0:DEC, q, :], ps[0:DEC, 6 + p, 0:NKEYS], ACT.Copy).then_inc(sc_ready, 1)

            keep_query(0, 0, True)
            keep_query(1, 1, True)
            keep_scores(0, 0)
            with act.Fori(1, HS // 2) as i:
                for j in range(2):
                    keep_query(i * 2 + j, j)
                    keep_scores(i * 2 + (j - 1), (j - 1) % 2)
            keep_scores(HS - 1, 1)

            def softmax_exp(h):
                act.wait_ge(fv_ready, h + 1)
                act.activation(tk_e[:], tk_fv[:], ACT.Exp, bias=tk_nm[:, 0:1], accum_out=tk_sum[:]).then_inc(ex_ready, 1)

            def groups(it, j):
                for q in range(TOPK // GROUP):
                    gi = it * (SLOTS // GROUP) + (j * (TOPK // GROUP) + q + 1)
                    act.wait_ge(gl_in, gi)
                    act.activation(gth[:], g3[:], ACT.Tanh, scale=GELU_S).then_inc(gl_th, 1)
                    act.wait_ge(w_ready, gi)
                    for s in range(GROUP):
                        sl = j * TOPK + q * GROUP + s
                        if not (isinstance(it, int) and sl < 4):
                            act.wait_ge(slot_free, it * SLOTS + (sl - 3))
                        act.activation(diag[:, s, :], ident, ACT.Copy,
                                       scale=slot_w[:, j, q * GROUP + s:q * GROUP + s + 1]).then_inc(diag_ready, 1)

            softmax_exp(0)
            softmax_exp(1)
            groups(0, 0)
            softmax_exp(2)
            groups(0, 1)
            with act.Fori(1, ITERS) as it:
                softmax_exp(it * 2 + 1)
                groups(it, 0)
                softmax_exp(it * 2 + 2)
                groups(it, 1)
            act.wait_ge(flushed, ITERS)
            token_norms(TILES)

        @block.gpsimd
        def _(pool):
            ch = Chain(pool, pool_s)
            ch.step(pool.memset(fss[:], 0.0))
            ch.step(pool.memset(cb[:, :, 0:PAD], 0.0))
            pool.memset(epst[:], EPS).then_inc(set_ready, 1)
            pool.wait_ge(ld_s, 16 * 3)

            def conv_side(n, p, frees, freed, first=False):
                if not first:
                    pool.wait_ge(conv_done, n - 1)
                pool.tensor_copy(seqs(cb[:, p, :])[:, :, 0:PAD], hist[:, n, :, :]).then_inc(hist_in, 1)
                pool.wait_ge(out_free[frees], freed)
                ch.step(pool.tensor_copy(cst[:, n, 0:PAD], cb[:, p, SEQ:PAD + SEQ]))
                pool.tensor_copy(cst[:, n, PAD:(1 + DEC_B) * PAD].rearrange("p (b l) -> p b l", l=PAD),
                                 seqs(cb[:, p, :])[:, :, DEC_L:SEQW]).then_inc(state_kept, 1)

            conv_side(0, 0, 0, 1, True)
            conv_side(1, 1, 1, 1, True)
            with pool.Fori(1, CONVB // 2) as i:
                ch.enter(i - 1, 2)
                for j in range(2):
                    conv_side(i * 2 + j, j, j, i + 1)
                ch.leave(CONVB // 2 - 1)

            pool.wait_ge(xbc_ready, CONVB)
            pool.wait_ge(dt_ready, 1)
            pool.memset(hT, 0.0).then_inc(set_ready, 1)

            def ssd_chunk(c, n, cols, first, sample=False):
                if not first:
                    pool.wait_ge(s_mm, c * NG)
                    pool.wait_ge(y_done, c * NG)
                ch.step(pool.tensor_copy(st[:, :, 0:n], cols))
                ch.step(pool.tensor_copy(dtc[0:n, 0, :], DT[0:n, c, :]))
                last = pool.tensor_copy(dtc[0:n, 1, :], DA[0:n, c, :])
                if sample:
                    ch.link(last)
                    last = pool.tensor_tensor(dam[0:n], bc1(dtc[0:n, 1, :], DEC_B), bc(cc("bcol", n), NH), ALU.mult)
                last.then_inc(st_ready, 1)
                pool.wait_ge(st_ready, c + 1)
                pool.tensor_tensor(xd[:, :, 0:n], st[:, 0:XB, 0:n], bc(pc("ssd_d"), n), ALU.mult).then_inc(xd_ready, 1)
                pool.wait_ge(ed_ready, c + 1)
                pool.wait_ge(tr_free_x, c * 4 + 4)
                pool.tensor_tensor(xs2[0:n].rearrange("p (h d) -> p h d", d=HD), xdt[0:n].rearrange("p (h d) -> p h d", d=HD),
                                   bc(ed[0:n, :], HD), ALU.mult).then_inc(xs2_ready, 1)

            chunked = XBC[:, :, 0:SEQ].rearrange("p k (c t) -> p k c t", t=CH)
            ssd_chunk(0, CH, chunked[:, :, 0, :], True)
            with pool.Fori(1, NCH) as c:
                ch.enter(c - 1, 2)
                ssd_chunk(c, CH, chunked[:, :, c, :], False)
                ch.leave(NCH - 1)
            n = DEC
            ssd_chunk(NCH, n, XBC[:, :, SEQ:TOK], False, True)
            pool.wait_ge(tr_free_b, NCH + 1)

            def sequence(b, j, first=False):
                if not first:
                    pool.wait_ge(s_mm, b + (NCH * NG - 1))
                pool.tensor_tensor(bm[0:n, j, :], bt[0:n, :], cc("bcol", n).unsqueeze(2)[:, b, :].to_broadcast([n, NG * NST]),
                                   ALU.mult).then_inc(bm_ready, 1)
                pool.wait_ge(inter_mm, b + (NCH * NG + 1))
                hv = h0[:, j, :].rearrange("p (h d) -> p h d", d=HD)
                pool.tensor_tensor(hv, hv, bc(cdec[:, b, :], HD), ALU.mult).then_inc(h0_dec, 1)

            sequence(0, 0, True)
            sequence(1, 1, True)
            with pool.Fori(1, DEC_B // 2) as i:
                for j in range(2):
                    sequence(i * 2 + j, j)

            pool.wait_ge(y_done, NCH * NG + 1)
            pool.wait_ge(hT_out, 16)
            pool.wait_ge(h_done, NCH * NG + DEC_B)
            ch.link(pool.memset(ssq, 0.0))

            def z_squares(i, j):
                b = i * 2 + j
                pool.wait_ge(out_free[j], i + (O_Z // 2 + 1))
                pool.tensor_tensor(pool_t[:, 0, :], gate[:, j, :], XBC[:, b, :], ALU.mult).then_inc(z_read, 1)
                pool.wait_ge(z_read, b + 1)
                ch.link(pool.tensor_tensor(pool_t[:, 1, :], pool_t[:, 0, :], pool_t[:, 0, :], ALU.mult))
                pool.tensor_tensor(ssq, ssq, pool_t[:, 1, :], ALU.add).then_inc(ssq_ready, 1)
                pool.wait_ge(ssq_ready, b + 1)

            with pool.Fori(0, XB // 2) as i:
                ch.enter(i, 2)
                for j in range(2):
                    z_squares(i, j)
                ch.leave(XB // 2)

            pool.wait_ge(ld_late, 16 * 2)
            ch.link(pool.memset(cb[:, :, 0:PAD], 0.0))

            def rg_side(b, j, first=False):
                if not first:
                    pool.wait_ge(ax_mm, b - 1)
                pool.tensor_copy(wax[:, j], wax_all[:, b]).then_inc(wax_ready, 1)
                conv_side(b + CONVB, j, 0, b + (O_RG // 2 + 1))

            rg_side(0, 0, True)
            rg_side(1, 1, True)
            with pool.Fori(1, RGB // 2) as i:
                ch.enter(i - 1, 2)
                for j in range(2):
                    rg_side(i * 2 + j, j)
                ch.leave(RGB // 2 - 1)
            pool.wait_ge(unit_done, U_WO)
            pool.memset(X2T[:, NCH, :], 0.0).then_inc(set_ready, 1)
            pool.wait_ge(hn_ready, 2)
            pool.memset(SC[:, ITERS, :], 0.0).then_inc(set_ready, 1)

            def gathers(it, j):
                pool.wait_ge(idx_ready, it * 2 + (j + 1))
                for s in range(TOPK):
                    sl = j * TOPK + s
                    if not (isinstance(it, int) and sl < RING):
                        pool.wait_ge(slot_free, it * SLOTS + (sl - RING + 1))
                        pool.nop(nofuse=True)
                    pool.indirect_dma_start(ring[sl % RING], None, a["uv"],
                                            bass.IndirectOffsetOnAxis(ap=gidx[:, j, s:s + 1], axis=0)
                                            ).then_inc(gath[sl % RING], 16)

            pool.wait_ge(unit_done, UNITS)
            gathers(0, 0)
            gathers(0, 1)
            with pool.Fori(1, ITERS) as it:
                gathers(it, 0)
                gathers(it, 1)

        @block.vector
        def _(dve):
            ch = Chain(dve, dve_s)

            def normalise(count):
                gain = "norm_mix" if count == 1 else "norm_ffn"
                dve.wait_ge(root_ready, 1 if count == 1 else 3)
                ch.link(dve.reciprocal(rs, rs))
                for k in range(KT):
                    last = dve.scalar_tensor_tensor(out=HN[:, k, :], in0=X[:, k, :], scalar=pcol(gain, k), in1=rs,
                                                    op0=ALU.mult, op1=ALU.mult)
                    if k < KT - 1:
                        ch.step(last)
                last.then_inc(hn_ready, 1)

            ch.step(dve.memset(sp1, 0.0))
            dve.wait_ge(ld_c, 32)
            normalise(1)
            dve.wait_ge(dt_mm, 1)
            ch.wait()
            nt = NCH * NH
            ch.step(dve.tensor_tensor(sp1[:, 0:nt].rearrange("p (t h) -> p t h", h=NH),
                                      ps[:, 6, 0:nt].rearrange("p (t h) -> p t h", h=NH), bc1(pc("dt_bias"), NCH), ALU.add))
            ch.step(dve.tensor_tensor(sp1[0:DEC, nt:nt + NH], ps[0:DEC, 6, nt:nt + NH], pc("dt_bias")[0:DEC, :], ALU.add))
            ch.link(dve.tensor_scalar(sp1[:, nt + NH:168], pc("rg_lam"), -1.0, None, ALU.mult))
            ch.link(dve.tensor_scalar(sp3, sp1, -1.0, None, ALU.mult))
            dve.tensor_tensor(sp3, sp3, sp1, ALU.min).then_inc(sp_in, 1)
            dve.wait_ge(sp_in, 1)
            dve.wait_ge(sp_exp, 2)
            ch.step(dve.tensor_scalar(sp1, sp1, 0.0, None, ALU.max))
            ch.link(dve.tensor_scalar(sp3, sp2, 2.0, None, ALU.add))
            ch.link(dve.reciprocal(sp3, sp3))
            ch.link(dve.tensor_tensor(sp2, sp2, sp3, ALU.mult))
            ch.link(dve.tensor_tensor(sp3, sp2, sp2, ALU.mult))
            ch.link(dve.tensor_scalar(sp4, sp3, 1.0 / 21, None, ALU.mult))
            for d in range(19, 1, -2):
                ch.link(dve.scalar_tensor_tensor(out=sp4, in0=sp4, scalar=1.0 / d, in1=sp3, op0=ALU.add, op1=ALU.mult))
            ch.link(dve.scalar_tensor_tensor(out=sp4, in0=sp4, scalar=1.0, in1=sp2, op0=ALU.add, op1=ALU.mult))
            ch.link(dve.scalar_tensor_tensor(out=sp4, in0=sp4, scalar=2.0, in1=sp1, op0=ALU.mult, op1=ALU.add))
            spt = sp4[:, 0:TILES * NH].rearrange("p (t h) -> p t h", h=NH)
            ch.step(dve.tensor_copy(DT[:], spt))
            ch.step(dve.scalar_tensor_tensor(out=DA[:], in0=spt, scalar=-1.0, in1=bc1(ea_log[:], TILES),
                                             op0=ALU.mult, op1=ALU.mult))
            ch.step(dve.tensor_scalar(ca[:], sp4[:, TILES * NH:168], -4.0, None, ALU.mult))
            ch.step(dve.tensor_scalar(half_b[:, 0:RGB], pc("rg_ba"), 0.5, None, ALU.mult))
            dve.tensor_scalar(half_b[:, RGB:2 * RGB], pc("rg_bx"), 0.5, None, ALU.mult).then_inc(dt_ready, 1)

            def conv(n, p, frees, freed, weights, bias, blk, guard):
                dve.wait_ge(out_free[frees], freed)
                dve.wait_ge(hist_in, n + 1)
                if guard is not None:
                    dve.wait_ge(*guard)
                row, o = cb[:, p, :], acc[:, p, 0:CONVN]
                ch.link(dve.tensor_scalar(o, row[:, PAD:CBW], pcol(weights, blk, PAD), pcol(bias, blk), ALU.mult, ALU.add))
                for k in range(PAD - 1, -1, -1):
                    ch.link(dve.scalar_tensor_tensor(out=o, in0=row[:, k:k + CONVN], scalar=pcol(weights, blk, k), in1=o,
                                                     op0=ALU.mult, op1=ALU.add))
                dve.tensor_copy(acc[:, p, SEQ:TOK].rearrange("p (b l) -> p b l", l=DEC_L),
                                seqs(acc[:, p, :])[:, :, 0:DEC_L]).then_inc(conv_done, 1)

            conv(0, 0, 0, 1, "conv_w", "conv_b", 0, None)
            conv(1, 1, 1, 1, "conv_w", "conv_b", 1, None)
            with dve.Fori(1, CONVB // 2) as i:
                ch.enter(i - 1, 8)
                for j in range(2):
                    n = i * 2 + j
                    conv(n, j, j, i + 1, "conv_w", "conv_b", n, (xbc_ready, i * 2 + (j - 1)))
                ch.leave(CONVB // 2 - 1)

            def ssd_chunk(c, first):
                dve.wait_ge(small_mm, c + 1)
                if not first:
                    dve.wait_ge(dec_ready, c * 8)
                    dve.wait_ge(ed_ready, c)
                ch.link(dve.tensor_scalar(nac[:], ps[:, 5, 0:NH], -1.0, None, ALU.mult))
                dve.tensor_tensor(el[:], ps[:, 5, NH:2 * NH], nac[:], ALU.add).then_inc(small_sb, 1)

                def segments(hb):
                    dve.wait_ge(ab_mm, c * 8 + (hb + 1))
                    if not (first and hb < 2):
                        dve.wait_ge(dec_ready, c * 8 + (hb - 1))
                    dve.tensor_tensor(seg[:, hb % 2, :].rearrange("p (k t) -> p k t", t=CH),
                                      ps[:, hb % 2, :].rearrange("p (k t) -> p k t", t=CH), bc1(cc("mneg"), 4),
                                      ALU.add).then_inc(seg_ready, 1)

                def weights(hb):
                    if hb == 0:
                        dve.wait_ge(cb_sb, c + 1)
                    dve.wait_ge(dec_ready, c * 8 + (hb + 1))
                    if not (first and hb < 2):
                        dve.wait_ge(intra_mm, c * 8 + (hb - 1))
                    dve.tensor_tensor(wgt[:, hb % 2, :].rearrange("p (k t) -> p k t", t=CH),
                                      dec[:, hb % 2, :].rearrange("p (k t) -> p k t", t=CH), bc1(cbs[:, hb // 2, :], 4),
                                      ALU.mult).then_inc(wgt_ready, 1)

                def scaled_x(b):
                    dve.wait_ge(tr_mm, c * 5 + (b + 1))
                    if b == 0 and not first:
                        dve.wait_ge(intra_mm, c * 8)
                        dve.wait_ge(xs2_ready, c)
                    dve.tensor_tensor(xdt[:, b * 512:(b + 1) * 512].rearrange("p (h d) -> p h d", d=HD),
                                      ps[:, 6 if b % 2 == 0 else 3, :].rearrange("p (h d) -> p h d", d=HD),
                                      bc(dtc[:, 0, 8 * b:8 * b + 8], HD), ALU.mult).then_inc(tr_free_x, 1)

                segments(0)
                scaled_x(0)
                scaled_x(1)
                segments(1)
                scaled_x(2)
                scaled_x(3)
                for g in range(NG):
                    weights(2 * g)
                    if g + 1 < NG:
                        segments(2 * g + 2)
                    weights(2 * g + 1)
                    if g + 1 < NG:
                        segments(2 * g + 3)
                    dve.wait_ge(eas_ready, c * NG + (g + 1))
                    dve.wait_ge(intra_mm, c * 8 + (2 * g + 2))
                    dve.wait_ge(xd_ready, c + 1)
                    ch.link(dve.tensor_tensor(yt, ps[:, 3, :], eas, ALU.mult))
                    ch.link(dve.tensor_tensor(yt, ps[:, 2, :], yt, ALU.add))
                    dve.tensor_tensor(XBC[:, 4 * g:4 * g + 4, 0:SEQ].rearrange("p k (c t) -> p k c t", t=CH)[:, :, c, :],
                                      yt.rearrange("p (k t) -> p k t", t=CH), xd[:, 4 * g:4 * g + 4, :],
                                      ALU.add).then_inc(y_done, 1)
                    dve.wait_ge(s_mm, c * NG + (g + 1))
                    hg = hT[:, g * 512:(g + 1) * 512]
                    ch.link(dve.tensor_tensor(hg.rearrange("p (h d) -> p h d", d=HD), hg.rearrange("p (h d) -> p h d", d=HD),
                                              bc(cdec[:, 0, 8 * g:8 * g + 8], HD), ALU.mult))
                    dve.tensor_tensor(hg, ps[:, 7, :], hg, ALU.add).then_inc(h_done, 1)

            dve.wait_ge(st_ready, 1)
            ssd_chunk(0, True)
            with dve.Fori(1, NCH) as c:
                ch.enter(c - 1, 13)
                ssd_chunk(c, False)
                ch.leave(NCH - 1)
            n = DEC
            dve.wait_ge(small_mm, NCH + 1)
            dve.wait_ge(dec_ready, NCH * 8)
            ch.link(dve.tensor_scalar(nac[0:n, :], ps[0:n, 5, 0:NH], -1.0, None, ALU.mult))
            dve.tensor_tensor(el[0:n, :], ps[0:n, 5, NH:2 * NH], nac[0:n, :], ALU.add).then_inc(small_sb, 1)
            for hb in range(2):
                sv = seg[0:n, hb, :].rearrange("p (k t) -> p k t", t=n)
                dve.wait_ge(ab_mm, NCH * 8 + hb + 1)
                ch.link(dve.tensor_tensor(sv, ps[0:n, hb, :].rearrange("p (k t) -> p k t", t=n), bc1(cc("mneg_s", n), 16),
                                          ALU.add))
                dve.tensor_tensor(sv, sv, bc(nac[0:n, 16 * hb:16 * hb + 16], n), ALU.add).then_inc(seg_ready, 1)
            for b in range(4):
                dve.wait_ge(tr_mm, NCH * 5 + b + 1)
                if b == 0:
                    dve.wait_ge(intra_mm, NCH * 8)
                    dve.wait_ge(xs2_ready, NCH)
                dve.tensor_tensor(xdt[0:n, b * 512:(b + 1) * 512].rearrange("p (h d) -> p h d", d=HD),
                                  ps[0:n, 6 if b % 2 == 0 else 3, :].rearrange("p (h d) -> p h d", d=HD),
                                  bc(dtc[0:n, 0, 8 * b:8 * b + 8], HD), ALU.mult).then_inc(tr_free_x, 1)
            dve.wait_ge(cb_sb, NCH + 1)
            for hb in range(2):
                dve.wait_ge(dec_ready, NCH * 8 + hb + 1)
                for k in range(2):
                    g = 2 * hb + k
                    last = dve.tensor_tensor(wgt[0:n, hb, k * 256:(k + 1) * 256].rearrange("p (k t) -> p k t", t=n),
                                             dec[0:n, hb, k * 256:(k + 1) * 256].rearrange("p (k t) -> p k t", t=n),
                                             bc1(cbs[0:n, 0, g * n:(g + 1) * n], 8), ALU.mult)
                    if k == 0:
                        ch.step(last)
                last.then_inc(wgt_ready, 1)

            def new_state(b, j):
                dve.wait_ge(h0_dec, b + 1)
                dve.wait_ge(s_mm, b + (NCH * NG + 1))
                hv = h0[:, j, :].rearrange("p (g d) -> p g d", d=512)
                dve.tensor_tensor(hv, ps[:, 4:8, :], hv, ALU.add).then_inc(h_done, 1)

            with dve.Fori(0, DEC_B // 2) as i:
                for j in range(2):
                    new_state(i * 2 + j, j)
            dve.wait_ge(inter_mm, NCH * NG + DEC_B)
            dve.wait_ge(eas_ready, NCH * NG + 1)
            dve.wait_ge(intra_mm, NCH * 8 + 2)
            dve.wait_ge(xd_ready, NCH + 1)
            ch.link(dve.tensor_tensor(yt, ps[:, 3, :], eas, ALU.mult))
            ch.link(dve.tensor_tensor(yt, ps[:, 2, :], yt, ALU.add))
            dve.tensor_tensor(XBC[:, 0:XB, SEQ:TOK], yt.rearrange("p (k t) -> p k t", t=n), xd[:, :, 0:n],
                              ALU.add).then_inc(y_done, 1)
            dve.wait_ge(y_done, NCH * NG + 1)
            dve.wait_ge(hT_out, 16)

            with dve.Fori(0, XB // 2) as i:
                for j in range(2):
                    b = i * 2 + j
                    dve.wait_ge(out_free[j], i + (O_Z // 2 + 1))
                    dve.wait_ge(z_read, b + 1)
                    dve.scalar_tensor_tensor(out=XBC[:, b, :], in0=gate[:, j, :], scalar=pcol("ssd_norm", b), in1=XBC[:, b, :],
                                             op0=ALU.mult, op1=ALU.mult).then_inc(y_gated, 1)
            dve.wait_ge(root_ready, 2)
            ch.link(dve.reciprocal(rs, rs))
            with dve.Fori(0, KT // 2) as i:
                for j in range(2):
                    dve.wait_ge(unit_done, i * 4 + (U_SO + 2 * j + 2))
                    dve.tensor_tensor(halves(M[:, i * 2 + j, :]), outb(j), halves(rs), ALU.mult).then_inc(out_free[j], 1)
            dve.wait_ge(out_free[1], O_GB // 2)
            with dve.Fori(0, KT // 2) as i:
                for j in range(2):
                    b = i * 2 + j
                    dve.wait_ge(out_free[j], i + (O_GB // 2 + 1))
                    dve.scalar_tensor_tensor(out=M[:, b, :], in0=gate[:, j, :], scalar=1.0, in1=M[:, b, :],
                                             op0=ALU.add, op1=ALU.mult).then_inc(m_ready, 1)

            def rg_block(b, j, guard):
                conv(b + CONVB, j, 0, b + (O_RG // 2 + 1), "rg_conv_w", "rg_conv_b", b, guard)
                dve.wait_ge(g_in, b + 1)
                ch.link(dve.tensor_scalar(rg_g3, rg_g2, GELU_C, 1.0, ALU.mult, ALU.add))
                dve.tensor_tensor(rg_g3, rg_g3, rg_g, ALU.mult).then_inc(g_u, 1)
                dve.wait_ge(rg_at, b + 1)
                ch.link(dve.tensor_tensor(tt[:, 0, :], rg_a, rg_a, ALU.mult))
                dve.scalar_tensor_tensor(out=tt[:, 0, :], in0=tt[:, 0, :], scalar=1.0, in1=rg_q,
                                         op0=ALU.add, op1=ALU.mult).then_inc(rg_arg, 1)
                dve.wait_ge(conv_done, b + (CONVB + 1))
                ch.link(dve.scalar_tensor_tensor(out=tt[:, 1, :], in0=rg_ti, scalar=1.0, in1=acc[:, j, 0:TOK],
                                                 op0=ALU.add, op1=ALU.mult))
                dve.wait_ge(rg_root, b + 1)
                ch.link(dve.tensor_tensor(tt[:, 1, :], tt[:, 1, :], rg_q, ALU.mult))
                a0 = rg_a[:, SEQ:TOK].rearrange("p (b l) -> p b l", l=DEC_L)[:, :, 0]
                b0 = tt[:, 1, SEQ:TOK].rearrange("p (b l) -> p b l", l=DEC_L)[:, :, 0]
                ch.link(dve.tensor_tensor(tt[:, 0, 0:DEC_B], a0, rgh0[:, b, :], ALU.mult))
                ch.link(dve.tensor_tensor(b0, b0, tt[:, 0, 0:DEC_B], ALU.add))
                ch.link(dve.memset(a0, 0.0))
                ch.link(dve.tensor_tensor_scan(rg_h, rg_a, tt[:, 1, :], 0.0, ALU.mult, ALU.add))
                ch.step(dve.tensor_copy(rgho[:, b, 0:1], rg_h[:, SEQ - 1:SEQ]))
                ch.step(dve.tensor_copy(rgho[:, b, 1:1 + DEC_B],
                                        rg_h[:, SEQ:TOK].rearrange("p (b l) -> p b l", l=DEC_L)[:, :, DEC_L - 1]))
                dve.wait_ge(g_th, b + 1)
                ch.link(dve.scalar_tensor_tensor(out=tt[:, 0, :], in0=rg_g2, scalar=1.0, in1=rg_g, op0=ALU.add, op1=ALU.mult))
                dve.tensor_tensor(R[:, b, :], tt[:, 0, :], rg_h, ALU.mult).then_inc(r_ready, 1)

            dve.wait_ge(m_ready, KT)
            rg_block(0, 0, None)
            rg_block(1, 1, None)
            with dve.Fori(1, RGB // 2) as i:
                ch.enter(i - 1, 2 * 15)
                for j in range(2):
                    rg_block(i * 2 + j, j, (ax_mm, i * 2 + (j - 1)))
                ch.leave(RGB // 2 - 1)
            dve.wait_ge(r_ready, RGB)
            with dve.Fori(0, KT) as b:
                dve.wait_ge(out_free[0], b + (O_GA // 2 + 1))
                dve.wait_ge(unit_done, b * 2 + (U_GA + 2))
                dve.scalar_tensor_tensor(out=halves(tt[:, 0, :]), in0=halves(gate[:, 0, :]), scalar=1.0, in1=outb(1),
                                         op0=ALU.add, op1=ALU.mult).then_inc(out_free[1], 1)
                dve.wait_ge(out_free[1], b + (O_GA // 2 + 1))
                dve.scalar_tensor_tensor(out=M[:, b, :], in0=tt[:, 0, :], scalar=0.5, in1=M[:, b, :],
                                         op0=ALU.mult, op1=ALU.add).then_inc(m_ready, 1)
                dve.wait_ge(m_ready, b + (KT + 1))
            for b in range(KT):
                p = b % 2
                dve.wait_ge(unit_done, U_WO + b + 1)
                if b >= 2:
                    dve.wait_ge(out_free[p], (O_WO + b) // 2)
                    dve.wait_ge(x2t_mm, b - 1)
                dve.scalar_tensor_tensor(out=halves(x2b[:, p, :]), in0=outb(p), scalar=0.5, in1=halves(X[:, b, :]),
                                         op0=ALU.mult, op1=ALU.add).then_inc(x2_ready, 1)
            normalise(2)
            dve.wait_ge(ss_root, 1)
            dve.wait_ge(ld_rows, 16)
            ch.link(dve.reciprocal(fss[:, TILES:2 * TILES], fss[:, TILES:2 * TILES]))
            for i in range(TILES):
                m = CH if i < NCH else DEC
                last = dve.scalar_tensor_tensor(out=H2T[:, i, :] if i < NCH else h2s[0:m, :], in0=X2T[0:m, i, :],
                                                scalar=fss[0:m, TILES + i:TILES + i + 1], in1=rows[0:m, 0, :],
                                                op0=ALU.mult, op1=ALU.mult)
                if i < NCH:
                    ch.step(last)
            last.then_inc(h2t_ready, 1)

            SCh = SC.rearrange("p t (j s n) -> p t j s n", j=2, n=NKEYS)

            def apart():
                dve.nop(nofuse=True)

            def top16(vals, idxs, src, src2):
                apart()
                ch.link(dve.max(vals[:, 0:8], src))
                apart()
                ch.step(dve.max_index(idxs[:, 0:8], vals[:, 0:8], src))
                ch.link(dve.match_replace(src2, vals[:, 0:8], src, LOWEST))
                apart()
                ch.link(dve.max(vals[:, 8:16], src2))
                apart()
                ch.link(dve.max_index(idxs[:, 8:16], vals[:, 8:16], src2))

            def route(it, j, h):
                ch.link(dve.tensor_copy(tk_s, SCh[:, it, j]))
                for s in range(2):
                    top16(tk_v[:, s, :], tk_i[:, s, :], tk_s[:, s, :], tk_s2[:, s, :])
                ch.step(dve.tensor_copy(tk_if[:], tk_i[:]))
                ch.link(dve.tensor_tensor(tk_c.rearrange("p (a b) -> p a b", b=TOPK), bc(tk_v[:, 0, :], TOPK),
                                          bc1(tk_v[:, 1, :], TOPK), ALU.add))
                top16(tk_fv[:], tk_fi[:], tk_c, tk_c2[:])
                dve.tensor_scalar(tk_nm[:], tk_fv[:, 0:1], -1.0, None, ALU.mult).then_inc(fv_ready, 1)
                ch.step(dve.tensor_scalar(tk_ab[:, 0, :], tk_fi[:], 4, None, ALU.logical_shift_right))
                ch.link(dve.tensor_scalar(tk_ab[:, 1, :], tk_fi[:], 15, None, ALU.bitwise_and))
                ch.link(dve.tensor_copy(tk_abf[:], tk_ab[:]))
                ch.link(dve.tensor_tensor(tk_eq, bc(tk_abf[:].rearrange("p s k -> p (s k)"), TOPK),
                                          bc1(cc("iota"), 2 * TOPK), ALU.is_equal))
                for s in range(2):
                    ev = tk_eq[:, s * TOPK:(s + 1) * TOPK, :]
                    ch.step(dve.tensor_tensor(ev, ev, bc1(tk_if[:, s, :], TOPK), ALU.mult))
                ch.wait()
                ch.link(dve.tensor_reduce(tk_sel[:].rearrange("p s k -> p (s k)"), tk_eq, AX_X, ALU.add))
                dve.scalar_tensor_tensor(out=gidx[:, j, :], in0=tk_sel[:, 0, :], scalar=float(NKEYS), in1=tk_sel[:, 1, :],
                                         op0=ALU.mult, op1=ALU.add).then_inc(idx_ready, 1)
                dve.wait_ge(ex_ready, h + 1)
                ch.link(dve.reciprocal(tk_r[:], tk_sum[:]))
                ch.link(dve.tensor_scalar(gw[:, j, :], tk_e[:], tk_r[:, 0:1], 0.5, ALU.mult, ALU.mult))

            ROUTE = 27

            def slots(it, j):
                for q in range(TOPK // GROUP):
                    gi = it * (SLOTS // GROUP) + (j * (TOPK // GROUP) + q + 1)
                    for s in range(GROUP):
                        k = q * GROUP + s
                        sl = j * TOPK + k
                        dve.wait_ge(gath[sl % RING], it * 64 + (sl // RING + 1) * 16)
                        u = ring[sl % RING][:, 0:D_MODEL]
                        ch.step(dve.tensor_tensor_reduce(out=u, in0=u, in1=tb, scale=1.0, scalar=0.0, op0=ALU.mult,
                                                         op1=ALU.add, accum_out=act_z[:, j, k:k + 1]))
                    ch.wait()
                    z = act_z[:, j, q * GROUP:(q + 1) * GROUP]
                    ch.link(dve.tensor_tensor(g1[:], z, z, ALU.mult))
                    ch.link(dve.tensor_scalar(g1[:], g1[:], GELU_C, 1.0, ALU.mult, ALU.add))
                    dve.tensor_tensor(g3[:], g1[:], z, ALU.mult).then_inc(gl_in, 1)
                    dve.wait_ge(gl_th, gi)
                    ch.link(dve.scalar_tensor_tensor(out=g1[:], in0=gth[:], scalar=1.0, in1=z, op0=ALU.add, op1=ALU.mult))
                    dve.tensor_tensor(slot_w[:, j, q * GROUP:(q + 1) * GROUP], g1[:], gw[:, j, q * GROUP:(q + 1) * GROUP],
                                      ALU.mult).then_inc(w_ready, 1)

            SLOTC = (TOPK // GROUP) * (GROUP + 3)

            def flush(it, tile):
                dve.wait_ge(slot_free, it * SLOTS + SLOTS if isinstance(it, int) else it * SLOTS)
                y = X2T[:, tile, :].rearrange("p (h d) -> p h d", h=2)
                dve.tensor_tensor(y, ps[:, 0:2, :], y, ALU.add).then_inc(flushed, 1)

            dve.wait_ge(sc_ready, HS)
            dve.wait_ge(sc_moved, 64)
            dve.wait_ge(set_ready, 4)
            route(0, 0, 0)
            dve.wait_ge(h2s_moved, 64)

            def iteration(it, tile, prev_tile):
                ch.link(dve.tensor_copy(tb, H2T[:, tile, :]))
                route(it, 1, it * 2 + 1)
                if prev_tile is not None:
                    flush(it, prev_tile)
                slots(it, 0)
                route(it + 1, 0, it * 2 + 2)
                slots(it, 1)

            iteration(0, 0, None)
            with dve.Fori(1, ITERS) as it:
                ch.enter(it - 1, 1 + 2 * (ROUTE + SLOTC))
                iteration(it, it // 4, (it - 1) // 4)
                ch.leave(ITERS - 1)
            flush(ITERS - 1, NCH)
            dve.wait_ge(fin_mm, 1)
            dve.tensor_copy(X2T[0:DEC, NCH, :].rearrange("p (h d) -> p h d", h=2), ps[0:DEC, 2:4, :]).then_inc(flushed, 1)
            dve.wait_ge(ss_root, 2)
            ch.link(dve.reciprocal(fss[:, TILES:2 * TILES], fss[:, TILES:2 * TILES]))
            for i in range(TILES):
                m = CH if i < NCH else DEC
                dve.scalar_tensor_tensor(out=X2T[0:m, i, :], in0=X2T[0:m, i, :], scalar=fss[0:m, TILES + i:TILES + i + 1],
                                         in1=rows[0:m, 1, :], op0=ALU.mult, op1=ALU.mult).then_inc(fin_ready, 1)


def _blocks(w, kb):
    i, o = w.shape
    return w.reshape(i // P // kb, kb, P, o // P, P).transpose(3, 0, 2, 1, 4)


def _chan(v):
    v = np.asarray(v)
    r = v.reshape(v.shape[:-1] + (v.shape[-1] // P, P))
    return np.moveaxis(np.moveaxis(r, -1, 0), -1, 1)


def _constants():
    c = np.zeros((P, NCON), np.float32)

    def put(name, v):
        o, w = CCOL[name]
        c[:v.shape[0], o:o + w] = v

    i, s = np.arange(P), np.arange(DEC)
    same = s[:, None] // DEC_L == s[None, :] // DEC_L
    put("ident", np.eye(P))
    put("tri", i[:, None] <= i[None, :])
    put("mneg", np.where(i[:, None] <= i[None, :], 0.0, NEG))
    put("ones", np.ones((P, P)))
    put("tri_s", same & (s[:, None] <= s[None, :]))
    put("mneg_s", np.where(same & (s[:, None] <= s[None, :]), 0.0, NEG))
    put("blk_s", same)
    put("bcol", s[:, None] // DEC_L == np.arange(DEC_B)[None, :])
    put("sel", i[:, None] % DEC == s[None, :])
    put("iota", np.broadcast_to(np.arange(TOPK), (P, TOPK)))
    return c


def kernel(**inputs):
    import concourse.bacc as bacc
    from concourse.bass_utils import run_bass_kernel_spmd

    g = {k: np.asarray(v) for k, v in inputs.items()}
    x = np.concatenate([g["x_prompt"][0], g["x_sample"].reshape(DEC, D_MODEL)], 0)
    w_in = g["w_in"][0]
    cuts = np.cumsum([0, RGB * P, RGB * P, INNER, CONVB * P, NH, D_MODEL, D_MODEL])
    rgx, rgg, z, xbc, dt, ga, gb = (w_in[:, cuts[i]:cuts[i + 1]] for i in range(7))
    b1 = {k: _blocks(v, KT)[:, 0] for k, v in dict(
        rgx=rgx, rgg=rgg, z=z, xbc=xbc, ga=ga, gb=gb, rgo=g["w_rg_out"][0], wo=g["w_out"][0], wq=g["peer_wq"][0]).items()}
    so = _blocks(g["w_ssd_out"][0], KT).reshape(2 * KT, P, KT, P)
    rg = np.stack([b1["rgx"], b1["rgg"]], 1).reshape(2 * KT, P, KT, P)
    gr = np.stack([b1["ga"], b1["rgo"]], 1).reshape(2 * KT, P, KT, P)
    arrays = {
        "wstream": np.concatenate([b1["xbc"], b1["z"], so, b1["gb"], rg, gr, b1["wo"], b1["wq"]], 0),
        "x": _chan(x),
        "consts": _constants(),
        "wdt": dt.reshape(KT, P, NH).transpose(1, 0, 2),
        "wax": np.stack([g["rg_wa"][0], g["rg_wx"][0]], 1).transpose(2, 0, 1, 3),
        "keys": g["peer_keys"][0].reshape(HS, NKEYS, P).transpose(2, 0, 1),
        "hist": np.concatenate([_chan(g["state_ssd_conv"][0]), _chan(g["state_rg_conv"][0])], 1),
        "rgh0": _chan(g["state_rg_h"][0]),
        "sample_h_in": g["state_ssd_h"][0].reshape(DEC_B, INNER, NST).transpose(0, 2, 1),
        "rows": np.broadcast_to(np.stack([g["norm_ffn"][0], g["norm_final"]]), (P, 2, D_MODEL)),
        "uv": np.concatenate([g["peer_u"][0], g["peer_v"][0]], 1),
    }
    par = {
        "norm_mix": _chan(g["norm_mix"][0]), "norm_ffn": _chan(g["norm_ffn"][0]), "ssd_norm": _chan(g["ssd_norm"][0]),
        "ssd_d": _chan(np.repeat(g["ssd_d"][0], HD)),
        "conv_w": _chan(g["ssd_conv_w"][0]), "conv_b": _chan(g["ssd_conv_b"][0]),
        "rg_conv_w": _chan(g["rg_conv_w"][0]), "rg_conv_b": _chan(g["rg_conv_b"][0]),
        "rg_ba": _chan(g["rg_ba"][0]), "rg_bx": _chan(g["rg_bx"][0]), "rg_lam": _chan(g["rg_lam"][0]),
        "dt_bias": np.broadcast_to(g["ssd_dt_bias"][0], (P, NH)), "a_log": np.broadcast_to(g["ssd_a_log"][0], (P, NH)),
    }
    arrays["params"] = np.concatenate([par[n].reshape(P, -1) for n, _ in _PARAMS], 1)

    outs = {"y_prompt": (SEQ, D_MODEL), "y_sample": (DEC, D_MODEL), "cst": (P, CONVB + RGB, (1 + DEC_B) * PAD),
            "rgho": (P, RGB, 1 + DEC_B), "prompt_h": (P, INNER), "sample_h_out": (DEC_B, P, INNER)}
    nc = bacc.Bacc("TRN2", target_bir_lowering=False, num_devices=1)
    aps = {}
    for k, v in arrays.items():
        arrays[k] = np.ascontiguousarray(v)
        aps[k] = nc.dram_tensor("in_" + k, v.shape, F32, kind="ExternalInput").ap()
    for k, s in outs.items():
        aps[k] = nc.dram_tensor("out_" + k, s, F32, kind="ExternalOutput").ap()
    hybrid_layer(nc, aps)
    r = run_bass_kernel_spmd(nc, [{"in_" + k: v for k, v in arrays.items()}], core_ids=[0]).results[0]
    o = {k: np.asarray(r["out_" + k]) for k in outs}

    def unchan(v):
        return np.moveaxis(np.moveaxis(v, 0, -1), 0, -2).reshape(v.shape[2:] + (-1,))

    hists, rgh = unchan(o["cst"]), unchan(o["rgho"])
    ssd_c, rg_c = hists[:, :CONVB * P], hists[:, CONVB * P:]
    return (
        o["y_prompt"][None], o["y_sample"].reshape(DEC_B, DEC_L, D_MODEL),
        rgh[None, 0:1], rg_c[None, None, 0:PAD],
        o["prompt_h"].T.reshape(1, 1, NH, HD, NST), ssd_c[None, None, 0:PAD],
        rgh[None, 1:], rg_c[PAD:].reshape(1, DEC_B, PAD, -1),
        o["sample_h_out"].transpose(0, 2, 1).reshape(1, DEC_B, NH, HD, NST), ssd_c[PAD:].reshape(1, DEC_B, PAD, -1),
    )
```

```python
from contextlib import ExitStack

import numpy as np

import concourse.bass as bass
from concourse import mybir

F32 = mybir.dt.float32
F32R = mybir.dt.float32r
U32 = mybir.dt.uint32
ALU = mybir.AluOpType
ACT = mybir.ActivationFunctionType
AX_X = mybir.AxisListType.X

P = 128
D_MODEL = 1024
SEQ = 512
DEC_B, DEC_L = 8, 4
DEC = DEC_B * DEC_L
TOK = SEQ + DEC
HALF = TOK // 2
EPS = 1e-6
CONV_W = 4
PAD = CONV_W - 1
KT = D_MODEL // P
INNER = 2 * D_MODEL
NH, HD, NG, NST = 32, 64, 4, 128
HPG = NH // NG
XB = INNER // P
CONVB = XB + 2 * NG
RGB = D_MODEL // P
CH = 128
NCH = SEQ // CH
TILES = NCH + 1
PH, NKEYS, TOPK = 8, 128, 16
HS = 2 * PH
EXPERTS = NKEYS * NKEYS
ROW = 2 * D_MODEL
NEG = -1e30
LOWEST = -3e38
GELU_C = 0.044715
GELU_S = float(np.sqrt(2.0 / np.pi))

RINGW = 4
U_XBC, U_GB, U_Z, U_SO, U_RG, U_GA, U_WO, U_WQ, UNITS = 0, 24, 32, 48, 64, 80, 96, 104, 120
O_XBC, O_Z, O_SO, O_RG, O_GA, O_WO, O_WQ = 0, 24, 40, 48, 64, 80, 88
SAMP0 = PAD + TOK
SEQW = PAD + DEC_L
CBW = SAMP0 + DEC_B * SEQW
CONVN = CBW - PAD

ITERS = NCH * 4 + 1
SLOTS = 2 * TOPK
RING = 8
GROUP = 2

_PARAMS = [("norm_mix", KT), ("norm_ffn", KT), ("ssd_norm", XB), ("ssd_d", XB), ("conv_w", CONVB * CONV_W),
           ("conv_b", CONVB), ("rg_conv_w", RGB * CONV_W), ("rg_conv_b", RGB), ("rg_ba", RGB), ("rg_bx", RGB),
           ("rg_lam", RGB), ("dt_bias", NH), ("a_log", NH)]
PCOL, NPAR = {}, 0
for _n, _w in _PARAMS:
    PCOL[_n] = (NPAR, _w)
    NPAR += _w
_CONSTS = [("ident", P), ("tri", P), ("mneg", P), ("ones", P), ("tri_s", DEC), ("mneg_s", DEC), ("blk_s", DEC),
           ("bcol", DEC_B), ("sel", DEC), ("iota", TOPK)]
CCOL, NCON = {}, 0
for _n, _w in _CONSTS:
    CCOL[_n] = (NCON, _w)
    NCON += _w


class Chain:

    def __init__(self, eng, sem):
        self.eng, self.sem, self.base, self.k, self.it, self.per = eng, sem, 0, 0, None, 0

    def value(self):
        if self.it is None:
            return self.base + self.k
        return self.it * self.per + (self.base + self.k)

    def step(self, ins):
        ins.then_inc(self.sem, 1)
        self.k += 1

    def wait(self):
        self.eng.wait_ge(self.sem, self.value())

    def link(self, ins):
        self.step(ins)
        self.wait()

    def enter(self, it, per):
        self.base += self.k
        self.k, self.it, self.per = 0, it, per

    def leave(self, n):
        assert self.k == self.per, f"steps in a pass: {self.k}, not {self.per}"
        self.base += n * self.per
        self.k, self.it = 0, None


def hybrid_layer(nc, a):
    with ExitStack() as ctx:
        def sb(name, shape, dt=F32):
            return ctx.enter_context(nc.sbuf_tensor("s_" + name, shape, dt))

        def sem(name):
            return ctx.enter_context(nc.semaphore(name))

        ps = ctx.enter_context(nc.psum_tensor("ps", [P, 8, 512], F32))

        WORK = 16448
        rounded = {}

        def region(name, n):
            t = sb(name, [P, n])
            rounded["s_" + name] = nc.alloc_sbuf_tensor_at("s_" + name + "_rounded", [P, n], F32R,
                                                           offset=nc.sbuf_base - 4 * n)
            return t

        R1 = region("r1", 2 * KT * TOK)
        R2 = region("r2", CONVB * TOK)
        R3 = region("r3", (RINGW + 2) * KT * P)
        R4 = region("r4", WORK)
        h0 = sb("h0", [P, 2, INNER])

        def view(region, at, *shape):
            v = region[:, at:at + int(np.prod(shape))]
            if len(shape) == 2:
                return v.rearrange("p (a b) -> p a b", b=shape[1])
            if len(shape) == 3:
                return v.rearrange("p (a b c) -> p a b c", b=shape[1], c=shape[2])
            return v

        def places(region, start, end, **shapes):
            out, at = {}, start
            for name, shape in shapes.items():
                out[name] = view(region, at, *shape)
                at += int(np.prod(shape))
            assert at <= end, (at, end)
            return out

        X = view(R1, 0, KT, TOK)
        HN = view(R1, KT * TOK, KT, TOK)
        wring = view(R3, 0, RINGW, KT, P)
        whi = view(R3, RINGW * KT * P, 2, KT, P)
        XBC = view(R2, 0, CONVB, TOK)
        M = XBC[:, XB:XB + KT, :]
        R = XBC[:, 0:KT, :]
        wax_all = view(R2, KT * TOK, RGB, 2, P)
        keys = view(R2, 2 * KT * TOK - HS * NKEYS, HS, NKEYS)
        X2T = view(R2, 0, TILES, D_MODEL)
        scs = R2[:, XB * TOK:XB * TOK + HS * NKEYS]
        rows = view(R2, XB * TOK + HS * NKEYS, 2, D_MODEL)
        LOW2 = WORK - KT * TOK
        w = places(R4, 0, LOW2, sq=(KT, TOK), cb=(2, CBW), acc=(2, CBW), rs=(TOK,), gate=(2, TOK),
                   yf=(2, TOK), ssq=(TOK,), t=(2, TOK))
        sq, cb, acc, rs, gate, yf, ssq, tt = w.values()
        w = places(R4, LOW2, WORK, sp1=(168,), sp2=(168,), sp3=(168,), sp4=(168,))
        sp1, sp2, sp3, sp4 = w.values()
        x2b = view(R4, WORK - 2 * TOK, 2, TOK)
        y_low = [sq, view(R4, LOW2, KT, TOK)]
        m_low, r_low = y_low
        w = places(R4, 0, KT * TOK, tr=(TOK,), ti=(TOK,), a=(TOK,), q=(TOK,), h=(TOK,), g3=(TOK,))
        rg_tr, rg_ti, rg_a, rg_q, rg_h, rg_g3 = w.values()
        rg_g, rg_g2 = gate, yf
        w = places(R4, 0, WORK, xdt=(INNER,), xs2=(INNER,), xd=(2, XB * CH), hT=(INNER,), bt=(NG * NST,),
                   cbs=(NG, CH), seg=(2, 512), dec=(2, 512), wgt=(2, 512), eas=(512,), yt=(512,))
        xdt, xs2, xd, hT, bt, cbs, seg, dec, wgt, eas, yt = w.values()
        bm = seg
        w = places(R4, 0, WORK - 2 * TOK, SC=(ITERS + 1, 512), H2T=(TILES, D_MODEL), tb=(D_MODEL,))
        SC, H2T, tb = w.values()
        h2s, qs = tb, x2b
        w = places(R2, TILES * D_MODEL, 2 * KT * TOK - HS * NKEYS, s=(2, NKEYS), s2=(2, NKEYS), c=(TOPK * TOPK,),
                   c2=(TOPK * TOPK,), eq=(2 * TOPK, TOPK))
        tk_s, tk_s2, tk_c, tk_c2, tk_eq = w.values()
        ring = [h0[:, i, :] for i in range(2)] + [R1[:, i * ROW:(i + 1) * ROW] for i in range(3)] \
            + [R3[:, i * ROW:(i + 1) * ROW] for i in range(3)]
        diag = view(R1, 3 * ROW, 4, P)

        par, con = sb("par", [P, NPAR]), sb("con", [P, NCON])
        wdt_all = region("wdt", 2 * KT * NH)
        wdt, wdt_hi = view(wdt_all, 0, KT, NH), view(wdt_all, KT * NH, KT, NH)
        wax = sb("wax", [P, 2, 2, P])
        hist = sb("hist", [P, CONVB + RGB, DEC_B, PAD])
        rgh0 = sb("rgh0", [P, RGB, DEC_B])
        hist_p = sb("hist_p", [P, CONVB + RGB, PAD])
        rgho = sb("rgho", [P, RGB, 1 + DEC_B])
        DT, DA = sb("DT", [P, TILES, NH]), sb("DA", [P, TILES, NH])
        half_b, ca, ea_log = sb("half_b", [P, 2 * RGB]), sb("ca", [P, RGB]), sb("ea_log", [P, NH])
        nac, el, ed = sb("nac", [P, NH]), sb("el", [P, NH]), sb("ed", [P, NH])
        c_s = sb("c_s", [P, NG, DEC])
        cdec, dam = sb("cdec", [P, DEC_B, NH]), sb("dam", [P, DEC_B, NH])
        epst = sb("epst", [P, 1])
        fss = sb("fss", [P, 2 * TILES])
        tk_v, tk_i, tk_if = sb("tk_v", [P, 2, TOPK]), sb("tk_i", [P, 2, TOPK], U32), sb("tk_if", [P, 2, TOPK])
        tk_fv, tk_fi = sb("tk_fv", [P, TOPK]), sb("tk_fi", [P, TOPK], U32)
        tk_ab, tk_abf = sb("tk_ab", [P, 2, TOPK], U32), sb("tk_abf", [P, 2, TOPK])
        tk_sel = sb("tk_sel", [P, 2, TOPK])
        tk_nm, tk_e, tk_sum, tk_r = sb("tk_nm", [P, 1]), sb("tk_e", [P, TOPK]), sb("tk_sum", [P, 1]), sb("tk_r", [P, 1])
        gidx, gw = sb("gidx", [P, 2, TOPK], U32), sb("gw", [P, 2, TOPK])
        act_z, slot_w = sb("act_z", [P, 2, TOPK]), sb("slot_w", [P, 2, TOPK])
        g1, g3, gth = sb("g1", [P, GROUP]), sb("g3", [P, GROUP]), sb("gth", [P, GROUP])

        def pc(name):
            o, n = PCOL[name]
            return par[:, o:o + n]

        def pcol(name, i, k=None):
            if k is None:
                return pc(name).unsqueeze(2)[:, i, :]
            return pc(name).rearrange("p (b k) -> p b k", k=CONV_W)[:, i, k:k + 1]

        def cc(name, n=P):
            o, m = CCOL[name]
            return con[0:n, o:o + m]

        ident, tri, ones = cc("ident"), cc("tri"), cc("ones")

        def first_pass(i):
            return isinstance(i, int) and i == 0

        def tokens(k, c):
            return XBC[:, k, c * CH:(c + 1) * CH if c < NCH else TOK]

        def halves(v):
            return v.rearrange("p (h t) -> p h t", h=2)

        def outb(p):
            return ps[:, 2 * p:2 * p + 2, 0:HALF]

        def bc(v, n):
            return v.unsqueeze(2).to_broadcast([v.shape[0], v.shape[1], n])

        def bc1(v, n):
            return v.unsqueeze(1).to_broadcast([v.shape[0], n, v.shape[1]])

        def seqs(v):
            return v[:, SAMP0:CBW].rearrange("p (b l) -> p b l", l=SEQW)

        def fr(v):
            return bass.AP(tensor=rounded[v.tensor.name], offset=v.offset, ap=v.ap)

        ld_x, ld_c, ld_s, ld_late, ld_rows = sem("ld_x"), sem("ld_consts"), sem("ld_small"), sem("ld_late"), sem("ld_rows")
        w_full = [sem(f"w_full{i}") for i in range(RINGW)]
        w_hi, w_lo, unit_done = sem("w_hi"), sem("w_lo"), sem("unit_done")
        xn_ready, hn_hi = sem("xn_ready"), sem("hn_hi")
        out_free = [sem("out_free0"), sem("out_free1")]
        dve_s, act_s, pool_s = sem("dve_steps"), sem("act_steps"), sem("pool_steps")
        sq_ready, stat_ready, root_ready, hn_ready = (sem(n) for n in ("sq_ready", "stat_ready", "root_ready", "hn_ready"))
        dt_mm, sp_in, sp_exp, dt_ready, set_ready = (sem(n) for n in ("dt_mm", "sp_in", "sp_exp", "dt_ready", "set_ready"))
        hist_in, conv_done, state_kept, xbc_ready = (sem(n) for n in ("hist_in", "conv_done", "state_kept", "xbc_ready"))
        samp_ready, small_mm, small_sb, cb_mm, cb_sb = (sem(n) for n in ("samp_ready", "small_mm", "small_sb", "cb_mm", "cb_sb"))
        tr_mm, tr_free_x, tr_free_b, ed_ready, xs2_ready = (
            sem(n) for n in ("tr_mm", "tr_free_x", "tr_free_b", "ed_ready", "xs2_ready"))
        ab_mm, seg_ready, dec_ready, wgt_ready, intra_mm = (
            sem(n) for n in ("ab_mm", "seg_ready", "dec_ready", "wgt_ready", "intra_mm"))
        inter_mm, eas_ready, y_done, s_mm, h_done, xd_ready = (
            sem(n) for n in ("inter_mm", "eas_ready", "y_done", "s_mm", "h_done", "xd_ready"))
        h0_in, h0_out = [sem("h0_in0"), sem("h0_in1")], [sem("h0_out0"), sem("h0_out1")]
        h0_dec, bm_ready, hT_out, gb_read = sem("h0_decayed"), sem("bm_ready"), sem("hT_out"), sem("gb_read")
        yg_ready, yf_ready, y_hi, y_gated, yg_sq, ssq_ready, m_ready = (
            sem(n) for n in ("yg_ready", "yf_ready", "y_hi", "y_gated", "yg_squared", "ssq_ready", "m_ready"))
        wax_ready, ax_mm, rg_ri, rg_at, rg_arg, rg_root, rg_scanned, g_in, g_u, g_th, r_ready = (
            sem(n) for n in ("wax_ready", "ax_mm", "rg_ri", "rg_at", "rg_arg", "rg_root", "rg_scanned", "g_in", "g_u", "g_th", "r_ready"))
        x2_ready, x2t_mm, x2t_ready, ss_ready, ss_root = (
            sem(n) for n in ("x2_ready", "x2t_mm", "x2t_ready", "ss_ready", "ss_root"))
        q_ready, sc_mm, sc_ready, sc_moved, h2t_ready, h2s_moved = (
            sem(n) for n in ("q_ready", "sc_mm", "sc_ready", "sc_moved", "h2t_ready", "h2s_moved"))
        fv_ready, ex_ready, idx_ready = sem("fv_ready"), sem("ex_ready"), sem("idx_ready")
        gath = [sem(f"gath{i}") for i in range(RING)]
        gl_in, gl_th, w_ready, diag_ready, slot_free, flushed = (
            sem(n) for n in ("gl_in", "gl_th", "w_ready", "diag_ready", "slot_free", "flushed"))
        fin_mm, fin_ready, stored = sem("fin_mm"), sem("fin_ready"), sem("stored")

        block = ctx.enter_context(nc.Block())

        @block.sync
        def _(sp):
            sp.dma_start(X, a["x"]).then_inc(ld_x, 16)
            sp.dma_start(con[:], a["consts"]).then_inc(ld_c, 16)
            sp.dma_start(par[:], a["params"]).then_inc(ld_c, 16)
            sp.dma_start(wdt, a["wdt"]).then_inc(ld_s, 16)
            for j in range(RINGW):
                sp.dma_start(wring[:, j], a["wstream"][j]).then_inc(w_full[j], 16)
            sp.dma_start(hist[:], a["hist"]).then_inc(ld_s, 16)
            sp.dma_start(rgh0[:], a["rgh0"]).then_inc(ld_s, 16)

            def refill(i):
                for j in range(RINGW):
                    sp.wait_ge(unit_done, (i - 1) * RINGW + (j + 1))
                    sp.dma_start(wring[:, j], a["wstream"][i * RINGW + j]).then_inc(w_full[j], 16)

            with sp.Fori(1, U_WO // RINGW + 1) as i:
                refill(i)
            sp.wait_ge(unit_done, U_WO)
            sp.dma_start(X, a["x"]).then_inc(ld_x, 16)
            with sp.Fori(U_WO // RINGW + 1, UNITS // RINGW) as i:
                refill(i)
            sp.wait_ge(state_kept, CONVB + RGB)
            sp.wait_ge(r_ready, RGB)
            sp.dma_start(a["hist_s"], hist[:].rearrange("p n b l -> p n (b l)")).then_inc(stored, 16)
            sp.dma_start(a["hist_p"], hist_p[:]).then_inc(stored, 16)
            sp.dma_start(a["rgho"], rgho[:]).then_inc(stored, 16)
            sp.wait_ge(h2t_ready, 1)
            for q in range(4):
                sp.dma_start(H2T[32 * q:32 * q + DEC, TILES - 1, :], h2s[0:DEC, :]).then_inc(h2s_moved, 16)
            sp.wait_ge(sc_ready, HS)
            for q in range(4):
                sp.dma_start(SC[32 * q:32 * q + DEC, ITERS - 1, :],
                             scs[0:DEC, 512 * q:512 * (q + 1)]).then_inc(sc_moved, 16)
            for i in range(TILES):
                sp.wait_ge(fin_ready, i + 1)
                if i < NCH:
                    sp.dma_start(a["y_prompt"][i * CH:(i + 1) * CH, :], X2T[:, i, :]).then_inc(stored, 16)
                else:
                    sp.dma_start(a["y_sample"], X2T[0:DEC, i, :]).then_inc(stored, 16)
            sp.wait_ge(stored, 16 * (3 + TILES))

        @block.tensor
        def _(pe):
            def unit(u, slot, p, rhs, start=True, stop=True):
                pe.wait_ge(w_lo, u + 1)
                w_high, w_low, (x_high, x_low) = whi[:, slot % 2], wring[:, slot], rhs
                for k in range(KT):
                    for t, (wp, xp) in enumerate(((w_high, x_high), (w_high, x_low), (w_low, x_high))):
                        for h in range(2):
                            last = pe.matmul(ps[:, 2 * p + h, 0:HALF], fr(wp[:, k, :]),
                                             fr(xp[:, k, h * HALF:(h + 1) * HALF]),
                                             start=start and k == 0 and t == 0, stop=stop and k == KT - 1 and t == 2)
                last.then_inc(unit_done, 1)

            def plain_section(u0, o0, n_out, rhs):
                if o0 == 0:
                    for j in range(RINGW):
                        if j >= 2:
                            pe.wait_ge(out_free[j % 2], j // 2)
                        unit(u0 + j, j, j % 2, rhs)
                with pe.Fori(1 if o0 == 0 else 0, n_out // RINGW) as i:
                    for j in range(RINGW):
                        pe.wait_ge(out_free[j % 2], i * 2 + (o0 + j) // 2)
                        unit(i * RINGW + (u0 + j), j, j % 2, rhs)

            def stats(src, n):
                for k in range(n):
                    for h in range(2):
                        last = pe.matmul(ps[:, 4 + h, 0:HALF], ones, src[:, k, h * HALF:(h + 1) * HALF],
                                         start=k == 0, stop=k == n - 1)
                last.then_inc(stat_ready, 1)

            pe.wait_ge(ld_c, 32)
            pe.wait_ge(sq_ready, 1)
            stats(sq, KT)
            pe.wait_ge(hn_ready, KT)
            hn_parts = (HN, X)
            for i in range(TILES):
                n = CH if i < NCH else DEC
                for k in range(KT):
                    for t, (xp, wp) in enumerate(((HN, wdt_hi), (X, wdt_hi), (HN, wdt))):
                        last = pe.matmul(ps[0:n, 6, i * NH:(i + 1) * NH], fr(xp[:, k, i * CH:i * CH + n]),
                                         fr(wp[:, k, :]), start=k == 0 and t == 0, stop=k == KT - 1 and t == 2)
            last.then_inc(dt_mm, 1)
            plain_section(U_XBC, O_XBC, CONVB, hn_parts)

            pe.wait_ge(out_free[0], O_Z // 2)
            pe.wait_ge(out_free[1], O_Z // 2)
            pe.wait_ge(dt_ready, 1)
            pe.wait_ge(root_ready, 1)

            def pair_sums(v, k, at, m, sums):
                for o in range(2):
                    pe.matmul(ps[o * HD:(o + 1) * HD, 4, at:at + m],
                              v[:, 2 * k + o:2 * k + o + 1].to_broadcast([v.shape[0], HD]), sums, start=True, stop=True)

            pe.wait_ge(xbc_ready, CONVB)

            def ssd_chunk(c, first):
                dac = DA[:, c, :]
                if not first:
                    pe.wait_ge(ed_ready, c)
                    pe.wait_ge(small_sb, c)
                    pe.wait_ge(h_done, c * NG)
                pe.matmul(ps[:, 5, 0:NH], tri, dac, start=True, stop=True)
                pe.matmul(ps[:, 5, NH:2 * NH], ones, dac, start=True, stop=True).then_inc(small_mm, 1)
                for g in range(NG):
                    last = pe.matmul(ps[:, 7, g * CH:(g + 1) * CH], tokens(XB + g, c), tokens(XB + NG + g, c),
                                     start=True, stop=True)
                last.then_inc(cb_mm, 1)

                def acum_rows(hb):
                    if not (first and hb < 2):
                        pe.wait_ge(seg_ready, c * 8 + (hb - 1))
                    for k in range(4):
                        h = 4 * hb + k
                        last = pe.matmul(ps[:, hb % 2, k * CH:(k + 1) * CH], dac[:, h:h + 1].to_broadcast([P, P]),
                                         tri, start=True, stop=True)
                    last.then_inc(ab_mm, 1)

                def transposes(b):
                    if b >= 2:
                        pe.wait_ge(tr_free_x, c * 4 + (b - 1))
                    elif not first and b == 0:
                        pe.wait_ge(tr_free_b, c)
                    elif not first:
                        pe.wait_ge(y_done, c * NG)
                    for k in range(4):
                        last = pe.transpose(ps[:, 6 if b % 2 == 0 else 3, k * CH:(k + 1) * CH], tokens(4 * b + k, c), ident)
                    last.then_inc(tr_mm, 1)

                def inter(g):
                    if g == 0:
                        pe.wait_ge(tr_free_x, c * 4 + 4)
                    if not (first and g == 0):
                        pe.wait_ge(y_done, c * NG + g)
                        pe.wait_ge(eas_ready, c * NG + g)
                        pe.wait_ge(h_done, c * NG)
                    else:
                        pe.wait_ge(set_ready, 2)
                    for k in range(4):
                        pair_sums(dac, 4 * g + k, k * CH, CH, tri)
                    for k in range(4):
                        pr = 4 * g + k
                        last = pe.matmul(ps[:, 3, k * CH:(k + 1) * CH], hT[:, pr * P:(pr + 1) * P],
                                         tokens(XB + NG + g, c), start=True, stop=True)
                    last.then_inc(inter_mm, 1)

                def intra(hb):
                    pe.wait_ge(wgt_ready, c * 8 + (hb + 1))
                    if hb % 2 == 0 and not (first and hb == 0):
                        pe.wait_ge(y_done, c * NG + hb // 2)
                    for k in range(4):
                        h = 4 * hb + k
                        o, pr = (h % 2) * HD, (h % HPG) // 2
                        last = pe.matmul(ps[o:o + HD, 2, pr * CH:(pr + 1) * CH], xdt[:, h * HD:(h + 1) * HD],
                                         wgt[:, hb % 2, k * CH:(k + 1) * CH], start=True, stop=True)
                    last.then_inc(intra_mm, 1)

                acum_rows(0)
                transposes(0)
                transposes(1)
                acum_rows(1)
                transposes(2)
                transposes(3)
                transposes(4)
                inter(0)
                for g in range(NG):
                    intra(2 * g)
                    if g + 1 < NG:
                        acum_rows(2 * g + 2)
                    intra(2 * g + 1)
                    if g + 1 < NG:
                        acum_rows(2 * g + 3)
                    if g == 0:
                        pe.wait_ge(xs2_ready, c + 1)
                        pe.wait_ge(tr_free_b, c + 1)
                        pe.wait_ge(cb_sb, c + 1)
                    else:
                        pe.wait_ge(h_done, c * NG + g)
                    pe.matmul(ps[:, 7, :], bt[:, g * NST:(g + 1) * NST], xs2[:, g * 512:(g + 1) * 512],
                              start=True, stop=True).then_inc(s_mm, 1)
                    if g + 1 < NG:
                        inter(g + 1)

            for c in range(NCH):
                ssd_chunk(c, c == 0)

            n = DEC
            dac = DA[0:n, NCH, :]
            tri_s, blk_s = cc("tri_s", n), cc("blk_s", n)
            pe.wait_ge(samp_ready, 1)
            pe.wait_ge(ed_ready, NCH)
            pe.wait_ge(h_done, NCH * NG)
            pe.wait_ge(seg_ready, NCH * 8)
            pe.wait_ge(y_done, NCH * NG)
            pe.wait_ge(eas_ready, NCH * NG)
            pe.wait_ge(tr_free_b, NCH)
            pe.matmul(ps[0:n, 5, 0:NH], tri_s, dac, start=True, stop=True)
            pe.matmul(ps[0:n, 5, NH:2 * NH], blk_s, dac, start=True, stop=True)
            pe.matmul(ps[:, 5, 2 * NH:(2 + DEC_B) * NH], ones[0:n, :], dam[0:n].rearrange("p b h -> p (b h)"),
                      start=True, stop=True).then_inc(small_mm, 1)
            for g in range(NG):
                last = pe.matmul(ps[0:n, 7, g * n:(g + 1) * n], tokens(XB + g, NCH), tokens(XB + NG + g, NCH),
                                 start=True, stop=True)
            last.then_inc(cb_mm, 1)
            for hb in range(2):
                for k in range(16):
                    h = 16 * hb + k
                    last = pe.matmul(ps[0:n, hb, k * n:(k + 1) * n], dac[:, h:h + 1].to_broadcast([n, n]), tri_s,
                                     start=True, stop=True)
                last.then_inc(ab_mm, 1)
            for b in range(5):
                if b >= 2:
                    pe.wait_ge(tr_free_x, NCH * 4 + b - 1)
                for k in range(4):
                    last = pe.transpose(ps[0:n, 6 if b % 2 == 0 else 3, k * P:(k + 1) * P], tokens(4 * b + k, NCH), ident)
                last.then_inc(tr_mm, 1)
            for k in range(XB):
                pair_sums(dac, k, k * n, n, tri_s)
            for hb in range(2):
                pe.wait_ge(wgt_ready, NCH * 8 + hb + 1)
                for k in range(16):
                    h = 16 * hb + k
                    o = (h % 2) * HD
                    last = pe.matmul(ps[o:o + HD, 2, (h // 2) * n:(h // 2 + 1) * n], xdt[0:n, h * HD:(h + 1) * HD],
                                     wgt[0:n, hb, k * n:(k + 1) * n], start=True, stop=True)
                last.then_inc(intra_mm, 1)
            pe.wait_ge(tr_free_x, (NCH + 1) * 4)
            pe.wait_ge(tr_free_b, NCH + 1)
            pe.wait_ge(cb_sb, NCH + 1)
            pe.wait_ge(ed_ready, NCH + 1)
            pe.wait_ge(small_sb, NCH + 1)
            pe.wait_ge(eas_ready, NCH * NG + 1)
            pe.wait_ge(xs2_ready, NCH + 1)
            inter_out = ps[:, 3, :].rearrange("p (k b l) -> p k b l", b=DEC_B, l=DEC_L)
            pe.wait_ge(seg_ready, NCH * 8 + 2)

            def sequences(i):
                for c in range(RINGW):
                    b, j = i * RINGW + c, c % 2
                    pe.wait_ge(h0_in[j], i * 32 + 16 * (c // 2 + 1))
                    for k in range(XB):
                        last = pe.matmul(inter_out[:, k, b, :], h0[:, j, k * P:(k + 1) * P],
                                         c_s[:, k // 4, :].rearrange("p (b l) -> p b l", l=DEC_L)[:, b, :],
                                         start=True, stop=True)
                    last.then_inc(inter_mm, 1)
                    if not (first_pass(i) and c == 0):
                        pe.wait_ge(gb_read, b)
                    unit(i * RINGW + (U_GB + c), c, 0, hn_parts)
                    pe.wait_ge(bm_ready, b + 1)
                    pe.wait_ge(h_done, b + NCH * NG)
                    for g in range(NG):
                        last = pe.matmul(ps[:, 4 + g, :], bm[0:n, j, g * NST:(g + 1) * NST],
                                         xs2[0:n, g * 512:(g + 1) * 512], start=True, stop=True)
                    last.then_inc(s_mm, 1)

            for i in range(DEC_B // RINGW):
                sequences(i)
            pe.wait_ge(h_done, NCH * NG + DEC_B)
            pe.wait_ge(y_done, NCH * NG + 1)
            pe.wait_ge(gb_read, KT)

            plain_section(U_Z, O_Z, XB, hn_parts)
            pe.wait_ge(ssq_ready, XB)
            stats(ssq.unsqueeze(1), 1)
            pe.wait_ge(y_gated, XB)
            with pe.Fori(0, KT // 2) as i:
                for j in range(2):
                    pe.wait_ge(out_free[j], i + O_SO // 2)
                    for kk in range(2):
                        unit(i * RINGW + (U_SO + 2 * j + kk), 2 * j + kk, j,
                             (XBC[:, KT * kk:KT * (kk + 1), :], y_low[kk]), start=kk == 0, stop=kk == 1)
            pe.wait_ge(root_ready, 2)

            def rg_products(i, j, first=False):
                for kk in range(2):
                    pe.wait_ge(out_free[kk], i * 2 + (O_RG // 2 + j))
                    unit(i * RINGW + (U_RG + 2 * j + kk), 2 * j + kk, kk, hn_parts)
                pe.wait_ge(wax_ready, i * 2 + (j + 1))
                pe.wait_ge(conv_done, i * 2 + (CONVB + j + 1))
                if not first:
                    pe.wait_ge(rg_ri, i * 4 + 2 * j)
                for m in range(2):
                    for h in range(2):
                        last = pe.matmul(ps[:, 4 + 2 * m + h, 0:HALF], wax[:, j, m, :],
                                         acc[:, j, h * HALF:(h + 1) * HALF], start=True, stop=True)
                last.then_inc(ax_mm, 1)

            rg_products(0, 0, True)
            rg_products(0, 1)
            with pe.Fori(1, RGB // 2) as i:
                for j in range(2):
                    rg_products(i, j)
            pe.wait_ge(r_ready, RGB)
            with pe.Fori(0, KT // 2) as i:
                for j in range(2):
                    for kk in range(2):
                        pe.wait_ge(out_free[kk], i * 2 + (O_GA // 2 + j))
                        unit(i * RINGW + (U_GA + 2 * j + kk), 2 * j + kk, kk, hn_parts if kk == 0 else (R, r_low))
            pe.wait_ge(m_ready, 2 * KT)
            pe.wait_ge(rg_ri, 2 * RGB)

            def turn(b):
                p = b % 2
                pe.wait_ge(x2_ready, b + 1)
                if b >= 2:
                    pe.wait_ge(x2t_ready, 2 * b - 2)
                for i in range(NCH):
                    pe.transpose(ps[:, 4 + p, i * CH:(i + 1) * CH], x2b[:, p, i * CH:(i + 1) * CH], ident)
                pe.transpose(ps[0:DEC, 6 + p, 0:P], x2b[:, p, SEQ:TOK], ident).then_inc(x2t_mm, 1)

            for b in range(KT):
                pe.wait_ge(out_free[b % 2], (O_WO + b) // 2)
                unit(U_WO + b, b % RINGW, b % 2, (M, m_low))
                if b >= 1:
                    turn(b - 1)
            turn(KT - 1)
            pe.wait_ge(sq_ready, 2)
            pe.wait_ge(x2t_ready, 2 * KT)
            stats(sq, KT)
            pe.wait_ge(hn_ready, 2 * KT)
            pe.wait_ge(ld_late, 32)

            def scores(q, p, first=False):
                pe.wait_ge(q_ready, q + 1)
                if not first:
                    pe.wait_ge(sc_ready, q - 1)
                for i in range(NCH):
                    pe.matmul(ps[:, 4 + p, i * CH:(i + 1) * CH], qs[:, p, i * CH:(i + 1) * CH], keys[:, q, :],
                              start=True, stop=True)
                pe.matmul(ps[0:DEC, 6 + p, 0:NKEYS], qs[:, p, SEQ:TOK], keys[:, q, :],
                          start=True, stop=True).then_inc(sc_mm, 1)

            def query(i, j, first=False):
                if not first:
                    pe.wait_ge(q_ready, i * RINGW + (j - 1))
                unit(i * RINGW + (U_WQ + j), j, j % 2, hn_parts)

            pe.wait_ge(out_free[0], O_WQ // 2)
            pe.wait_ge(out_free[1], O_WQ // 2)
            query(0, 0, True)
            query(0, 1, True)
            scores(0, 0, True)
            query(0, 2)
            scores(1, 1, True)
            query(0, 3)
            scores(2, 0)
            with pe.Fori(1, HS // RINGW) as i:
                for j in range(RINGW):
                    query(i, j)
                    scores(i * RINGW + (j - 1), (j - 1) % 2)
            scores(HS - 1, 1)

            def experts(it):
                if isinstance(it, int):
                    pe.wait_ge(q_ready, HS)
                else:
                    pe.wait_ge(flushed, it)
                for s in range(SLOTS):
                    pe.wait_ge(diag_ready, it * SLOTS + (s + 1))
                    for h in range(2):
                        last = pe.matmul(ps[:, h, :], diag[:, s % 4, :],
                                         ring[s % RING][:, D_MODEL + 512 * h:D_MODEL + 512 * (h + 1)],
                                         start=s == 0, stop=s == SLOTS - 1)
                    last.then_inc(slot_free, 1)

            experts(0)
            with pe.Fori(1, ITERS) as it:
                experts(it)
            pe.wait_ge(flushed, ITERS)
            for h in range(2):
                last = pe.matmul(ps[0:DEC, 2 + h, :], cc("sel"), X2T[:, TILES - 1, 512 * h:512 * (h + 1)],
                                 start=True, stop=True)
            last.then_inc(fin_mm, 1)

        @block.scalar
        def _(act):
            ch = Chain(act, act_s)

            def root(src, dst, scale, done):
                act.activation(dst, src, ACT.Sqrt, bias=epst[:, 0:1], scale=scale).then_inc(done, 1)

            def high(u, slot, fills):
                act.wait_ge(w_full[slot], fills * 16)
                act.activation(fr(whi[:, slot % 2]), wring[:, slot], ACT.Copy).then_inc(w_hi, 1)

            def done_and_next(i, u0, c):
                act.wait_ge(unit_done, i * RINGW + (u0 + c + 1))
                if isinstance(i, int) and i * RINGW + u0 + c + 2 >= UNITS:
                    return
                high(i * RINGW + (u0 + c + 2), (c + 2) % RINGW, i + ((u0 + c + 2) // RINGW + 1))

            def normalised_high(count):
                for k in range(KT):
                    act.wait_ge(xn_ready, count * KT + k + 1)
                    act.activation(fr(HN[:, k, :]), X[:, k, :], ACT.Copy).then_inc(hn_hi, 1)

            for j in range(2):
                act.dma_start(h0[:, j, :], a["sample_h_in"][j]).then_inc(h0_in[j], 16)
            act.wait_ge(ld_x, 16)
            act.activation(sq, X, ACT.Square).then_inc(sq_ready, 1)
            act.wait_ge(set_ready, 1)
            act.wait_ge(stat_ready, 1)
            root(ps[:, 4:6, 0:HALF], halves(rs), 1.0 / D_MODEL, root_ready)
            high(0, 0, 1)
            high(1, 1, 1)
            normalised_high(0)
            act.wait_ge(ld_c, 32)
            act.activation(ea_log[:], pc("a_log"), ACT.Exp).then_inc(sp_exp, 1)
            act.wait_ge(sp_in, 1)
            act.activation(sp2, sp3, ACT.Exp).then_inc(sp_exp, 1)

            def to_conv(n, p, banks, frees, first=False):
                if not first:
                    act.wait_ge(conv_done, n - 1)
                    act.wait_ge(state_kept, n - 1)
                ch.step(act.activation(halves(cb[:, p, PAD:PAD + TOK]), outb(banks), ACT.Copy))
                act.activation(seqs(cb[:, p, :])[:, :, PAD:SEQW],
                               ps[:, 2 * banks + 1, SEQ - HALF:HALF].rearrange("p (b l) -> p b l", l=DEC_L),
                               ACT.Copy).then_inc(out_free[frees], 1)

            def silu_out(n, p):
                act.wait_ge(conv_done, n + 1)
                act.activation(XBC[:, n, :], acc[:, p, 0:TOK], ACT.Silu).then_inc(xbc_ready, 1)

            def xbc_block(i, c):
                done_and_next(i, U_XBC, c)
                first = first_pass(i)
                to_conv(i * RINGW + c, c % 2, c % 2, c % 2, first and c < 2)
                if not (first and c == 0):
                    silu_out(i * RINGW + (c - 1), (c - 1) % 2)

            for c in range(RINGW):
                xbc_block(0, c)
            with act.Fori(1, CONVB // RINGW) as i:
                for c in range(RINGW):
                    xbc_block(i, c)
            silu_out(CONVB - 1, 1)

            act.wait_ge(state_kept, CONVB)

            def ssd_chunk(c, first):
                act.wait_ge(cb_mm, c + 1)
                if not first:
                    act.wait_ge(wgt_ready, c * 8)
                act.activation(cbs, ps[:, 7, :].rearrange("p (g t) -> p g t", t=CH), ACT.Copy).then_inc(cb_sb, 1)
                act.wait_ge(small_sb, c + 1)
                if not first:
                    act.wait_ge(xs2_ready, c)
                    act.wait_ge(h_done, c * NG)
                ch.step(act.activation(cdec[:, 0, :], ps[:, 5, NH:2 * NH], ACT.Exp))
                act.activation(ed[:], el[:], ACT.Exp).then_inc(ed_ready, 1)

                def decays(hb):
                    act.wait_ge(seg_ready, c * 8 + (hb + 1))
                    if not (first and hb < 2):
                        act.wait_ge(wgt_ready, c * 8 + (hb - 1))
                    for k in range(4):
                        last = act.activation(dec[:, hb % 2, k * CH:(k + 1) * CH], seg[:, hb % 2, k * CH:(k + 1) * CH],
                                              ACT.Exp, bias=nac[:, 4 * hb + k:4 * hb + k + 1])
                    last.then_inc(dec_ready, 1)

                decays(0)
                act.wait_ge(tr_mm, c * 5 + 5)
                if not first:
                    act.wait_ge(s_mm, c * NG)
                act.activation(bt, ps[:, 6, :], ACT.Copy).then_inc(tr_free_b, 1)
                for g in range(NG):
                    if g:
                        decays(2 * g)
                    act.wait_ge(inter_mm, c * NG + (g + 1))
                    if not (first and g == 0):
                        act.wait_ge(y_done, c * NG + g)
                    act.activation(eas, ps[:, 4, :], ACT.Exp).then_inc(eas_ready, 1)
                    decays(2 * g + 1)

            for c in range(NCH):
                ssd_chunk(c, c == 0)
            act.wait_ge(h_done, NCH * NG)
            act.dma_start(a["prompt_h"], hT).then_inc(hT_out, 16)
            n = DEC
            act.wait_ge(cb_mm, NCH + 1)
            act.wait_ge(wgt_ready, NCH * 8)
            act.activation(cbs[0:n, 0, 0:NG * n], ps[0:n, 7, 0:NG * n], ACT.Copy).then_inc(cb_sb, 1)
            act.wait_ge(small_sb, NCH + 1)
            act.wait_ge(xs2_ready, NCH)
            ch.step(act.activation(cdec[:], ps[:, 5, 2 * NH:(2 + DEC_B) * NH].rearrange("p (b h) -> p b h", h=NH), ACT.Exp))
            act.activation(ed[0:n, :], el[0:n, :], ACT.Exp).then_inc(ed_ready, 1)
            for hb in range(2):
                act.wait_ge(seg_ready, NCH * 8 + hb + 1)
                act.activation(dec[0:n, hb, :], seg[0:n, hb, :], ACT.Exp).then_inc(dec_ready, 1)
            act.wait_ge(tr_mm, NCH * 5 + 5)
            act.wait_ge(s_mm, NCH * NG)
            act.activation(bt[0:n, :], ps[0:n, 6, :], ACT.Copy).then_inc(tr_free_b, 1)
            act.wait_ge(intra_mm, NCH * 8 + 2)
            act.wait_ge(y_done, NCH * NG)
            act.activation(eas, ps[:, 4, :], ACT.Exp).then_inc(eas_ready, 1)

            for b in range(DEC_B):
                j = b % 2
                done_and_next(b // RINGW, U_GB, b % RINGW)
                act.activation(halves(M[:, b, :]), outb(0), ACT.Tanh, scale=0.5).then_inc(gb_read, 1)
                if 1 <= b < DEC_B - 1:
                    act.wait_ge(h0_out[1 - j], 16 * ((b + 1) // 2))
                    act.dma_start(h0[:, 1 - j, :], a["sample_h_in"][b + 1]).then_inc(h0_in[1 - j], 16)
                act.wait_ge(h_done, b + (NCH * NG + 1))
                act.dma_start(a["sample_h_out"][b], h0[:, j, :]).then_inc(h0_out[j], 16)

            act.wait_ge(y_done, NCH * NG + 1)
            act.wait_ge(hT_out, 16)

            def z_gate(i, c):
                done_and_next(i, U_Z, c)
                if not (first_pass(i) and c < 2):
                    act.wait_ge(yg_ready, i * RINGW + (c - 1))
                act.activation(halves(gate[:, c % 2, :]), outb(c % 2), ACT.Silu).then_inc(out_free[c % 2], 1)

            def gated_parts(i, c):
                j = c % 2
                act.wait_ge(yg_ready, i * RINGW + (c + 1))
                if not (first_pass(i) and c < 2):
                    act.wait_ge(ssq_ready, i * RINGW + (c - 1))
                act.activation(acc[:, j, 0:TOK], tt[:, j, :], ACT.Square).then_inc(yg_sq, 1)
                act.wait_ge(yf_ready, i * RINGW + (c + 1))
                act.activation(fr(XBC[:, i * RINGW + c, :]), yf[:, j, :], ACT.Copy).then_inc(y_hi, 1)

            z_gate(0, 0)
            for c in range(1, RINGW):
                z_gate(0, c)
                gated_parts(0, c - 1)
            with act.Fori(1, XB // RINGW) as i:
                for c in range(RINGW):
                    z_gate(i, c)
                    gated_parts((i - 1) if c == 0 else i, (c - 1) % RINGW)
            gated_parts(XB // RINGW - 1, RINGW - 1)
            act.wait_ge(stat_ready, 2)
            root(ps[:, 4:6, 0:HALF], halves(rs), 1.0 / INNER, root_ready)

            with act.Fori(0, 2 * KT // RINGW) as i:
                for c in range(RINGW):
                    done_and_next(i, U_SO, c)

            act.wait_ge(unit_done, U_RG)
            act.dma_start(wax_all, a["wax"]).then_inc(ld_late, 16)
            act.dma_start(keys, a["keys"]).then_inc(ld_late, 16)

            def rg_block(i, j, first=False):
                b = i * 2 + j
                done_and_next(i, U_RG, 2 * j)
                to_conv(b + CONVB, j, 0, 0)
                done_and_next(i, U_RG, 2 * j + 1)
                if not (first_pass(i)):
                    act.wait_ge(r_ready, b - 1)
                act.activation(halves(rg_g[:, j, :]), outb(1), ACT.Copy).then_inc(out_free[1], 1)
                act.wait_ge(out_free[1], b + (O_RG // 2 + 1))
                act.activation(rg_g2[:, j, :], rg_g[:, j, :], ACT.Square).then_inc(g_in, 1)
                act.wait_ge(ax_mm, b + 1)
                if not first:
                    act.wait_ge(rg_scanned, b)
                act.activation(halves(rg_tr), ps[:, 4:6, 0:HALF], ACT.Tanh, scale=0.5,
                               bias=half_b[:].unsqueeze(2)[:, b, :]).then_inc(rg_ri, 1)
                act.activation(halves(rg_ti), ps[:, 6:8, 0:HALF], ACT.Tanh, scale=0.5,
                               bias=half_b[:, RGB:2 * RGB].unsqueeze(2)[:, b, :]).then_inc(rg_ri, 1)
                cab = ca[:].unsqueeze(2)[:, b, :]
                act.wait_ge(rg_ri, b * 2 + 2)
                ch.step(act.activation(rg_a, rg_tr, ACT.Exp, scale=cab, bias=cab))
                act.activation(rg_q, rg_tr, ACT.Tanh, scale=cab, bias=cab).then_inc(rg_at, 1)
                act.wait_ge(g_u, b + 1)
                act.activation(rg_g2[:, j, :], rg_g3, ACT.Tanh, scale=GELU_S).then_inc(g_th, 1)
                act.wait_ge(rg_arg, b + 1)
                act.activation(rg_q, tt[:, 0, :], ACT.Sqrt, scale=-0.25).then_inc(rg_root, 1)

            act.wait_ge(y_gated, XB)
            rg_block(0, 0, True)
            rg_block(0, 1)
            with act.Fori(1, RGB // 2) as i:
                for j in range(2):
                    rg_block(i, j)

            act.wait_ge(r_ready, RGB)
            with act.Fori(0, KT // 2) as i:
                for j in range(2):
                    done_and_next(i, U_GA, 2 * j)
                    act.wait_ge(m_ready, i * 2 + (j + KT))
                    act.activation(halves(gate[:, 0, :]), outb(0), ACT.Tanh, scale=0.5).then_inc(out_free[0], 1)
                    done_and_next(i, U_GA, 2 * j + 1)

            act.wait_ge(set_ready, 3)
            for b in range(KT):
                p = b % 2
                done_and_next(0, U_WO, b) if b < RINGW else done_and_next(1, U_WO, b - RINGW)
                act.wait_ge(x2_ready, b + 1)
                act.activation(X[:, b, :], x2b[:, p, :], ACT.Copy).then_inc(out_free[p], 1)
                act.wait_ge(x2t_mm, b + 1)
                act.activation(X2T[:, 0:NCH, b * P:(b + 1) * P], ps[:, 4 + p, :].rearrange("p (t d) -> p t d", d=P),
                               ACT.Copy).then_inc(x2t_ready, 1)
                act.activation(X2T[0:DEC, NCH, b * P:(b + 1) * P], ps[0:DEC, 6 + p, 0:P], ACT.Copy).then_inc(x2t_ready, 1)
            act.dma_start(rows, a["rows"]).then_inc(ld_rows, 16)
            act.wait_ge(out_free[1], O_WQ // 2)
            act.activation(sq, X, ACT.Square).then_inc(sq_ready, 1)
            act.wait_ge(stat_ready, 3)
            root(ps[:, 4:6, 0:HALF], halves(rs), 1.0 / D_MODEL, root_ready)
            normalised_high(1)

            def token_norms(base):
                for i in range(TILES):
                    m = CH if i < NCH else DEC
                    if base and i == NCH:
                        act.wait_ge(flushed, ITERS + 1)
                    act.activation(tb[0:m, :], X2T[0:m, i, :], ACT.Square, accum_out=fss[0:m, i:i + 1]).then_inc(ss_ready, 1)
                    act.wait_ge(ss_ready, base + i + 1)
                root(fss[:, 0:TILES], fss[:, TILES:2 * TILES], 1.0 / D_MODEL, ss_root)

            act.wait_ge(x2t_ready, 2 * KT)
            token_norms(0)

            SCv = SC[:, 0:NCH * 4, :].rearrange("p (t r) (k n) -> p t (r k) n", r=4, n=NKEYS)
            scsv = scs.rearrange("p (q n) -> p q n", n=NKEYS)

            def keep_query(i, c):
                done_and_next(i, U_WQ, c)
                if not (isinstance(i, int) and i * RINGW + c < 2):
                    act.wait_ge(sc_mm, i * RINGW + (c - 1))
                act.activation(halves(qs[:, c % 2, :]), outb(c % 2), ACT.Copy).then_inc(q_ready, 1)

            def keep_scores(q, p):
                act.wait_ge(sc_mm, q + 1)
                for i in range(NCH):
                    ch.step(act.activation(SC[:, i * 4:(i + 1) * 4, :].rearrange("p r (k n) -> p (r k) n", n=NKEYS)[:, q, :],
                                           ps[:, 4 + p, i * NKEYS:(i + 1) * NKEYS], ACT.Copy))
                act.activation(scsv[0:DEC, q, :], ps[0:DEC, 6 + p, 0:NKEYS], ACT.Copy).then_inc(sc_ready, 1)

            def softmax_exp(h):
                act.wait_ge(fv_ready, h + 1)
                act.activation(tk_e[:], tk_fv[:], ACT.Exp, bias=tk_nm[:, 0:1], accum_out=tk_sum[:]).then_inc(ex_ready, 1)

            last_group = HS // RINGW - 1
            keep_query(0, 0)
            for c in range(1, RINGW):
                keep_query(0, c)
                keep_scores(c - 1, (c - 1) % 2)
            with act.Fori(1, last_group) as i:
                for c in range(RINGW):
                    keep_query(i, c)
                    keep_scores(i * RINGW + (c - 1), (c - 1) % 2)
            softmax_exp(0)
            for c in range(RINGW):
                keep_query(last_group, c)
                keep_scores(last_group * RINGW + c - 1, (c - 1) % 2)
            keep_scores(HS - 1, 1)

            def groups(it, j):
                for q in range(TOPK // GROUP):
                    gi = it * (SLOTS // GROUP) + (j * (TOPK // GROUP) + q + 1)
                    act.wait_ge(gl_in, gi)
                    act.activation(gth[:], g3[:], ACT.Tanh, scale=GELU_S).then_inc(gl_th, 1)
                    act.wait_ge(w_ready, gi)
                    for s in range(GROUP):
                        sl = j * TOPK + q * GROUP + s
                        if not (isinstance(it, int) and sl < 4):
                            act.wait_ge(slot_free, it * SLOTS + (sl - 3))
                        act.activation(diag[:, sl % 4, :], ident, ACT.Copy,
                                       scale=slot_w[:, j, q * GROUP + s:q * GROUP + s + 1]).then_inc(diag_ready, 1)

            softmax_exp(1)
            groups(0, 0)
            softmax_exp(2)
            groups(0, 1)
            with act.Fori(1, ITERS) as it:
                softmax_exp(it * 2 + 1)
                groups(it, 0)
                softmax_exp(it * 2 + 2)
                groups(it, 1)
            act.wait_ge(flushed, ITERS)
            token_norms(TILES)

        @block.gpsimd
        def _(pool):
            ch = Chain(pool, pool_s)
            ch.step(pool.memset(fss[:], 0.0))
            ch.step(pool.memset(cb[:, :, 0:PAD], 0.0))
            pool.memset(epst[:], EPS).then_inc(set_ready, 1)

            def low(u, slot):
                pool.wait_ge(w_hi, u + 1)
                pool.tensor_tensor(fr(wring[:, slot]), wring[:, slot], fr(whi[:, slot % 2]), ALU.subtract).then_inc(w_lo, 1)

            def normalised_low(count):
                for k in range(KT):
                    pool.wait_ge(hn_hi, count * KT + k + 1)
                    pool.tensor_tensor(fr(X[:, k, :]), X[:, k, :], fr(HN[:, k, :]), ALU.subtract).then_inc(hn_ready, 1)

            low(0, 0)
            low(1, 1)
            normalised_low(0)
            pool.wait_ge(ld_s, 16 * 3)

            def conv_side(n, p, frees, freed, first=False):
                if not first:
                    pool.wait_ge(conv_done, n - 1)
                pool.tensor_copy(seqs(cb[:, p, :])[:, :, 0:PAD], hist[:, n, :, :]).then_inc(hist_in, 1)
                pool.wait_ge(out_free[frees], freed)
                pool.wait_ge(hist_in, n + 1)
                ch.step(pool.tensor_copy(hist_p[:, n, :], cb[:, p, SEQ:PAD + SEQ]))
                pool.tensor_copy(hist[:, n, :, :], seqs(cb[:, p, :])[:, :, DEC_L:SEQW]).then_inc(state_kept, 1)

            def xbc_side(i, c):
                low(i * RINGW + (U_XBC + c + 2), (c + 2) % RINGW)
                conv_side(i * RINGW + c, c % 2, c % 2, i * 2 + (c // 2 + 1), first_pass(i) and c < 2)

            for c in range(RINGW):
                xbc_side(0, c)
            with pool.Fori(1, CONVB // RINGW) as i:
                ch.enter(i - 1, RINGW)
                for c in range(RINGW):
                    xbc_side(i, c)
                ch.leave(CONVB // RINGW - 1)

            pool.wait_ge(xbc_ready, CONVB)
            pool.wait_ge(state_kept, CONVB)
            pool.wait_ge(dt_ready, 1)
            pool.memset(hT, 0.0).then_inc(set_ready, 1)

            def skips(c, n):
                if c >= 2:
                    pool.wait_ge(y_done, (c - 1) * NG)
                pool.tensor_tensor(xd[:, c % 2, 0:XB * n].rearrange("p (k t) -> p k t", t=n), XBC[:, 0:XB, c * CH:c * CH + n],
                                   bc(pc("ssd_d"), n), ALU.mult).then_inc(xd_ready, 1)

            def state_inputs(c, n):
                if c:
                    pool.wait_ge(s_mm, c * NG)
                pool.wait_ge(ed_ready, c + 1)
                pool.wait_ge(tr_free_x, c * 4 + 4)
                pool.tensor_tensor(xs2[0:n].rearrange("p (h d) -> p h d", d=HD), xdt[0:n].rearrange("p (h d) -> p h d", d=HD),
                                   bc(ed[0:n, :], HD), ALU.mult).then_inc(xs2_ready, 1)

            n = DEC
            skips(0, CH)
            for c in range(NCH):
                state_inputs(c, CH)
                skips(c + 1, CH if c + 1 < NCH else n)
            ch.step(pool.tensor_copy(c_s[:], XBC[:, XB + NG:CONVB, SEQ:TOK]))
            pool.tensor_tensor(dam[0:n], bc1(DA[0:n, NCH, :], DEC_B), bc(cc("bcol", n), NH), ALU.mult).then_inc(samp_ready, 1)
            state_inputs(NCH, n)
            pool.wait_ge(tr_free_b, NCH + 1)

            pool.wait_ge(dec_ready, NCH * 8 + 2)

            def sequence(i, c, first=False):
                b, j = i * RINGW + c, c % 2
                if not first:
                    pool.wait_ge(s_mm, b + (NCH * NG - 1))
                pool.tensor_tensor(bm[0:n, j, :], bt[0:n, :], cc("bcol", n).unsqueeze(2)[:, b, :].to_broadcast([n, NG * NST]),
                                   ALU.mult).then_inc(bm_ready, 1)
                pool.wait_ge(inter_mm, b + (NCH * NG + 1))
                hv = h0[:, j, :].rearrange("p (h d) -> p h d", d=HD)
                pool.tensor_tensor(hv, hv, bc(cdec[:, b, :], HD), ALU.mult).then_inc(h0_dec, 1)
                low(i * RINGW + (U_GB + c + 2), (c + 2) % RINGW)

            for i in range(DEC_B // RINGW):
                for c in range(RINGW):
                    sequence(i, c, i == 0 and c < 2)

            pool.wait_ge(hT_out, 16)

            def y_lows(half, i):
                for c in range(RINGW):
                    n = i * RINGW + (half * KT + c)
                    low(n + (U_Z + 2), (c + 2) % RINGW)
                    pool.wait_ge(y_hi, n + 1)
                    pool.tensor_tensor(fr(y_low[half][:, i * RINGW + c, :]), yf[:, c % 2, :], fr(XBC[:, n, :]),
                                       ALU.subtract).then_inc(y_gated, 1)

            for half in range(2):
                with pool.Fori(0, KT // RINGW) as i:
                    y_lows(half, i)

            def lows(u0, u1):
                with pool.Fori(0, (u1 - u0) // RINGW) as i:
                    for c in range(RINGW):
                        low(i * RINGW + (u0 + c + 2), (c + 2) % RINGW)

            lows(U_SO, U_RG)
            pool.wait_ge(ld_late, 16 * 2)
            ch.link(pool.memset(cb[:, :, 0:PAD], 0.0))

            def rg_side(i, j, first=False):
                b = i * 2 + j
                if not first:
                    pool.wait_ge(ax_mm, b - 1)
                low(i * RINGW + (U_RG + 2 * j + 2), (2 * j + 2) % RINGW)
                pool.tensor_copy(wax[:, j], wax_all[:, b]).then_inc(wax_ready, 1)
                conv_side(b + CONVB, j, 0, b + (O_RG // 2 + 1))
                low(i * RINGW + (U_RG + 2 * j + 3), (2 * j + 3) % RINGW)

            rg_side(0, 0, True)
            rg_side(0, 1, True)
            with pool.Fori(1, RGB // 2) as i:
                ch.enter(i - 1, 2)
                for j in range(2):
                    rg_side(i, j)
                ch.leave(RGB // 2 - 1)
            lows(U_GA, U_WO)
            pool.wait_ge(unit_done, U_WO)
            pool.memset(X2T[:, NCH, :], 0.0).then_inc(set_ready, 1)
            lows(U_WO, U_WQ)
            normalised_low(1)
            pool.memset(SC[:, ITERS, :], 0.0).then_inc(set_ready, 1)
            lows(U_WQ, UNITS - RINGW)
            low(UNITS - 2, RINGW - 2)
            low(UNITS - 1, RINGW - 1)

            def gathers(it, j):
                pool.wait_ge(idx_ready, it * 2 + (j + 1))
                for s in range(TOPK):
                    sl = j * TOPK + s
                    if isinstance(it, int) and sl == 2:
                        pool.wait_ge(unit_done, UNITS)
                    if not (isinstance(it, int) and sl < RING):
                        pool.wait_ge(slot_free, it * SLOTS + (sl - RING + 1))
                        pool.nop(nofuse=True)
                    pool.indirect_dma_start(ring[sl % RING], None, a["uv"],
                                            bass.IndirectOffsetOnAxis(ap=gidx[:, j, s:s + 1], axis=0)
                                            ).then_inc(gath[sl % RING], 16)

            for j in range(2):
                pool.wait_ge(h0_out[j], 16 * DEC_B // 2)
            gathers(0, 0)
            gathers(0, 1)
            with pool.Fori(1, ITERS) as it:
                gathers(it, 0)
                gathers(it, 1)

        @block.vector
        def _(dve):
            ch = Chain(dve, dve_s)

            def normalise(count):
                gain = "norm_mix" if count == 1 else "norm_ffn"
                dve.wait_ge(root_ready, 1 if count == 1 else 3)
                ch.link(dve.reciprocal(rs, rs))
                for k in range(KT):
                    dve.scalar_tensor_tensor(out=X[:, k, :], in0=X[:, k, :], scalar=pcol(gain, k), in1=rs,
                                             op0=ALU.mult, op1=ALU.mult).then_inc(xn_ready, 1)

            ch.step(dve.memset(sp1, 0.0))
            dve.wait_ge(ld_c, 32)
            dve.wait_ge(ld_s, 16 * 3)
            ch.link(dve.tensor_copy(fr(wdt_hi), wdt))
            ch.step(dve.tensor_tensor(fr(wdt), wdt, fr(wdt_hi), ALU.subtract))
            normalise(1)
            dve.wait_ge(dt_mm, 1)
            ch.wait()
            nt = NCH * NH
            ch.step(dve.tensor_tensor(sp1[:, 0:nt].rearrange("p (t h) -> p t h", h=NH),
                                      ps[:, 6, 0:nt].rearrange("p (t h) -> p t h", h=NH), bc1(pc("dt_bias"), NCH), ALU.add))
            ch.step(dve.tensor_tensor(sp1[0:DEC, nt:nt + NH], ps[0:DEC, 6, nt:nt + NH], pc("dt_bias")[0:DEC, :], ALU.add))
            ch.link(dve.tensor_scalar(sp1[:, nt + NH:168], pc("rg_lam"), -1.0, None, ALU.mult))
            ch.link(dve.tensor_scalar(sp3, sp1, -1.0, None, ALU.mult))
            dve.tensor_tensor(sp3, sp3, sp1, ALU.min).then_inc(sp_in, 1)
            dve.wait_ge(sp_in, 1)
            dve.wait_ge(sp_exp, 2)
            ch.step(dve.tensor_scalar(sp1, sp1, 0.0, None, ALU.max))
            ch.link(dve.tensor_scalar(sp3, sp2, 2.0, None, ALU.add))
            ch.link(dve.reciprocal(sp3, sp3))
            ch.link(dve.tensor_tensor(sp2, sp2, sp3, ALU.mult))
            ch.link(dve.tensor_tensor(sp3, sp2, sp2, ALU.mult))
            ch.link(dve.tensor_scalar(sp4, sp3, 1.0 / 21, None, ALU.mult))
            for d in range(19, 1, -2):
                ch.link(dve.scalar_tensor_tensor(out=sp4, in0=sp4, scalar=1.0 / d, in1=sp3, op0=ALU.add, op1=ALU.mult))
            ch.link(dve.scalar_tensor_tensor(out=sp4, in0=sp4, scalar=1.0, in1=sp2, op0=ALU.add, op1=ALU.mult))
            ch.link(dve.scalar_tensor_tensor(out=sp4, in0=sp4, scalar=2.0, in1=sp1, op0=ALU.mult, op1=ALU.add))
            spt = sp4[:, 0:TILES * NH].rearrange("p (t h) -> p t h", h=NH)
            ch.step(dve.tensor_copy(DT[:], spt))
            ch.step(dve.scalar_tensor_tensor(out=DA[:], in0=spt, scalar=-1.0, in1=bc1(ea_log[:], TILES),
                                             op0=ALU.mult, op1=ALU.mult))
            ch.step(dve.tensor_scalar(ca[:], sp4[:, TILES * NH:168], -4.0, None, ALU.mult))
            ch.step(dve.tensor_scalar(half_b[:, 0:RGB], pc("rg_ba"), 0.5, None, ALU.mult))
            dve.tensor_scalar(half_b[:, RGB:2 * RGB], pc("rg_bx"), 0.5, None, ALU.mult).then_inc(dt_ready, 1)

            def conv(n, p, frees, freed, weights, bias, blk, guard):
                dve.wait_ge(out_free[frees], freed)
                dve.wait_ge(hist_in, n + 1)
                if guard is not None:
                    dve.wait_ge(*guard)
                row, o = cb[:, p, :], acc[:, p, 0:CONVN]
                ch.link(dve.tensor_scalar(o, row[:, PAD:CBW], pcol(weights, blk, PAD), pcol(bias, blk), ALU.mult, ALU.add))
                for k in range(PAD - 1, -1, -1):
                    ch.link(dve.scalar_tensor_tensor(out=o, in0=row[:, k:k + CONVN], scalar=pcol(weights, blk, k), in1=o,
                                                     op0=ALU.mult, op1=ALU.add))
                dve.tensor_copy(acc[:, p, SEQ:TOK].rearrange("p (b l) -> p b l", l=DEC_L),
                                seqs(acc[:, p, :])[:, :, 0:DEC_L]).then_inc(conv_done, 1)

            conv(0, 0, 0, 1, "conv_w", "conv_b", 0, None)
            conv(1, 1, 1, 1, "conv_w", "conv_b", 1, None)
            with dve.Fori(1, CONVB // 2) as i:
                ch.enter(i - 1, 8)
                for j in range(2):
                    n = i * 2 + j
                    conv(n, j, j, i + 1, "conv_w", "conv_b", n, (xbc_ready, i * 2 + (j - 1)))
                ch.leave(CONVB // 2 - 1)

            def ssd_chunk(c, first):
                dve.wait_ge(small_mm, c + 1)
                if not first:
                    dve.wait_ge(dec_ready, c * 8)
                    dve.wait_ge(ed_ready, c)
                ch.link(dve.tensor_scalar(nac[:], ps[:, 5, 0:NH], -1.0, None, ALU.mult))
                dve.tensor_tensor(el[:], ps[:, 5, NH:2 * NH], nac[:], ALU.add).then_inc(small_sb, 1)

                def segments(hb):
                    dve.wait_ge(ab_mm, c * 8 + (hb + 1))
                    if not (first and hb < 2):
                        dve.wait_ge(dec_ready, c * 8 + (hb - 1))
                    dve.tensor_tensor(seg[:, hb % 2, :].rearrange("p (k t) -> p k t", t=CH),
                                      ps[:, hb % 2, :].rearrange("p (k t) -> p k t", t=CH), bc1(cc("mneg"), 4),
                                      ALU.add).then_inc(seg_ready, 1)

                def weights(hb):
                    if hb == 0:
                        dve.wait_ge(cb_sb, c + 1)
                    dve.wait_ge(dec_ready, c * 8 + (hb + 1))
                    if not (first and hb < 2):
                        dve.wait_ge(intra_mm, c * 8 + (hb - 1))
                    dve.tensor_tensor(wgt[:, hb % 2, :].rearrange("p (k t) -> p k t", t=CH),
                                      dec[:, hb % 2, :].rearrange("p (k t) -> p k t", t=CH), bc1(cbs[:, hb // 2, :], 4),
                                      ALU.mult).then_inc(wgt_ready, 1)

                def scaled_x(b):
                    dve.wait_ge(tr_mm, c * 5 + (b + 1))
                    if b == 0 and not first:
                        dve.wait_ge(intra_mm, c * 8)
                        dve.wait_ge(xs2_ready, c)
                    dve.tensor_tensor(xdt[:, b * 512:(b + 1) * 512].rearrange("p (h d) -> p h d", d=HD),
                                      ps[:, 6 if b % 2 == 0 else 3, :].rearrange("p (h d) -> p h d", d=HD),
                                      bc(DT[:, c, 8 * b:8 * b + 8], HD), ALU.mult).then_inc(tr_free_x, 1)

                segments(0)
                scaled_x(0)
                scaled_x(1)
                segments(1)
                scaled_x(2)
                scaled_x(3)
                for g in range(NG):
                    weights(2 * g)
                    if g + 1 < NG:
                        segments(2 * g + 2)
                    weights(2 * g + 1)
                    if g + 1 < NG:
                        segments(2 * g + 3)
                    dve.wait_ge(eas_ready, c * NG + (g + 1))
                    dve.wait_ge(intra_mm, c * 8 + (2 * g + 2))
                    dve.wait_ge(xd_ready, c + 1)
                    ch.link(dve.tensor_tensor(yt, ps[:, 3, :], eas, ALU.mult))
                    ch.link(dve.tensor_tensor(yt, ps[:, 2, :], yt, ALU.add))
                    dve.tensor_tensor(XBC[:, 4 * g:4 * g + 4, c * CH:(c + 1) * CH],
                                      yt.rearrange("p (k t) -> p k t", t=CH), xd[:, c % 2, 512 * g:512 * (g + 1)].rearrange("p (k t) -> p k t", t=CH),
                                      ALU.add).then_inc(y_done, 1)
                    dve.wait_ge(s_mm, c * NG + (g + 1))
                    hg = hT[:, g * 512:(g + 1) * 512]
                    ch.link(dve.tensor_tensor(hg.rearrange("p (h d) -> p h d", d=HD), hg.rearrange("p (h d) -> p h d", d=HD),
                                              bc(cdec[:, 0, 8 * g:8 * g + 8], HD), ALU.mult))
                    dve.tensor_tensor(hg, ps[:, 7, :], hg, ALU.add).then_inc(h_done, 1)

            dve.wait_ge(state_kept, CONVB)
            dve.wait_ge(xbc_ready, CONVB)
            dve.wait_ge(set_ready, 2)
            for c in range(NCH):
                ssd_chunk(c, c == 0)
            n = DEC
            dve.wait_ge(small_mm, NCH + 1)
            dve.wait_ge(dec_ready, NCH * 8)
            ch.link(dve.tensor_scalar(nac[0:n, :], ps[0:n, 5, 0:NH], -1.0, None, ALU.mult))
            dve.tensor_tensor(el[0:n, :], ps[0:n, 5, NH:2 * NH], nac[0:n, :], ALU.add).then_inc(small_sb, 1)
            for hb in range(2):
                sv = seg[0:n, hb, :].rearrange("p (k t) -> p k t", t=n)
                dve.wait_ge(ab_mm, NCH * 8 + hb + 1)
                ch.link(dve.tensor_tensor(sv, ps[0:n, hb, :].rearrange("p (k t) -> p k t", t=n), bc1(cc("mneg_s", n), 16),
                                          ALU.add))
                dve.tensor_tensor(sv, sv, bc(nac[0:n, 16 * hb:16 * hb + 16], n), ALU.add).then_inc(seg_ready, 1)
            for b in range(4):
                dve.wait_ge(tr_mm, NCH * 5 + b + 1)
                if b == 0:
                    dve.wait_ge(intra_mm, NCH * 8)
                    dve.wait_ge(xs2_ready, NCH)
                dve.tensor_tensor(xdt[0:n, b * 512:(b + 1) * 512].rearrange("p (h d) -> p h d", d=HD),
                                  ps[0:n, 6 if b % 2 == 0 else 3, :].rearrange("p (h d) -> p h d", d=HD),
                                  bc(DT[0:n, NCH, 8 * b:8 * b + 8], HD), ALU.mult).then_inc(tr_free_x, 1)
            dve.wait_ge(cb_sb, NCH + 1)
            for hb in range(2):
                dve.wait_ge(dec_ready, NCH * 8 + hb + 1)
                for k in range(2):
                    g = 2 * hb + k
                    last = dve.tensor_tensor(wgt[0:n, hb, k * 256:(k + 1) * 256].rearrange("p (k t) -> p k t", t=n),
                                             dec[0:n, hb, k * 256:(k + 1) * 256].rearrange("p (k t) -> p k t", t=n),
                                             bc1(cbs[0:n, 0, g * n:(g + 1) * n], 8), ALU.mult)
                    if k == 0:
                        ch.step(last)
                last.then_inc(wgt_ready, 1)

            def new_state(b, j):
                dve.wait_ge(h0_dec, b + 1)
                dve.wait_ge(s_mm, b + (NCH * NG + 1))
                hv = h0[:, j, :].rearrange("p (g d) -> p g d", d=512)
                dve.tensor_tensor(hv, ps[:, 4:8, :], hv, ALU.add).then_inc(h_done, 1)

            with dve.Fori(0, DEC_B // 2) as i:
                for j in range(2):
                    new_state(i * 2 + j, j)
            dve.wait_ge(inter_mm, NCH * NG + DEC_B)
            dve.wait_ge(eas_ready, NCH * NG + 1)
            dve.wait_ge(intra_mm, NCH * 8 + 2)
            dve.wait_ge(xd_ready, NCH + 1)
            ch.link(dve.tensor_tensor(yt, ps[:, 3, :], eas, ALU.mult))
            ch.link(dve.tensor_tensor(yt, ps[:, 2, :], yt, ALU.add))
            dve.tensor_tensor(XBC[:, 0:XB, SEQ:TOK], yt.rearrange("p (k t) -> p k t", t=n), xd[:, NCH % 2, 0:XB * n].rearrange("p (k t) -> p k t", t=n),
                              ALU.add).then_inc(y_done, 1)
            dve.wait_ge(y_done, NCH * NG + 1)
            dve.wait_ge(hT_out, 16)

            ch.link(dve.memset(ssq, 0.0))

            def gated(i, j, first=False):
                b = i * 2 + j
                dve.wait_ge(out_free[j], i + (O_Z // 2 + 1))
                if not first:
                    dve.wait_ge(yg_sq, b - 1)
                    dve.wait_ge(y_gated, b - 1)
                dve.tensor_tensor(tt[:, j, :], gate[:, j, :], XBC[:, b, :], ALU.mult).then_inc(yg_ready, 1)
                dve.wait_ge(yg_ready, b + 1)
                dve.tensor_scalar(yf[:, j, :], tt[:, j, :], pcol("ssd_norm", b), None, ALU.mult).then_inc(yf_ready, 1)

            def square_sum(b, j):
                dve.wait_ge(yg_sq, b + 1)
                dve.tensor_tensor(ssq, ssq, acc[:, j, 0:TOK], ALU.add).then_inc(ssq_ready, 1)
                dve.wait_ge(ssq_ready, b + 1)

            gated(0, 0, True)
            gated(0, 1, True)
            square_sum(0, 0)
            with dve.Fori(1, XB // 2) as i:
                for j in range(2):
                    gated(i, j)
                    square_sum(i * 2 + (j - 1), (j - 1) % 2)
            square_sum(XB - 1, 1)
            dve.wait_ge(root_ready, 2)
            ch.link(dve.reciprocal(rs, rs))
            dve.wait_ge(gb_read, KT)
            with dve.Fori(0, KT // 2) as i:
                for j in range(2):
                    b = i * 2 + j
                    dve.wait_ge(unit_done, i * 4 + (U_SO + 2 * j + 2))
                    dve.scalar_tensor_tensor(out=halves(M[:, b, :]), in0=halves(M[:, b, :]), scalar=1.0, in1=outb(j),
                                             op0=ALU.add, op1=ALU.mult).then_inc(out_free[j], 1)
                    dve.wait_ge(out_free[j], i + (O_SO // 2 + 1))
                    dve.tensor_tensor(M[:, b, :], M[:, b, :], rs, ALU.mult).then_inc(m_ready, 1)

            def rg_conv(b, j, guard):
                conv(b + CONVB, j, 0, b + (O_RG // 2 + 1), "rg_conv_w", "rg_conv_b", b, guard)

            def rg_arguments(b, j):
                dve.wait_ge(g_in, b + 1)
                ch.link(dve.tensor_scalar(rg_g3, rg_g2[:, j, :], GELU_C, 1.0, ALU.mult, ALU.add))
                dve.tensor_tensor(rg_g3, rg_g3, rg_g[:, j, :], ALU.mult).then_inc(g_u, 1)
                dve.wait_ge(rg_at, b + 1)
                ch.link(dve.tensor_tensor(tt[:, 0, :], rg_a, rg_a, ALU.mult))
                dve.scalar_tensor_tensor(out=tt[:, 0, :], in0=tt[:, 0, :], scalar=1.0, in1=rg_q,
                                         op0=ALU.add, op1=ALU.mult).then_inc(rg_arg, 1)

            def rg_states(b, j):
                dve.wait_ge(conv_done, b + (CONVB + 1))
                ch.link(dve.scalar_tensor_tensor(out=tt[:, 1, :], in0=rg_ti, scalar=1.0, in1=acc[:, j, 0:TOK],
                                                 op0=ALU.add, op1=ALU.mult))
                dve.wait_ge(rg_root, b + 1)
                ch.link(dve.tensor_tensor(tt[:, 1, :], tt[:, 1, :], rg_q, ALU.mult))
                a0 = rg_a[:, SEQ:TOK].rearrange("p (b l) -> p b l", l=DEC_L)[:, :, 0]
                b0 = tt[:, 1, SEQ:TOK].rearrange("p (b l) -> p b l", l=DEC_L)[:, :, 0]
                ch.link(dve.tensor_tensor(tt[:, 0, 0:DEC_B], a0, rgh0[:, b, :], ALU.mult))
                ch.link(dve.tensor_tensor(b0, b0, tt[:, 0, 0:DEC_B], ALU.add))
                ch.link(dve.memset(a0, 0.0))
                dve.tensor_tensor_scan(rg_h, rg_a, tt[:, 1, :], 0.0, ALU.mult, ALU.add).then_inc(rg_scanned, 1)
                dve.wait_ge(rg_scanned, b + 1)
                ch.step(dve.tensor_copy(rgho[:, b, 0:1], rg_h[:, SEQ - 1:SEQ]))
                ch.step(dve.tensor_copy(rgho[:, b, 1:1 + DEC_B],
                                        rg_h[:, SEQ:TOK].rearrange("p (b l) -> p b l", l=DEC_L)[:, :, DEC_L - 1]))
                dve.wait_ge(g_th, b + 1)
                ch.link(dve.scalar_tensor_tensor(out=tt[:, 0, :], in0=rg_g2[:, j, :], scalar=1.0, in1=rg_g[:, j, :], op0=ALU.add, op1=ALU.mult))
                ch.link(dve.tensor_tensor(tt[:, 0, :], tt[:, 0, :], rg_h, ALU.mult))
                ch.link(dve.tensor_scalar(fr(R[:, b, :]), tt[:, 0, :], 1.0, None, ALU.mult))
                dve.tensor_tensor(fr(r_low[:, b, :]), tt[:, 0, :], fr(R[:, b, :]), ALU.subtract).then_inc(r_ready, 1)

            def rg_block(b, j, guard):
                rg_arguments(b, j)
                rg_conv(b + 1, 1 - j, guard)
                rg_states(b, j)

            dve.wait_ge(m_ready, KT)
            rg_conv(0, 0, None)
            rg_block(0, 0, None)
            rg_block(1, 1, (ax_mm, 1))
            with dve.Fori(1, RGB // 2 - 1) as i:
                ch.enter(i - 1, 2 * 16)
                for j in range(2):
                    rg_block(i * 2 + j, j, (ax_mm, i * 2 + j))
                ch.leave(RGB // 2 - 2)
            rg_block(RGB - 2, 0, (ax_mm, RGB - 2))
            rg_arguments(RGB - 1, 1)
            rg_states(RGB - 1, 1)
            dve.wait_ge(r_ready, RGB)
            with dve.Fori(0, KT) as b:
                ch.enter(b, 2)
                dve.wait_ge(out_free[0], b + (O_GA // 2 + 1))
                dve.wait_ge(unit_done, b * 2 + (U_GA + 2))
                dve.scalar_tensor_tensor(out=halves(tt[:, 0, :]), in0=halves(gate[:, 0, :]), scalar=1.0, in1=outb(1),
                                         op0=ALU.add, op1=ALU.mult).then_inc(out_free[1], 1)
                dve.wait_ge(out_free[1], b + (O_GA // 2 + 1))
                ch.link(dve.scalar_tensor_tensor(out=tt[:, 1, :], in0=tt[:, 0, :], scalar=0.5, in1=M[:, b, :],
                                                 op0=ALU.mult, op1=ALU.add))
                ch.link(dve.tensor_scalar(fr(M[:, b, :]), tt[:, 1, :], 1.0, None, ALU.mult))
                dve.tensor_tensor(fr(m_low[:, b, :]), tt[:, 1, :], fr(M[:, b, :]), ALU.subtract).then_inc(m_ready, 1)
                dve.wait_ge(m_ready, b + (KT + 1))
                ch.leave(KT)
            dve.wait_ge(ld_x, 32)
            for b in range(KT):
                p = b % 2
                dve.wait_ge(unit_done, U_WO + b + 1)
                if b >= 2:
                    dve.wait_ge(out_free[p], (O_WO + b) // 2)
                    dve.wait_ge(x2t_mm, b - 1)
                dve.scalar_tensor_tensor(out=halves(x2b[:, p, :]), in0=outb(p), scalar=0.5, in1=halves(X[:, b, :]),
                                         op0=ALU.mult, op1=ALU.add).then_inc(x2_ready, 1)
            normalise(2)
            dve.wait_ge(ss_root, 1)
            dve.wait_ge(ld_rows, 16)
            ch.link(dve.reciprocal(fss[:, TILES:2 * TILES], fss[:, TILES:2 * TILES]))
            for i in range(TILES):
                m = CH if i < NCH else DEC
                last = dve.scalar_tensor_tensor(out=H2T[:, i, :] if i < NCH else h2s[0:m, :], in0=X2T[0:m, i, :],
                                                scalar=fss[0:m, TILES + i:TILES + i + 1], in1=rows[0:m, 0, :],
                                                op0=ALU.mult, op1=ALU.mult)
                if i < NCH:
                    ch.step(last)
            last.then_inc(h2t_ready, 1)

            SCh = SC.rearrange("p t (j s n) -> p t j s n", j=2, n=NKEYS)

            def apart():
                dve.nop(nofuse=True)

            def top16(vals, idxs, src, src2):
                apart()
                ch.link(dve.max(vals[:, 0:8], src))
                apart()
                ch.step(dve.max_index(idxs[:, 0:8], vals[:, 0:8], src))
                ch.link(dve.match_replace(src2, vals[:, 0:8], src, LOWEST))
                apart()
                ch.link(dve.max(vals[:, 8:16], src2))
                apart()
                ch.link(dve.max_index(idxs[:, 8:16], vals[:, 8:16], src2))

            def route(it, j, h):
                ch.link(dve.tensor_copy(tk_s, SCh[:, it, j]))
                for s in range(2):
                    top16(tk_v[:, s, :], tk_i[:, s, :], tk_s[:, s, :], tk_s2[:, s, :])
                ch.step(dve.tensor_copy(tk_if[:], tk_i[:]))
                ch.link(dve.tensor_tensor(tk_c.rearrange("p (a b) -> p a b", b=TOPK), bc(tk_v[:, 0, :], TOPK),
                                          bc1(tk_v[:, 1, :], TOPK), ALU.add))
                top16(tk_fv[:], tk_fi[:], tk_c, tk_c2[:])
                dve.tensor_scalar(tk_nm[:], tk_fv[:, 0:1], -1.0, None, ALU.mult).then_inc(fv_ready, 1)
                ch.step(dve.tensor_scalar(tk_ab[:, 0, :], tk_fi[:], 4, None, ALU.logical_shift_right))
                ch.link(dve.tensor_scalar(tk_ab[:, 1, :], tk_fi[:], 15, None, ALU.bitwise_and))
                ch.link(dve.tensor_copy(tk_abf[:], tk_ab[:]))
                ch.link(dve.tensor_tensor(tk_eq, bc(tk_abf[:].rearrange("p s k -> p (s k)"), TOPK),
                                          bc1(cc("iota"), 2 * TOPK), ALU.is_equal))
                for s in range(2):
                    ev = tk_eq[:, s * TOPK:(s + 1) * TOPK, :]
                    ch.step(dve.tensor_tensor(ev, ev, bc1(tk_if[:, s, :], TOPK), ALU.mult))
                ch.wait()
                ch.link(dve.tensor_reduce(tk_sel[:].rearrange("p s k -> p (s k)"), tk_eq, AX_X, ALU.add))
                dve.scalar_tensor_tensor(out=gidx[:, j, :], in0=tk_sel[:, 0, :], scalar=float(NKEYS), in1=tk_sel[:, 1, :],
                                         op0=ALU.mult, op1=ALU.add).then_inc(idx_ready, 1)
                dve.wait_ge(ex_ready, h + 1)
                ch.link(dve.reciprocal(tk_r[:], tk_sum[:]))
                ch.link(dve.tensor_scalar(gw[:, j, :], tk_e[:], tk_r[:, 0:1], 0.5, ALU.mult, ALU.mult))

            ROUTE = 27

            def slots(it, j):
                for q in range(TOPK // GROUP):
                    gi = it * (SLOTS // GROUP) + (j * (TOPK // GROUP) + q + 1)
                    for s in range(GROUP):
                        k = q * GROUP + s
                        sl = j * TOPK + k
                        dve.wait_ge(gath[sl % RING], it * 64 + (sl // RING + 1) * 16)
                        u = ring[sl % RING][:, 0:D_MODEL]
                        ch.step(dve.tensor_tensor_reduce(out=u, in0=u, in1=tb, scale=1.0, scalar=0.0, op0=ALU.mult,
                                                         op1=ALU.add, accum_out=act_z[:, j, k:k + 1]))
                    ch.wait()
                    z = act_z[:, j, q * GROUP:(q + 1) * GROUP]
                    ch.link(dve.tensor_tensor(g1[:], z, z, ALU.mult))
                    ch.link(dve.tensor_scalar(g1[:], g1[:], GELU_C, 1.0, ALU.mult, ALU.add))
                    dve.tensor_tensor(g3[:], g1[:], z, ALU.mult).then_inc(gl_in, 1)
                    dve.wait_ge(gl_th, gi)
                    ch.link(dve.scalar_tensor_tensor(out=g1[:], in0=gth[:], scalar=1.0, in1=z, op0=ALU.add, op1=ALU.mult))
                    dve.tensor_tensor(slot_w[:, j, q * GROUP:(q + 1) * GROUP], g1[:], gw[:, j, q * GROUP:(q + 1) * GROUP],
                                      ALU.mult).then_inc(w_ready, 1)

            SLOTC = (TOPK // GROUP) * (GROUP + 3)

            def flush(it, tile):
                dve.wait_ge(slot_free, it * SLOTS + SLOTS if isinstance(it, int) else it * SLOTS)
                y = X2T[:, tile, :].rearrange("p (h d) -> p h d", h=2)
                dve.tensor_tensor(y, ps[:, 0:2, :], y, ALU.add).then_inc(flushed, 1)

            dve.wait_ge(sc_ready, 2)
            route(0, 0, 0)
            dve.wait_ge(sc_ready, 4)
            route(0, 1, 1)
            dve.wait_ge(set_ready, 4)
            dve.wait_ge(h2s_moved, 64)

            def iteration(it, tile, prev_tile):
                ch.link(dve.tensor_copy(tb, H2T[:, tile, :]))
                if prev_tile is not None:
                    route(it, 1, it * 2 + 1)
                    flush(it, prev_tile)
                slots(it, 0)
                route(it + 1, 0, it * 2 + 2)
                slots(it, 1)

            dve.wait_ge(sc_ready, HS)
            iteration(0, 0, None)
            dve.wait_ge(sc_moved, 64)
            with dve.Fori(1, ITERS) as it:
                ch.enter(it - 1, 1 + 2 * (ROUTE + SLOTC))
                iteration(it, it // 4, (it - 1) // 4)
                ch.leave(ITERS - 1)
            flush(ITERS - 1, NCH)
            dve.wait_ge(fin_mm, 1)
            dve.tensor_copy(X2T[0:DEC, NCH, :].rearrange("p (h d) -> p h d", h=2), ps[0:DEC, 2:4, :]).then_inc(flushed, 1)
            dve.wait_ge(ss_root, 2)
            ch.link(dve.reciprocal(fss[:, TILES:2 * TILES], fss[:, TILES:2 * TILES]))
            for i in range(TILES):
                m = CH if i < NCH else DEC
                dve.scalar_tensor_tensor(out=X2T[0:m, i, :], in0=X2T[0:m, i, :], scalar=fss[0:m, TILES + i:TILES + i + 1],
                                         in1=rows[0:m, 1, :], op0=ALU.mult, op1=ALU.mult).then_inc(fin_ready, 1)


def _blocks(w, kb):
    i, o = w.shape
    return w.reshape(i // P // kb, kb, P, o // P, P).transpose(3, 0, 2, 1, 4)


def _chan(v):
    v = np.asarray(v)
    r = v.reshape(v.shape[:-1] + (v.shape[-1] // P, P))
    return np.moveaxis(np.moveaxis(r, -1, 0), -1, 1)


def _constants():
    c = np.zeros((P, NCON), np.float32)

    def put(name, v):
        o, w = CCOL[name]
        c[:v.shape[0], o:o + w] = v

    i, s = np.arange(P), np.arange(DEC)
    same = s[:, None] // DEC_L == s[None, :] // DEC_L
    put("ident", np.eye(P))
    put("tri", i[:, None] <= i[None, :])
    put("mneg", np.where(i[:, None] <= i[None, :], 0.0, NEG))
    put("ones", np.ones((P, P)))
    put("tri_s", same & (s[:, None] <= s[None, :]))
    put("mneg_s", np.where(same & (s[:, None] <= s[None, :]), 0.0, NEG))
    put("blk_s", same)
    put("bcol", s[:, None] // DEC_L == np.arange(DEC_B)[None, :])
    put("sel", i[:, None] % DEC == s[None, :])
    put("iota", np.broadcast_to(np.arange(TOPK), (P, TOPK)))
    return c


def kernel(**inputs):
    import concourse.bacc as bacc
    from concourse.bass_utils import run_bass_kernel_spmd

    g = {k: np.asarray(v) for k, v in inputs.items()}
    x = np.concatenate([g["x_prompt"][0], g["x_sample"].reshape(DEC, D_MODEL)], 0)
    w_in = g["w_in"][0]
    cuts = np.cumsum([0, RGB * P, RGB * P, INNER, CONVB * P, NH, D_MODEL, D_MODEL])
    rgx, rgg, z, xbc, dt, ga, gb = (w_in[:, cuts[i]:cuts[i + 1]] for i in range(7))
    b1 = {k: _blocks(v, KT)[:, 0] for k, v in dict(
        rgx=rgx, rgg=rgg, z=z, xbc=xbc, ga=ga, gb=gb, rgo=g["w_rg_out"][0], wo=g["w_out"][0], wq=g["peer_wq"][0]).items()}
    so = _blocks(g["w_ssd_out"][0], KT).reshape(2 * KT, P, KT, P)
    rg = np.stack([b1["rgx"], b1["rgg"]], 1).reshape(2 * KT, P, KT, P)
    gr = np.stack([b1["ga"], b1["rgo"]], 1).reshape(2 * KT, P, KT, P)
    arrays = {
        "wstream": np.concatenate([b1["xbc"], b1["gb"], b1["z"], so, rg, gr, b1["wo"], b1["wq"]], 0),
        "x": _chan(x),
        "consts": _constants(),
        "wdt": dt.reshape(KT, P, NH).transpose(1, 0, 2),
        "wax": np.stack([g["rg_wa"][0], g["rg_wx"][0]], 1).transpose(2, 0, 1, 3),
        "keys": g["peer_keys"][0].reshape(HS, NKEYS, P).transpose(2, 0, 1),
        "hist": np.concatenate([_chan(g["state_ssd_conv"][0]), _chan(g["state_rg_conv"][0])], 1),
        "rgh0": _chan(g["state_rg_h"][0]),
        "sample_h_in": g["state_ssd_h"][0].reshape(DEC_B, INNER, NST).transpose(0, 2, 1),
        "rows": np.broadcast_to(np.stack([g["norm_ffn"][0], g["norm_final"]]), (P, 2, D_MODEL)),
        "uv": np.concatenate([g["peer_u"][0], g["peer_v"][0]], 1),
    }
    par = {
        "norm_mix": _chan(g["norm_mix"][0]), "norm_ffn": _chan(g["norm_ffn"][0]), "ssd_norm": _chan(g["ssd_norm"][0]),
        "ssd_d": _chan(np.repeat(g["ssd_d"][0], HD)),
        "conv_w": _chan(g["ssd_conv_w"][0]), "conv_b": _chan(g["ssd_conv_b"][0]),
        "rg_conv_w": _chan(g["rg_conv_w"][0]), "rg_conv_b": _chan(g["rg_conv_b"][0]),
        "rg_ba": _chan(g["rg_ba"][0]), "rg_bx": _chan(g["rg_bx"][0]), "rg_lam": _chan(g["rg_lam"][0]),
        "dt_bias": np.broadcast_to(g["ssd_dt_bias"][0], (P, NH)), "a_log": np.broadcast_to(g["ssd_a_log"][0], (P, NH)),
    }
    arrays["params"] = np.concatenate([par[n].reshape(P, -1) for n, _ in _PARAMS], 1)

    outs = {"y_prompt": (SEQ, D_MODEL), "y_sample": (DEC, D_MODEL), "hist_s": (P, CONVB + RGB, DEC_B * PAD),
            "hist_p": (P, CONVB + RGB, PAD),
            "rgho": (P, RGB, 1 + DEC_B), "prompt_h": (P, INNER), "sample_h_out": (DEC_B, P, INNER)}
    nc = bacc.Bacc("TRN2", target_bir_lowering=False, num_devices=1)
    aps = {}
    for k, v in arrays.items():
        arrays[k] = np.ascontiguousarray(v)
        aps[k] = nc.dram_tensor("in_" + k, v.shape, F32, kind="ExternalInput").ap()
    for k, s in outs.items():
        aps[k] = nc.dram_tensor("out_" + k, s, F32, kind="ExternalOutput").ap()
    hybrid_layer(nc, aps)
    r = run_bass_kernel_spmd(nc, [{"in_" + k: v for k, v in arrays.items()}], core_ids=[0]).results[0]
    o = {k: np.asarray(r["out_" + k]) for k in outs}

    def unchan(v):
        return np.moveaxis(np.moveaxis(v, 0, -1), 0, -2).reshape(v.shape[2:] + (-1,))

    hists, rgh = np.concatenate([unchan(o["hist_p"]), unchan(o["hist_s"])], 0), unchan(o["rgho"])
    ssd_c, rg_c = hists[:, :CONVB * P], hists[:, CONVB * P:]
    return (
        o["y_prompt"][None], o["y_sample"].reshape(DEC_B, DEC_L, D_MODEL),
        rgh[None, 0:1], rg_c[None, None, 0:PAD],
        o["prompt_h"].T.reshape(1, 1, NH, HD, NST), ssd_c[None, None, 0:PAD],
        rgh[None, 1:], rg_c[PAD:].reshape(1, DEC_B, PAD, -1),
        o["sample_h_out"].transpose(0, 2, 1).reshape(1, DEC_B, NH, HD, NST), ssd_c[PAD:].reshape(1, DEC_B, PAD, -1),
    )
```

```python
from contextlib import ExitStack

import numpy as np

import concourse.bass as bass
from concourse import mybir

F32 = mybir.dt.float32
F32R = mybir.dt.float32r
U32 = mybir.dt.uint32
ALU = mybir.AluOpType
ACT = mybir.ActivationFunctionType
AX_X = mybir.AxisListType.X

P = 128
D_MODEL = 1024
SEQ = 512
DEC_B, DEC_L = 8, 4
DEC = DEC_B * DEC_L
TOK = SEQ + DEC
HALF = TOK // 2
EPS = 1e-6
CONV_W = 4
PAD = CONV_W - 1
KT = D_MODEL // P
INNER = 2 * D_MODEL
NH, HD, NG, NST = 32, 64, 4, 128
HPG = NH // NG
XB = INNER // P
CONVB = XB + 2 * NG
RGB = D_MODEL // P
CH = 128
NCH = SEQ // CH
TILES = NCH + 1
PH, NKEYS, TOPK = 8, 128, 16
HS = 2 * PH
ROW = 2 * D_MODEL
NEG = -1e30
LOWEST = -3e38
GELU_C = 0.044715
GELU_S = float(np.sqrt(2.0 / np.pi))

RINGW = 4
U_XBC, U_GB, U_Z, U_SO, U_RG, U_GA, U_WO, U_WQ, UNITS = 0, 24, 32, 48, 64, 80, 96, 104, 120
O_XBC, O_Z, O_SO, O_RG, O_GA, O_WO, O_WQ = 0, 24, 40, 48, 64, 80, 88
SAMP0 = PAD + TOK
SEQW = PAD + DEC_L
CBW = SAMP0 + DEC_B * SEQW
CONVN = CBW - PAD

ITERS = NCH * 4 + 1
SLOTS = 2 * TOPK
RING = 8
GROUP = 2

_PARAMS = [("norm_mix", KT), ("norm_ffn", KT), ("ssd_norm", XB), ("ssd_d", XB), ("conv_w", CONVB * CONV_W),
           ("conv_b", CONVB), ("rg_conv_w", RGB * CONV_W), ("rg_conv_b", RGB), ("rg_ba", RGB), ("rg_bx", RGB),
           ("rg_lam", RGB), ("dt_bias", NH), ("a_log", NH)]
PCOL, NPAR = {}, 0
for _n, _w in _PARAMS:
    PCOL[_n] = (NPAR, _w)
    NPAR += _w
_CONSTS = [("ident", P), ("tri", P), ("mneg", P), ("ones", P), ("tri_s", DEC), ("mneg_s", DEC), ("blk_s", DEC),
           ("bcol", DEC_B), ("sel", DEC), ("iota", TOPK)]
CCOL, NCON = {}, 0
for _n, _w in _CONSTS:
    CCOL[_n] = (NCON, _w)
    NCON += _w


class Chain:

    def __init__(self, eng, sem):
        self.eng, self.sem, self.base, self.k, self.it, self.per = eng, sem, 0, 0, None, 0

    def value(self):
        if self.it is None:
            return self.base + self.k
        return self.it * self.per + (self.base + self.k)

    def step(self, ins):
        ins.then_inc(self.sem, 1)
        self.k += 1

    def wait(self):
        self.eng.wait_ge(self.sem, self.value())

    def link(self, ins):
        self.step(ins)
        self.wait()

    def enter(self, it, per):
        self.base += self.k
        self.k, self.it, self.per = 0, it, per

    def leave(self, n):
        assert self.k == self.per, f"steps in a pass: {self.k}, not {self.per}"
        self.base += n * self.per
        self.k, self.it = 0, None


def hybrid_layer(nc, a):
    with ExitStack() as ctx:
        def sb(name, shape, dt=F32):
            return ctx.enter_context(nc.sbuf_tensor("s_" + name, shape, dt))

        def sem(name):
            return ctx.enter_context(nc.semaphore(name))

        ps = ctx.enter_context(nc.psum_tensor("ps", [P, 8, 512], F32))

        WORK = 16448
        rounded = {}

        def region(name, n):
            t = sb(name, [P, n])
            rounded["s_" + name] = nc.alloc_sbuf_tensor_at("s_" + name + "_rounded", [P, n], F32R,
                                                           offset=nc.sbuf_base - 4 * n)
            return t

        R1 = region("r1", 2 * KT * TOK)
        R2 = region("r2", CONVB * TOK)
        R3 = region("r3", (RINGW + 2) * KT * P)
        R4 = region("r4", WORK)
        h0 = sb("h0", [P, 2, INNER])

        def view(region, at, *shape):
            v = region[:, at:at + int(np.prod(shape))]
            if len(shape) == 2:
                return v.rearrange("p (a b) -> p a b", b=shape[1])
            if len(shape) == 3:
                return v.rearrange("p (a b c) -> p a b c", b=shape[1], c=shape[2])
            return v

        def places(region, start, end, **shapes):
            out, at = {}, start
            for name, shape in shapes.items():
                out[name] = view(region, at, *shape)
                at += int(np.prod(shape))
            assert at <= end, (at, end)
            return out

        X = view(R1, 0, KT, TOK)
        HN = view(R1, KT * TOK, KT, TOK)
        wring = view(R3, 0, RINGW, KT, P)
        whi = view(R3, RINGW * KT * P, 2, KT, P)
        XBC = view(R2, 0, CONVB, TOK)
        M = XBC[:, XB:XB + KT, :]
        R = XBC[:, 0:KT, :]
        wax_all = view(R2, KT * TOK, RGB, 2, P)
        keys = view(R2, 2 * KT * TOK - HS * NKEYS, HS, NKEYS)
        X2T = view(R2, 0, TILES, D_MODEL)
        scs = R2[:, XB * TOK:XB * TOK + HS * NKEYS]
        rows = view(R2, XB * TOK + HS * NKEYS, 2, D_MODEL)
        LOW2 = WORK - KT * TOK
        w = places(R4, 0, LOW2, sq=(KT, TOK), cb=(2, CBW), acc=(2, CBW), rs=(TOK,), gate=(2, TOK),
                   yf=(2, TOK), ssq=(TOK,), t=(2, TOK))
        sq, cb, acc, rs, gate, yf, ssq, tt = w.values()
        w = places(R4, LOW2, WORK, sp1=(168,), sp2=(168,), sp3=(168,), sp4=(168,), dt_row=(TOK,))
        sp1, sp2, sp3, sp4, dt_row = w.values()
        x2b = view(R4, WORK - 2 * TOK, 2, TOK)
        w = places(R4, KT * TOK, LOW2, a=(KT // 2, TOK), other=(4 * CBW - KT // 2 * TOK + TOK,), b=(KT // 2, TOK))
        sq2 = [w["a" if b < KT // 2 else "b"][:, b % (KT // 2), :] for b in range(KT)]
        y_low = [sq, view(R4, LOW2, KT, TOK)]
        m_low, r_low = y_low
        w = places(R4, 0, KT * TOK, tr=(TOK,), ti=(TOK,), a=(TOK,), q=(TOK,), h=(TOK,), g3=(TOK,))
        rg_tr, rg_ti, rg_a, rg_q, rg_h, rg_g3 = w.values()
        rg_g, rg_g2 = gate, yf
        w = places(R4, 0, WORK, xdt=(INNER,), xs2=(INNER,), xd=(2, XB * CH), hT=(INNER,), bt=(NG * NST,),
                   cbs=(NG, CH), seg=(2, 512), dec=(2, 512), wgt=(2, 512), eas=(512,), yt=(512,))
        xdt, xs2, xd, hT, bt, cbs, seg, dec, wgt, eas, yt = w.values()
        bm = seg
        w = places(R4, 0, WORK - 2 * TOK, SC=(ITERS, 512), H2T=(TILES, D_MODEL), tb=(D_MODEL,))
        SC, H2T, tb = w.values()
        h2s, qs = tb, x2b
        w = places(R2, TILES * D_MODEL, 2 * KT * TOK - HS * NKEYS, s=(2, NKEYS), s2=(2, NKEYS), c=(TOPK * TOPK,),
                   c2=(TOPK * TOPK,), eq=(2 * TOPK, TOPK))
        tk_s, tk_s2, tk_c, tk_c2, tk_eq = w.values()
        ring = [h0[:, i, :] for i in range(2)] + [R1[:, i * ROW:(i + 1) * ROW] for i in range(3)] \
            + [R3[:, i * ROW:(i + 1) * ROW] for i in range(3)]
        diag = view(R1, 3 * ROW, 4, P)

        par, con = sb("par", [P, NPAR]), sb("con", [P, NCON])
        wdt_all = region("wdt", 2 * KT * NH)
        wdt, wdt_hi = view(wdt_all, 0, KT, NH), view(wdt_all, KT * NH, KT, NH)
        wax = sb("wax", [P, 2, 2, P])
        hist = sb("hist", [P, CONVB + RGB, DEC_B, PAD])
        rgh0 = sb("rgh0", [P, RGB, DEC_B])
        hist_p = sb("hist_p", [P, CONVB + RGB, PAD])
        rgho = sb("rgho", [P, RGB, 1 + DEC_B])
        DT, DA = sb("DT", [P, TILES, NH]), sb("DA", [P, TILES, NH])
        half_b, ca, ea_log = sb("half_b", [P, 2 * RGB]), sb("ca", [P, RGB]), sb("ea_log", [P, NH])
        nac, el, ed = sb("nac", [P, NH]), sb("el", [P, NH]), sb("ed", [P, NH])
        c_s = sb("c_s", [P, NG, DEC])
        cdec, dam = sb("cdec", [P, DEC_B, NH]), sb("dam", [P, DEC_B, NH])
        epst = sb("epst", [P, 1])
        fss = sb("fss", [P, 2 * TILES])
        tk_v, tk_i, tk_if = sb("tk_v", [P, 2, TOPK]), sb("tk_i", [P, 2, TOPK], U32), sb("tk_if", [P, 2, TOPK])
        tk_fv, tk_fi = sb("tk_fv", [P, TOPK]), sb("tk_fi", [P, TOPK], U32)
        tk_ab, tk_abf = sb("tk_ab", [P, 2, TOPK], U32), sb("tk_abf", [P, 2, TOPK])
        tk_sel = sb("tk_sel", [P, 2, TOPK])
        tk_nm, tk_e, tk_sum, tk_r = sb("tk_nm", [P, 1]), sb("tk_e", [P, TOPK]), sb("tk_sum", [P, 1]), sb("tk_r", [P, 1])
        gidx, gw = sb("gidx", [P, 2, TOPK], U32), sb("gw", [P, 2, TOPK])
        act_z, slot_w = sb("act_z", [P, 2, TOPK]), sb("slot_w", [P, 2, TOPK])
        g1, g3, gth = sb("g1", [P, GROUP]), sb("g3", [P, GROUP]), sb("gth", [P, GROUP])

        def pc(name):
            o, n = PCOL[name]
            return par[:, o:o + n]

        def pcol(name, i, k=None):
            if k is None:
                return pc(name).unsqueeze(2)[:, i, :]
            return pc(name).rearrange("p (b k) -> p b k", k=CONV_W)[:, i, k:k + 1]

        def cc(name, n=P):
            o, m = CCOL[name]
            return con[0:n, o:o + m]

        ident, tri, ones = cc("ident"), cc("tri"), cc("ones")

        def first_pass(i):
            return isinstance(i, int) and i == 0

        def tokens(k, c):
            return XBC[:, k, c * CH:(c + 1) * CH if c < NCH else TOK]

        def halfway(half):
            n = TOPK // GROUP // 2
            return range(half * n, (half + 1) * n)

        def halves(v):
            return v.rearrange("p (h t) -> p h t", h=2)

        def outb(p):
            return ps[:, 2 * p:2 * p + 2, 0:HALF]

        def bc(v, n):
            return v.unsqueeze(2).to_broadcast([v.shape[0], v.shape[1], n])

        def bc1(v, n):
            return v.unsqueeze(1).to_broadcast([v.shape[0], n, v.shape[1]])

        def seqs(v):
            return v[:, SAMP0:CBW].rearrange("p (b l) -> p b l", l=SEQW)

        def fr(v):
            return bass.AP(tensor=rounded[v.tensor.name], offset=v.offset, ap=v.ap)

        ld_x, ld_c, ld_s, ld_late = (sem(n) for n in ("ld_x", "ld_consts", "ld_small", "ld_late"))
        ld_rows = sem("ld_rows")
        ld_xp = [sem(f"ld_x_part{i}") for i in range(4)]
        w_hi, w_lo, unit_done = (sem(n) for n in ("w_hi", "w_lo", "unit_done"))
        w_full = [sem(f"w_full{i}") for i in range(RINGW)]
        out_free = [sem("out_free0"), sem("out_free1")]
        dve_s, act_s, pool_s = (sem(n) for n in ("dve_steps", "act_steps", "pool_steps"))
        sq_ready, stat_ready, root_ready = (sem(n) for n in ("sq_ready", "stat_ready", "root_ready"))
        xn_ready, hn_hi, hn_ready, set_ready = (sem(n) for n in ("xn_ready", "hn_hi", "hn_ready", "set_ready"))
        dtt_mm, dtt_ready, dt_mm, sp_in = (sem(n) for n in ("dtt_mm", "dtt_ready", "dt_mm", "sp_in"))
        sp_exp, dt_ready = (sem(n) for n in ("sp_exp", "dt_ready"))
        hist_in, conv_done, state_kept = (sem(n) for n in ("hist_in", "conv_done", "state_kept"))
        xbc_ready = sem("xbc_ready")
        samp_ready, small_mm, small_sb, cb_mm = (sem(n) for n in ("samp_ready", "small_mm", "small_sb", "cb_mm"))
        cb_sb, tr_mm, tr_free_x, tr_free_b = (sem(n) for n in ("cb_sb", "tr_mm", "tr_free_x", "tr_free_b"))
        ed_ready, xs2_ready = (sem(n) for n in ("ed_ready", "xs2_ready"))
        ab_mm, seg_ready, dec_ready, wgt_ready = (sem(n) for n in ("ab_mm", "seg_ready", "dec_ready", "wgt_ready"))
        intra_mm = sem("intra_mm")
        pair_mm, eas_ready, inter_mm = (sem(n) for n in ("pair_mm", "eas_ready", "inter_mm"))
        inter_read, intra_read, y_done, s_mm = (sem(n) for n in ("inter_read", "intra_read", "y_done", "s_mm"))
        h_done, xd_ready = (sem(n) for n in ("h_done", "xd_ready"))
        h0_dec, bm_ready, hT_out, gb_read = (sem(n) for n in ("h0_decayed", "bm_ready", "hT_out", "gb_read"))
        h0_in, h0_out = [sem("h0_in0"), sem("h0_in1")], [sem("h0_out0"), sem("h0_out1")]
        yg_ready, yg_sq, ssq_ready, yf_ready = (sem(n) for n in ("yg_ready", "yg_squared", "ssq_ready", "yf_ready"))
        y_hi, y_gated, m_ready = (sem(n) for n in ("y_hi", "y_gated", "m_ready"))
        wax_ready, ax_mm, rg_ri, rg_at, rg_arg = (sem(n) for n in ("wax_ready", "ax_mm", "rg_ri", "rg_at", "rg_arg"))
        rg_root, rg_scanned, g_in, g_u, g_th = (sem(n) for n in ("rg_root", "rg_scanned", "g_in", "g_u", "g_th"))
        r_ready = sem("r_ready")
        x2_ready, x2t_mm, x2t_ready, ss_ready = (sem(n) for n in ("x2_ready", "x2t_mm", "x2t_ready", "ss_ready"))
        ss_root = sem("ss_root")
        q_ready, sc_mm, sc_ready, sc_moved = (sem(n) for n in ("q_ready", "sc_mm", "sc_ready", "sc_moved"))
        h2t_ready, h2s_moved = (sem(n) for n in ("h2t_ready", "h2s_moved"))
        fv_ready, ex_ready, idx_ready, gl_in = (sem(n) for n in ("fv_ready", "ex_ready", "idx_ready", "gl_in"))
        gl_th, w_ready, diag_ready, slot_free = (sem(n) for n in ("gl_th", "w_ready", "diag_ready", "slot_free"))
        flushed = sem("flushed")
        gath = [sem(f"gathered{i}") for i in range(RING)]
        fin_mm, fin_ready, stored = (sem(n) for n in ("fin_mm", "fin_ready", "stored"))

        block = ctx.enter_context(nc.Block())

        @block.sync
        def _(sp):
            sp.dma_start(con[:], a["consts"]).then_inc(ld_c, 16)
            for i in range(4):
                sp.dma_start(X[:, 2 * i:2 * i + 2, :], a["x"][:, 2 * i:2 * i + 2, :]).then_inc(ld_xp[i], 16)
            sp.dma_start(par[:], a["params"]).then_inc(ld_c, 16)
            sp.dma_start(wdt, a["wdt"]).then_inc(ld_s, 16)
            for j in range(RINGW):
                sp.dma_start(wring[:, j], a["wstream"][j]).then_inc(w_full[j], 16)
            sp.dma_start(hist[:], a["hist"]).then_inc(ld_s, 16)
            sp.dma_start(rgh0[:], a["rgh0"]).then_inc(ld_s, 16)

            def refill(i):
                for j in range(RINGW):
                    sp.wait_ge(unit_done, (i - 1) * RINGW + (j + 1))
                    sp.dma_start(wring[:, j], a["wstream"][i * RINGW + j]).then_inc(w_full[j], 16)

            with sp.Fori(1, U_WO // RINGW + 1) as i:
                refill(i)
            sp.wait_ge(unit_done, U_WO)
            sp.dma_start(X, a["x"]).then_inc(ld_x, 16)
            with sp.Fori(U_WO // RINGW + 1, UNITS // RINGW) as i:
                refill(i)
            sp.wait_ge(state_kept, CONVB + RGB)
            sp.wait_ge(r_ready, RGB)
            sp.dma_start(a["hist_s"], hist[:].rearrange("p n b l -> p n (b l)")).then_inc(stored, 16)
            sp.dma_start(a["hist_p"], hist_p[:]).then_inc(stored, 16)
            sp.dma_start(a["rgho"], rgho[:]).then_inc(stored, 16)
            sp.wait_ge(h2t_ready, 1)
            for q in range(4):
                sp.dma_start(H2T[32 * q:32 * q + DEC, TILES - 1, :], h2s[0:DEC, :]).then_inc(h2s_moved, 16)
            sp.wait_ge(sc_ready, HS)
            for q in range(4):
                sp.dma_start(SC[32 * q:32 * q + DEC, ITERS - 1, :],
                             scs[0:DEC, 512 * q:512 * (q + 1)]).then_inc(sc_moved, 16)
            for i in range(TILES):
                sp.wait_ge(fin_ready, i + 1)
                if i < NCH:
                    sp.dma_start(a["y_prompt"][i * CH:(i + 1) * CH, :], X2T[:, i, :]).then_inc(stored, 16)
                else:
                    sp.dma_start(a["y_sample"], X2T[0:DEC, i, :]).then_inc(stored, 16)
            sp.wait_ge(stored, 16 * (3 + TILES))

        @block.tensor
        def _(pe):
            def unit(u, slot, p, rhs, start=True, stop=True, blocks=None):
                pe.wait_ge(w_lo, u + 1)
                w_high, w_low, (x_high, x_low) = whi[:, slot % 2], wring[:, slot], rhs
                for k in range(KT):
                    if blocks is not None:
                        pe.wait_ge(blocks[0], blocks[1] + k + 1)
                    for t, (wp, xp) in enumerate(((w_high, x_high), (w_high, x_low), (w_low, x_high))):
                        for h in range(2):
                            last = pe.matmul(ps[:, 2 * p + h, 0:HALF], fr(wp[:, k, :]),
                                             fr(xp[:, k, h * HALF:(h + 1) * HALF]),
                                             start=start and k == 0 and t == 0, stop=stop and k == KT - 1 and t == 2)
                last.then_inc(unit_done, 1)

            def plain_section(u0, o0, n_out, rhs):
                if o0 == 0:
                    for j in range(RINGW):
                        if j >= 2:
                            pe.wait_ge(out_free[j % 2], j // 2)
                        unit(u0 + j, j, j % 2, rhs)
                        if j == 1:
                            pe.wait_ge(dtt_ready, 1)
                            for i in range(TILES):
                                n = CH if i < NCH else DEC
                                last = pe.transpose(ps[0:n, 5, i * NH:(i + 1) * NH], dt_row[0:NH, i * CH:i * CH + n],
                                                    ident[0:NH, 0:NH])
                            last.then_inc(dt_mm, 1)
                with pe.Fori(1 if o0 == 0 else 0, n_out // RINGW) as i:
                    for j in range(RINGW):
                        pe.wait_ge(out_free[j % 2], i * 2 + (o0 + j) // 2)
                        unit(i * RINGW + (u0 + j), j, j % 2, rhs)

            def stats(src, k, n, bank, col):
                for h in range(2):
                    last = pe.matmul(ps[:, bank + h, col:col + HALF], ones, src[:, h * HALF:(h + 1) * HALF],
                                     start=k == 0, stop=k == n - 1)
                if k == n - 1:
                    last.then_inc(stat_ready, 1)

            pe.wait_ge(ld_c, 32)
            for k in range(KT):
                pe.wait_ge(sq_ready, k // 2 + 1)
                stats(sq[:, k, :], k, KT, 4, 0)
            hn_parts = (HN, X)
            for k in range(KT):
                pe.wait_ge(hn_ready, k + 1)
                for t, (wp, xp) in enumerate(((wdt_hi, HN), (wdt_hi, X), (wdt, HN))):
                    for h in range(2):
                        last = pe.matmul(ps[0:NH, 6 + h, 0:HALF], fr(wp[:, k, :]), fr(xp[:, k, h * HALF:(h + 1) * HALF]),
                                         start=k == 0 and t == 0, stop=k == KT - 1 and t == 2)
            last.then_inc(dtt_mm, 1)
            plain_section(U_XBC, O_XBC, CONVB, hn_parts)

            pe.wait_ge(out_free[0], O_Z // 2)
            pe.wait_ge(out_free[1], O_Z // 2)
            pe.wait_ge(dt_ready, 1)
            pe.wait_ge(root_ready, 1)

            def pair_sums(v, k, at, m, sums):
                for o in range(2):
                    last = pe.matmul(ps[o * HD:(o + 1) * HD, 4, at:at + m],
                                     v[:, 2 * k + o:2 * k + o + 1].to_broadcast([v.shape[0], HD]), sums,
                                     start=True, stop=True)
                return last

            pe.wait_ge(xbc_ready, CONVB)

            def ssd_chunk(c, first):
                dac = DA[:, c, :]
                if not first:
                    pe.wait_ge(ed_ready, c)
                    pe.wait_ge(small_sb, c)
                    pe.wait_ge(h_done, c * NG)
                pe.matmul(ps[:, 5, 0:NH], tri, dac, start=True, stop=True)
                pe.matmul(ps[:, 5, NH:2 * NH], ones, dac, start=True, stop=True).then_inc(small_mm, 1)
                for g in range(NG):
                    last = pe.matmul(ps[:, 7, g * CH:(g + 1) * CH], tokens(XB + g, c), tokens(XB + NG + g, c),
                                     start=True, stop=True)
                last.then_inc(cb_mm, 1)

                def acum_rows(hb):
                    if not (first and hb < 2):
                        pe.wait_ge(seg_ready, c * 8 + (hb - 1))
                    for k in range(4):
                        h = 4 * hb + k
                        last = pe.matmul(ps[:, hb % 2, k * CH:(k + 1) * CH], dac[:, h:h + 1].to_broadcast([P, P]),
                                         tri, start=True, stop=True)
                    last.then_inc(ab_mm, 1)

                def transposes(b):
                    if b >= 2:
                        pe.wait_ge(tr_free_x, c * 4 + (b - 1))
                    elif not first and b == 0:
                        pe.wait_ge(tr_free_b, c)
                    elif not first:
                        pe.wait_ge(y_done, c * NG)
                    for k in range(4):
                        last = pe.transpose(ps[:, 6 if b % 2 == 0 else 3, k * CH:(k + 1) * CH], tokens(4 * b + k, c), ident)
                    last.then_inc(tr_mm, 1)

                def decay_sums(g):
                    if not (first and g == 0):
                        pe.wait_ge(eas_ready, c * NG + g)
                    for k in range(4):
                        last = pair_sums(dac, 4 * g + k, k * CH, CH, tri)
                    last.then_inc(pair_mm, 1)

                def inter(g):
                    if g == 0:
                        pe.wait_ge(tr_free_x, c * 4 + 4)
                    else:
                        pe.wait_ge(inter_read, c * NG + g)
                    if first and g == 0:
                        pe.wait_ge(set_ready, 2)
                    elif not first:
                        pe.wait_ge(h_done, c * NG)
                    for k in range(4):
                        pr = 4 * g + k
                        last = pe.matmul(ps[:, 3, k * CH:(k + 1) * CH], hT[:, pr * P:(pr + 1) * P],
                                         tokens(XB + NG + g, c), start=True, stop=True)
                    last.then_inc(inter_mm, 1)

                def intra(hb):
                    pe.wait_ge(wgt_ready, c * 8 + (hb + 1))
                    if hb % 2 == 0 and not (first and hb == 0):
                        pe.wait_ge(intra_read, c * NG + hb // 2)
                    for k in range(4):
                        h = 4 * hb + k
                        o, pr = (h % 2) * HD, (h % HPG) // 2
                        last = pe.matmul(ps[o:o + HD, 2, pr * CH:(pr + 1) * CH], xdt[:, h * HD:(h + 1) * HD],
                                         wgt[:, hb % 2, k * CH:(k + 1) * CH], start=True, stop=True)
                    last.then_inc(intra_mm, 1)

                acum_rows(0)
                transposes(0)
                transposes(1)
                acum_rows(1)
                transposes(2)
                transposes(3)
                transposes(4)
                decay_sums(0)
                inter(0)
                for g in range(NG):
                    if g + 1 < NG:
                        acum_rows(2 * g + 2)
                        acum_rows(2 * g + 3)
                    intra(2 * g)
                    intra(2 * g + 1)
                    if g + 1 < NG:
                        decay_sums(g + 1)
                    if g == 0:
                        pe.wait_ge(xs2_ready, c + 1)
                        pe.wait_ge(tr_free_b, c + 1)
                        pe.wait_ge(cb_sb, c + 1)
                    else:
                        pe.wait_ge(h_done, c * NG + g)
                    pe.matmul(ps[:, 7, :], bt[:, g * NST:(g + 1) * NST], xs2[:, g * 512:(g + 1) * 512],
                              start=True, stop=True).then_inc(s_mm, 1)
                    if g + 1 < NG:
                        inter(g + 1)

            for c in range(NCH):
                ssd_chunk(c, c == 0)

            n = DEC
            dac = DA[0:n, NCH, :]
            tri_s, blk_s = cc("tri_s", n), cc("blk_s", n)
            pe.wait_ge(samp_ready, 1)
            pe.wait_ge(ed_ready, NCH)
            pe.wait_ge(h_done, NCH * NG)
            pe.wait_ge(seg_ready, NCH * 8)
            pe.wait_ge(y_done, NCH * NG)
            pe.wait_ge(eas_ready, NCH * NG)
            pe.wait_ge(tr_free_b, NCH)
            pe.matmul(ps[0:n, 5, 0:NH], tri_s, dac, start=True, stop=True)
            pe.matmul(ps[0:n, 5, NH:2 * NH], blk_s, dac, start=True, stop=True)
            pe.matmul(ps[:, 5, 2 * NH:(2 + DEC_B) * NH], ones[0:n, :], dam[0:n].rearrange("p b h -> p (b h)"),
                      start=True, stop=True).then_inc(small_mm, 1)
            for g in range(NG):
                last = pe.matmul(ps[0:n, 7, g * n:(g + 1) * n], tokens(XB + g, NCH), tokens(XB + NG + g, NCH),
                                 start=True, stop=True)
            last.then_inc(cb_mm, 1)
            for hb in range(2):
                for k in range(16):
                    h = 16 * hb + k
                    last = pe.matmul(ps[0:n, hb, k * n:(k + 1) * n], dac[:, h:h + 1].to_broadcast([n, n]), tri_s,
                                     start=True, stop=True)
                last.then_inc(ab_mm, 1)
            for b in range(5):
                if b >= 2:
                    pe.wait_ge(tr_free_x, NCH * 4 + b - 1)
                for k in range(4):
                    last = pe.transpose(ps[0:n, 6 if b % 2 == 0 else 3, k * P:(k + 1) * P], tokens(4 * b + k, NCH), ident)
                last.then_inc(tr_mm, 1)
            for k in range(XB):
                pair_sums(dac, k, k * n, n, tri_s)
            for hb in range(2):
                pe.wait_ge(wgt_ready, NCH * 8 + hb + 1)
                for k in range(16):
                    h = 16 * hb + k
                    o = (h % 2) * HD
                    last = pe.matmul(ps[o:o + HD, 2, (h // 2) * n:(h // 2 + 1) * n], xdt[0:n, h * HD:(h + 1) * HD],
                                     wgt[0:n, hb, k * n:(k + 1) * n], start=True, stop=True)
                last.then_inc(intra_mm, 1)
            pe.wait_ge(tr_free_x, (NCH + 1) * 4)
            pe.wait_ge(tr_free_b, NCH + 1)
            pe.wait_ge(cb_sb, NCH + 1)
            pe.wait_ge(ed_ready, NCH + 1)
            pe.wait_ge(small_sb, NCH + 1)
            pe.wait_ge(eas_ready, NCH * NG + 1)
            pe.wait_ge(xs2_ready, NCH + 1)
            inter_out = ps[:, 3, :].rearrange("p (k b l) -> p k b l", b=DEC_B, l=DEC_L)
            pe.wait_ge(seg_ready, NCH * 8 + 2)

            def sequences(i):
                for c in range(RINGW):
                    b, j = i * RINGW + c, c % 2
                    pe.wait_ge(h0_in[j], i * 32 + 16 * (c // 2 + 1))
                    for k in range(XB):
                        last = pe.matmul(inter_out[:, k, b, :], h0[:, j, k * P:(k + 1) * P],
                                         c_s[:, k // 4, :].rearrange("p (b l) -> p b l", l=DEC_L)[:, b, :],
                                         start=True, stop=True)
                    last.then_inc(inter_mm, 1)
                    if not (first_pass(i) and c == 0):
                        pe.wait_ge(gb_read, b)
                    unit(i * RINGW + (U_GB + c), c, 0, hn_parts)
                    pe.wait_ge(bm_ready, b + 1)
                    pe.wait_ge(h_done, b + NCH * NG)
                    for g in range(NG):
                        last = pe.matmul(ps[:, 4 + g, :], bm[0:n, j, g * NST:(g + 1) * NST],
                                         xs2[0:n, g * 512:(g + 1) * 512], start=True, stop=True)
                    last.then_inc(s_mm, 1)

            for i in range(DEC_B // RINGW):
                sequences(i)
            pe.wait_ge(h_done, NCH * NG + DEC_B)
            pe.wait_ge(y_done, NCH * NG + 1)
            pe.wait_ge(gb_read, KT)

            plain_section(U_Z, O_Z, XB, hn_parts)
            def so_units(i, j, first=False):
                pe.wait_ge(out_free[j], i + O_SO // 2)
                for kk in range(2):
                    unit(i * RINGW + (U_SO + 2 * j + kk), 2 * j + kk, j, (XBC[:, KT * kk:KT * (kk + 1), :], y_low[kk]),
                         start=kk == 0, stop=kk == 1, blocks=(y_gated, KT * kk) if first else None)
                    if first and kk == 0:
                        pe.wait_ge(ssq_ready, XB)
                        stats(ssq, 0, 1, 4, 0)

            so_units(0, 0, True)
            so_units(0, 1)
            with pe.Fori(1, KT // 2) as i:
                for j in range(2):
                    so_units(i, j)
            pe.wait_ge(root_ready, 2)

            def rg_products(i, j, first=False):
                for kk in range(2):
                    pe.wait_ge(out_free[kk], i * 2 + (O_RG // 2 + j))
                    unit(i * RINGW + (U_RG + 2 * j + kk), 2 * j + kk, kk, hn_parts)
                pe.wait_ge(wax_ready, i * 2 + (j + 1))
                pe.wait_ge(conv_done, i * 2 + (CONVB + j + 1))
                if not first:
                    pe.wait_ge(rg_ri, i * 4 + 2 * j)
                for m in range(2):
                    for h in range(2):
                        last = pe.matmul(ps[:, 4 + 2 * m + h, 0:HALF], wax[:, j, m, :],
                                         acc[:, j, h * HALF:(h + 1) * HALF], start=True, stop=True)
                last.then_inc(ax_mm, 1)

            rg_products(0, 0, True)
            rg_products(0, 1)
            with pe.Fori(1, RGB // 2) as i:
                for j in range(2):
                    rg_products(i, j)
            with pe.Fori(0, KT // 2) as i:
                for j in range(2):
                    for kk in range(2):
                        pe.wait_ge(out_free[kk], i * 2 + (O_GA // 2 + j))
                        if kk == 1:
                            pe.wait_ge(r_ready, RGB)
                        unit(i * RINGW + (U_GA + 2 * j + kk), 2 * j + kk, kk, hn_parts if kk == 0 else (R, r_low))
            pe.wait_ge(rg_ri, 2 * RGB)

            def turn(b):
                p = b % 2
                pe.wait_ge(x2_ready, b + 1)
                if b >= 1:
                    pe.wait_ge(x2t_ready, 2 * b)
                for i in range(NCH):
                    pe.transpose(ps[:, 4, i * CH:(i + 1) * CH], x2b[:, p, i * CH:(i + 1) * CH], ident)
                pe.transpose(ps[0:DEC, 5, 0:P], x2b[:, p, SEQ:TOK], ident).then_inc(x2t_mm, 1)

            def row_squares(b):
                pe.wait_ge(sq_ready, 4 + b + 1)
                stats(sq2[b], b, KT, 6, 0)

            for b in range(KT):
                pe.wait_ge(out_free[b % 2], (O_WO + b) // 2)
                unit(U_WO + b, b % RINGW, b % 2, (M, m_low), blocks=(m_ready, KT) if b == 0 else None)
                if b >= 1:
                    turn(b - 1)
                if b >= 2:
                    row_squares(b - 2)
            turn(KT - 1)
            row_squares(KT - 2)
            row_squares(KT - 1)
            pe.wait_ge(ld_late, 32)

            def scores(q, p, first=False):
                pe.wait_ge(q_ready, q + 1)
                if not first:
                    pe.wait_ge(sc_ready, q - 1)
                for i in range(NCH):
                    pe.matmul(ps[:, 4 + p, i * CH:(i + 1) * CH], qs[:, p, i * CH:(i + 1) * CH], keys[:, q, :],
                              start=True, stop=True)
                pe.matmul(ps[0:DEC, 6 + p, 0:NKEYS], qs[:, p, SEQ:TOK], keys[:, q, :],
                          start=True, stop=True).then_inc(sc_mm, 1)

            def query(i, j, first=False):
                if not first:
                    pe.wait_ge(q_ready, i * RINGW + (j - 1))
                unit(i * RINGW + (U_WQ + j), j, j % 2, hn_parts, blocks=(hn_ready, KT) if first and j == 0 else None)

            pe.wait_ge(out_free[0], O_WQ // 2)
            pe.wait_ge(out_free[1], O_WQ // 2)
            query(0, 0, True)
            query(0, 1, True)
            scores(0, 0, True)
            query(0, 2)
            scores(1, 1, True)
            query(0, 3)
            scores(2, 0)
            with pe.Fori(1, HS // RINGW) as i:
                for j in range(RINGW):
                    query(i, j)
                    scores(i * RINGW + (j - 1), (j - 1) % 2)
            scores(HS - 1, 1)

            def experts(it):
                if isinstance(it, int):
                    pe.wait_ge(q_ready, HS)
                else:
                    pe.wait_ge(flushed, it)
                for s in range(SLOTS):
                    pe.wait_ge(diag_ready, it * SLOTS + (s + 1))
                    for h in range(2):
                        last = pe.matmul(ps[:, h, :], diag[:, s % 4, :],
                                         ring[s % RING][:, D_MODEL + 512 * h:D_MODEL + 512 * (h + 1)],
                                         start=s == 0, stop=s == SLOTS - 1)
                    last.then_inc(slot_free, 1)

            experts(0)
            with pe.Fori(1, ITERS) as it:
                experts(it)
            pe.wait_ge(flushed, ITERS)
            for h in range(2):
                last = pe.matmul(ps[0:DEC, 2 + h, :], cc("sel"), X2T[:, TILES - 1, 512 * h:512 * (h + 1)],
                                 start=True, stop=True)
            last.then_inc(fin_mm, 1)

        @block.scalar
        def _(act):
            ch = Chain(act, act_s)

            def root(src, dst, scale, done):
                act.activation(dst, src, ACT.Sqrt, bias=epst[:, 0:1], scale=scale).then_inc(done, 1)

            def high(u, slot, fills):
                act.wait_ge(w_full[slot], fills * 16)
                act.activation(fr(whi[:, slot % 2]), wring[:, slot], ACT.Copy).then_inc(w_hi, 1)

            def done(i, u0, c):
                act.wait_ge(unit_done, i * RINGW + (u0 + c + 1))

            def done_and_next(i, u0, c):
                done(i, u0, c)
                after_next(i, u0, c)

            def after_next(i, u0, c):
                if isinstance(i, int) and i * RINGW + u0 + c + 2 >= UNITS:
                    return
                high(i * RINGW + (u0 + c + 2), (c + 2) % RINGW, i + ((u0 + c + 2) // RINGW + 1))

            def normalised_high(count):
                for k in range(KT):
                    act.wait_ge(xn_ready, count * KT + k + 1)
                    act.activation(fr(HN[:, k, :]), X[:, k, :], ACT.Copy).then_inc(hn_hi, 1)

            for i in range(4):
                act.wait_ge(ld_xp[i], 16)
                act.activation(sq[:, 2 * i:2 * i + 2, :], X[:, 2 * i:2 * i + 2, :], ACT.Square).then_inc(sq_ready, 1)
            for j in range(2):
                act.dma_start(h0[:, j, :], a["sample_h_in"][j]).then_inc(h0_in[j], 16)
            act.wait_ge(set_ready, 1)
            act.wait_ge(stat_ready, 1)
            root(ps[:, 4:6, 0:HALF], halves(rs), 1.0 / D_MODEL, root_ready)
            high(0, 0, 1)
            high(1, 1, 1)
            normalised_high(0)
            act.wait_ge(dtt_mm, 1)
            act.activation(halves(dt_row[0:NH, :]), ps[0:NH, 6:8, 0:HALF], ACT.Copy).then_inc(dtt_ready, 1)

            def to_conv(n, p, banks, frees, first=False):
                if not first:
                    act.wait_ge(conv_done, n - 1)
                    act.wait_ge(state_kept, n - 1)
                ch.step(act.activation(halves(cb[:, p, PAD:PAD + TOK]), outb(banks), ACT.Copy))
                act.activation(seqs(cb[:, p, :])[:, :, PAD:SEQW],
                               ps[:, 2 * banks + 1, SEQ - HALF:HALF].rearrange("p (b l) -> p b l", l=DEC_L),
                               ACT.Copy).then_inc(out_free[frees], 1)

            def silu_out(n, p):
                act.wait_ge(conv_done, n + 1)
                act.activation(XBC[:, n, :], acc[:, p, 0:TOK], ACT.Silu).then_inc(xbc_ready, 1)

            def xbc_block(i, c):
                done_and_next(i, U_XBC, c)
                first = first_pass(i)
                to_conv(i * RINGW + c, c % 2, c % 2, c % 2, first and c < 2)
                if not (first and c == 0):
                    silu_out(i * RINGW + (c - 1), (c - 1) % 2)

            xbc_block(0, 0)
            xbc_block(0, 1)
            act.wait_ge(ld_c, 32)
            act.activation(ea_log[:], pc("a_log"), ACT.Exp).then_inc(sp_exp, 1)
            act.wait_ge(sp_in, 1)
            act.activation(sp2, sp3, ACT.Exp).then_inc(sp_exp, 1)
            xbc_block(0, 2)
            xbc_block(0, 3)
            with act.Fori(1, CONVB // RINGW) as i:
                for c in range(RINGW):
                    xbc_block(i, c)
            silu_out(CONVB - 1, 1)

            act.wait_ge(state_kept, CONVB)

            def ssd_chunk(c, first):
                act.wait_ge(cb_mm, c + 1)
                if not first:
                    act.wait_ge(wgt_ready, c * 8)
                act.activation(cbs, ps[:, 7, :].rearrange("p (g t) -> p g t", t=CH), ACT.Copy).then_inc(cb_sb, 1)
                act.wait_ge(small_sb, c + 1)
                if not first:
                    act.wait_ge(xs2_ready, c)
                    act.wait_ge(h_done, c * NG)
                ch.step(act.activation(cdec[:, 0, :], ps[:, 5, NH:2 * NH], ACT.Exp))
                act.activation(ed[:], el[:], ACT.Exp).then_inc(ed_ready, 1)

                def decays(hb):
                    act.wait_ge(seg_ready, c * 8 + (hb + 1))
                    if not (first and hb < 2):
                        act.wait_ge(wgt_ready, c * 8 + (hb - 1))
                    for k in range(4):
                        last = act.activation(dec[:, hb % 2, k * CH:(k + 1) * CH], seg[:, hb % 2, k * CH:(k + 1) * CH],
                                              ACT.Exp, bias=nac[:, 4 * hb + k:4 * hb + k + 1])
                    last.then_inc(dec_ready, 1)

                decays(0)
                act.wait_ge(tr_mm, c * 5 + 5)
                if not first:
                    act.wait_ge(s_mm, c * NG)
                act.activation(bt, ps[:, 6, :], ACT.Copy).then_inc(tr_free_b, 1)
                for g in range(NG):
                    if g:
                        decays(2 * g)
                    decays(2 * g + 1)
                    act.wait_ge(pair_mm, c * NG + (g + 1))
                    if not (first and g == 0):
                        act.wait_ge(inter_read, c * NG + g)
                    act.activation(eas, ps[:, 4, :], ACT.Exp).then_inc(eas_ready, 1)

            for c in range(NCH):
                ssd_chunk(c, c == 0)
            act.wait_ge(h_done, NCH * NG)
            act.dma_start(a["prompt_h"], hT).then_inc(hT_out, 16)
            n = DEC
            act.wait_ge(cb_mm, NCH + 1)
            act.wait_ge(wgt_ready, NCH * 8)
            act.activation(cbs[0:n, 0, 0:NG * n], ps[0:n, 7, 0:NG * n], ACT.Copy).then_inc(cb_sb, 1)
            act.wait_ge(small_sb, NCH + 1)
            act.wait_ge(xs2_ready, NCH)
            ch.step(act.activation(cdec[:], ps[:, 5, 2 * NH:(2 + DEC_B) * NH].rearrange("p (b h) -> p b h", h=NH), ACT.Exp))
            act.activation(ed[0:n, :], el[0:n, :], ACT.Exp).then_inc(ed_ready, 1)
            for hb in range(2):
                act.wait_ge(seg_ready, NCH * 8 + hb + 1)
                act.activation(dec[0:n, hb, :], seg[0:n, hb, :], ACT.Exp).then_inc(dec_ready, 1)
            act.wait_ge(tr_mm, NCH * 5 + 5)
            act.wait_ge(s_mm, NCH * NG)
            act.activation(bt[0:n, :], ps[0:n, 6, :], ACT.Copy).then_inc(tr_free_b, 1)
            act.wait_ge(intra_mm, NCH * 8 + 2)
            act.wait_ge(y_done, NCH * NG)
            act.activation(eas, ps[:, 4, :], ACT.Exp).then_inc(eas_ready, 1)

            for b in range(DEC_B):
                j = b % 2
                if 1 <= b < DEC_B - 1:
                    act.wait_ge(h0_out[1 - j], 16 * ((b + 1) // 2))
                    act.dma_start(h0[:, 1 - j, :], a["sample_h_in"][b + 1]).then_inc(h0_in[1 - j], 16)
                done_and_next(b // RINGW, U_GB, b % RINGW)
                act.activation(halves(M[:, b, :]), outb(0), ACT.Tanh, scale=0.5).then_inc(gb_read, 1)
                act.wait_ge(h_done, b + (NCH * NG + 1))
                act.dma_start(a["sample_h_out"][b], h0[:, j, :]).then_inc(h0_out[j], 16)

            act.wait_ge(y_done, NCH * NG + 1)
            act.wait_ge(hT_out, 16)

            def z_gate(i, c):
                done_and_next(i, U_Z, c)
                if not (first_pass(i) and c < 2):
                    act.wait_ge(yg_ready, i * RINGW + (c - 1))
                act.activation(halves(gate[:, c % 2, :]), outb(c % 2), ACT.Silu).then_inc(out_free[c % 2], 1)

            def gated_parts(i, c):
                j = c % 2
                act.wait_ge(yg_ready, i * RINGW + (c + 1))
                if not (first_pass(i) and c < 2):
                    act.wait_ge(ssq_ready, i * RINGW + (c - 1))
                act.activation(acc[:, j, 0:TOK], tt[:, j, :], ACT.Square).then_inc(yg_sq, 1)
                act.wait_ge(yf_ready, i * RINGW + (c + 1))
                act.activation(fr(XBC[:, i * RINGW + c, :]), yf[:, j, :], ACT.Copy).then_inc(y_hi, 1)

            z_gate(0, 0)
            for c in range(1, RINGW):
                z_gate(0, c)
                gated_parts(0, c - 1)
            with act.Fori(1, XB // RINGW) as i:
                for c in range(RINGW):
                    z_gate(i, c)
                    gated_parts((i - 1) if c == 0 else i, (c - 1) % RINGW)
            gated_parts(XB // RINGW - 1, RINGW - 1)
            act.wait_ge(stat_ready, 2)
            root(ps[:, 4:6, 0:HALF], halves(rs), 1.0 / INNER, root_ready)

            with act.Fori(0, 2 * KT // RINGW) as i:
                for c in range(RINGW):
                    done_and_next(i, U_SO, c)

            act.wait_ge(unit_done, U_RG)
            act.dma_start(wax_all, a["wax"]).then_inc(ld_late, 16)
            act.dma_start(keys, a["keys"]).then_inc(ld_late, 16)

            def rg_block(i, j, first=False):
                b = i * 2 + j
                done(i, U_RG, 2 * j)
                to_conv(b + CONVB, j, 0, 0)
                after_next(i, U_RG, 2 * j)
                done_and_next(i, U_RG, 2 * j + 1)
                if not (first_pass(i)):
                    act.wait_ge(r_ready, b - 1)
                act.activation(halves(rg_g[:, j, :]), outb(1), ACT.Copy).then_inc(out_free[1], 1)
                act.wait_ge(out_free[1], b + (O_RG // 2 + 1))
                act.activation(rg_g2[:, j, :], rg_g[:, j, :], ACT.Square).then_inc(g_in, 1)
                act.wait_ge(ax_mm, b + 1)
                if not first:
                    act.wait_ge(rg_scanned, b)
                act.activation(halves(rg_tr), ps[:, 4:6, 0:HALF], ACT.Tanh, scale=0.5,
                               bias=half_b[:].unsqueeze(2)[:, b, :]).then_inc(rg_ri, 1)
                act.activation(halves(rg_ti), ps[:, 6:8, 0:HALF], ACT.Tanh, scale=0.5,
                               bias=half_b[:, RGB:2 * RGB].unsqueeze(2)[:, b, :]).then_inc(rg_ri, 1)
                cab = ca[:].unsqueeze(2)[:, b, :]
                act.wait_ge(rg_ri, b * 2 + 2)
                ch.step(act.activation(rg_a, rg_tr, ACT.Exp, scale=cab, bias=cab))
                act.activation(rg_q, rg_tr, ACT.Tanh, scale=cab, bias=cab).then_inc(rg_at, 1)
                act.wait_ge(g_u, b + 1)
                act.activation(rg_g2[:, j, :], rg_g3, ACT.Tanh, scale=GELU_S).then_inc(g_th, 1)
                act.wait_ge(rg_arg, b + 1)
                act.activation(rg_q, tt[:, 0, :], ACT.Sqrt, scale=-0.25).then_inc(rg_root, 1)

            act.wait_ge(y_gated, XB)
            rg_block(0, 0, True)
            rg_block(0, 1)
            with act.Fori(1, RGB // 2) as i:
                for j in range(2):
                    rg_block(i, j)

            act.wait_ge(r_ready, RGB)
            with act.Fori(0, KT // 2) as i:
                for j in range(2):
                    done_and_next(i, U_GA, 2 * j)
                    act.wait_ge(m_ready, i * 2 + (j + KT))
                    act.activation(halves(gate[:, 0, :]), outb(0), ACT.Tanh, scale=0.5).then_inc(out_free[0], 1)
                    done_and_next(i, U_GA, 2 * j + 1)

            act.wait_ge(state_kept, CONVB + RGB)
            act.wait_ge(set_ready, 3)
            for b in range(KT):
                p = b % 2
                done_and_next(0, U_WO, b) if b < RINGW else done_and_next(1, U_WO, b - RINGW)
                act.wait_ge(x2_ready, b + 1)
                act.activation(X[:, b, :], x2b[:, p, :], ACT.Copy).then_inc(out_free[p], 1)
                act.activation(sq2[b], x2b[:, p, :], ACT.Square).then_inc(sq_ready, 1)
                act.wait_ge(x2t_mm, b + 1)
                act.activation(X2T[:, 0:NCH, b * P:(b + 1) * P], ps[:, 4, :].rearrange("p (t d) -> p t d", d=P),
                               ACT.Copy).then_inc(x2t_ready, 1)
                act.activation(X2T[0:DEC, NCH, b * P:(b + 1) * P], ps[0:DEC, 5, 0:P], ACT.Copy).then_inc(x2t_ready, 1)
            act.dma_start(rows, a["rows"]).then_inc(ld_rows, 16)
            act.wait_ge(out_free[1], O_WQ // 2)
            act.wait_ge(stat_ready, 3)
            root(ps[:, 6:8, 0:HALF], halves(rs), 1.0 / D_MODEL, root_ready)
            normalised_high(1)

            def token_norms(i0, i1, base, squares):
                for i in range(i0, i1):
                    m = CH if i < NCH else DEC
                    act.activation(squares[0:m, :], X2T[0:m, i, :], ACT.Square,
                                   accum_out=fss[0:m, i:i + 1]).then_inc(ss_ready, 1)
                    act.wait_ge(ss_ready, base + i + 1)
                root(fss[:, i0:i1], fss[:, TILES + i0:TILES + i1], 1.0 / D_MODEL, ss_root)

            act.wait_ge(x2t_ready, 2 * KT)
            token_norms(0, TILES, 0, tb)

            scsv = scs.rearrange("p (q n) -> p q n", n=NKEYS)

            def keep_query(i, c):
                done_and_next(i, U_WQ, c)
                if not (isinstance(i, int) and i * RINGW + c < 2):
                    act.wait_ge(sc_mm, i * RINGW + (c - 1))
                act.activation(halves(qs[:, c % 2, :]), outb(c % 2), ACT.Copy).then_inc(q_ready, 1)

            def keep_scores(q, p):
                act.wait_ge(sc_mm, q + 1)
                for i in range(NCH):
                    ch.step(act.activation(SC[:, i * 4:(i + 1) * 4, :].rearrange("p r (k n) -> p (r k) n", n=NKEYS)[:, q, :],
                                           ps[:, 4 + p, i * NKEYS:(i + 1) * NKEYS], ACT.Copy))
                act.activation(scsv[0:DEC, q, :], ps[0:DEC, 6 + p, 0:NKEYS], ACT.Copy).then_inc(sc_ready, 1)

            def softmax_exp(h):
                act.wait_ge(fv_ready, h + 1)
                act.activation(tk_e[:], tk_fv[:], ACT.Exp, bias=tk_nm[:, 0:1], accum_out=tk_sum[:]).then_inc(ex_ready, 1)

            last_group = HS // RINGW - 1
            keep_query(0, 0)
            for c in range(1, RINGW):
                keep_query(0, c)
                keep_scores(c - 1, (c - 1) % 2)
            with act.Fori(1, last_group) as i:
                for c in range(RINGW):
                    keep_query(i, c)
                    keep_scores(i * RINGW + (c - 1), (c - 1) % 2)
            softmax_exp(0)
            for c in range(RINGW):
                keep_query(last_group, c)
                keep_scores(last_group * RINGW + c - 1, (c - 1) % 2)
            keep_scores(HS - 1, 1)

            def groups(it, j, half):
                for q in halfway(half):
                    gi = it * (SLOTS // GROUP) + (j * (TOPK // GROUP) + q + 1)
                    act.wait_ge(gl_in, gi)
                    act.activation(gth[:], g3[:], ACT.Tanh, scale=GELU_S).then_inc(gl_th, 1)
                    act.wait_ge(w_ready, gi)
                    for s in range(GROUP):
                        sl = j * TOPK + q * GROUP + s
                        if not (first_pass(it) and sl < 4):
                            act.wait_ge(slot_free, it * SLOTS + (sl - 3))
                        act.activation(diag[:, sl % 4, :], ident, ACT.Copy,
                                       scale=slot_w[:, j, q * GROUP + s:q * GROUP + s + 1]).then_inc(diag_ready, 1)

            def experts(it, last=False):
                groups(it, 0, 0)
                if not first_pass(it):
                    softmax_exp(it * 2 + 1)
                groups(it, 0, 1)
                groups(it, 1, 0)
                if last:
                    act.wait_ge(flushed, ITERS - 1)
                    token_norms(0, NCH, TILES, squares)
                else:
                    softmax_exp(it * 2 + 2)
                groups(it, 1, 1)

            squares = SC[:, 0:2, :].rearrange("p a b -> p (a b)")
            softmax_exp(1)
            experts(0)
            with act.Fori(1, ITERS - 1) as it:
                experts(it)
            experts(ITERS - 1, True)
            act.wait_ge(flushed, ITERS + 1)
            token_norms(NCH, TILES, TILES, squares)

        @block.gpsimd
        def _(pool):
            ch = Chain(pool, pool_s)
            ch.step(pool.memset(fss[:], 0.0))
            ch.step(pool.memset(cb[:, :, 0:PAD], 0.0))
            pool.memset(epst[:], EPS).then_inc(set_ready, 1)

            def low(u, slot):
                pool.wait_ge(w_hi, u + 1)
                pool.tensor_tensor(fr(wring[:, slot]), wring[:, slot], fr(whi[:, slot % 2]), ALU.subtract).then_inc(w_lo, 1)

            low(0, 0)
            low(1, 1)
            pool.wait_ge(ld_s, 16 * 3)

            def old_history(n, p, first=False):
                if not first:
                    pool.wait_ge(conv_done, n - 1)
                pool.tensor_copy(seqs(cb[:, p, :])[:, :, 0:PAD], hist[:, n, :, :]).then_inc(hist_in, 1)

            def new_history(n, p, frees, freed):
                pool.wait_ge(out_free[frees], freed)
                pool.wait_ge(hist_in, n + 1)
                ch.step(pool.tensor_copy(hist_p[:, n, :], cb[:, p, SEQ:PAD + SEQ]))
                pool.tensor_copy(hist[:, n, :, :], seqs(cb[:, p, :])[:, :, DEC_L:SEQW]).then_inc(state_kept, 1)

            def xbc_side(i, c):
                old_history(i * RINGW + c, c % 2, first_pass(i) and c < 2)
                low(i * RINGW + (U_XBC + c + 2), (c + 2) % RINGW)
                new_history(i * RINGW + c, c % 2, c % 2, i * 2 + (c // 2 + 1))

            for c in range(RINGW):
                xbc_side(0, c)
            with pool.Fori(1, CONVB // RINGW) as i:
                ch.enter(i - 1, RINGW)
                for c in range(RINGW):
                    xbc_side(i, c)
                ch.leave(CONVB // RINGW - 1)

            pool.wait_ge(xbc_ready, CONVB)
            pool.wait_ge(state_kept, CONVB)
            pool.wait_ge(dt_ready, 1)
            pool.memset(hT, 0.0).then_inc(set_ready, 1)

            def skips(c, n):
                if c >= 2:
                    pool.wait_ge(y_done, (c - 1) * NG)
                pool.tensor_tensor(xd[:, c % 2, 0:XB * n].rearrange("p (k t) -> p k t", t=n), XBC[:, 0:XB, c * CH:c * CH + n],
                                   bc(pc("ssd_d"), n), ALU.mult).then_inc(xd_ready, 1)

            def state_inputs(c, n):
                if c:
                    pool.wait_ge(s_mm, c * NG)
                pool.wait_ge(ed_ready, c + 1)
                pool.wait_ge(tr_free_x, c * 4 + 4)
                pool.tensor_tensor(xs2[0:n].rearrange("p (h d) -> p h d", d=HD), xdt[0:n].rearrange("p (h d) -> p h d", d=HD),
                                   bc(ed[0:n, :], HD), ALU.mult).then_inc(xs2_ready, 1)

            n = DEC
            skips(0, CH)
            for c in range(NCH):
                state_inputs(c, CH)
                skips(c + 1, CH if c + 1 < NCH else n)
            ch.step(pool.tensor_copy(c_s[:], XBC[:, XB + NG:CONVB, SEQ:TOK]))
            pool.tensor_tensor(dam[0:n], bc1(DA[0:n, NCH, :], DEC_B), bc(cc("bcol", n), NH), ALU.mult).then_inc(samp_ready, 1)
            state_inputs(NCH, n)
            pool.wait_ge(tr_free_b, NCH + 1)

            pool.wait_ge(dec_ready, NCH * 8 + 2)

            def sequence(i, c, first=False):
                b, j = i * RINGW + c, c % 2
                if not first:
                    pool.wait_ge(s_mm, b + (NCH * NG - 1))
                pool.tensor_tensor(bm[0:n, j, :], bt[0:n, :], cc("bcol", n).unsqueeze(2)[:, b, :].to_broadcast([n, NG * NST]),
                                   ALU.mult).then_inc(bm_ready, 1)
                pool.wait_ge(inter_mm, b + (NCH * NG + 1))
                hv = h0[:, j, :].rearrange("p (h d) -> p h d", d=HD)
                pool.tensor_tensor(hv, hv, bc(cdec[:, b, :], HD), ALU.mult).then_inc(h0_dec, 1)
                low(i * RINGW + (U_GB + c + 2), (c + 2) % RINGW)

            for i in range(DEC_B // RINGW):
                for c in range(RINGW):
                    sequence(i, c, i == 0 and c < 2)

            pool.wait_ge(hT_out, 16)

            def y_lows(half, i):
                for c in range(RINGW):
                    n = i * RINGW + (half * KT + c)
                    low(n + (U_Z + 2), (c + 2) % RINGW)
                    pool.wait_ge(y_hi, n + 1)
                    pool.tensor_tensor(fr(y_low[half][:, i * RINGW + c, :]), yf[:, c % 2, :], fr(XBC[:, n, :]),
                                       ALU.subtract).then_inc(y_gated, 1)

            for half in range(2):
                with pool.Fori(0, KT // RINGW) as i:
                    y_lows(half, i)

            def lows(u0, u1):
                with pool.Fori(0, (u1 - u0) // RINGW) as i:
                    for c in range(RINGW):
                        low(i * RINGW + (u0 + c + 2), (c + 2) % RINGW)

            lows(U_SO, U_RG)
            pool.wait_ge(ld_late, 16 * 2)
            ch.link(pool.memset(cb[:, :, 0:PAD], 0.0))

            def rg_side(i, j, first=False):
                b = i * 2 + j
                if not first:
                    pool.wait_ge(ax_mm, b - 1)
                old_history(b + CONVB, j)
                pool.tensor_copy(wax[:, j], wax_all[:, b]).then_inc(wax_ready, 1)
                low(i * RINGW + (U_RG + 2 * j + 2), (2 * j + 2) % RINGW)
                new_history(b + CONVB, j, 0, b + (O_RG // 2 + 1))
                low(i * RINGW + (U_RG + 2 * j + 3), (2 * j + 3) % RINGW)

            rg_side(0, 0, True)
            rg_side(0, 1, True)
            with pool.Fori(1, RGB // 2) as i:
                ch.enter(i - 1, 2)
                for j in range(2):
                    rg_side(i, j)
                ch.leave(RGB // 2 - 1)
            lows(U_GA, U_WO)
            pool.wait_ge(unit_done, U_WO)
            pool.memset(X2T[:, NCH, :], 0.0).then_inc(set_ready, 1)
            lows(U_WO, U_WQ)
            lows(U_WQ, UNITS - RINGW)
            low(UNITS - 2, RINGW - 2)
            low(UNITS - 1, RINGW - 1)

            def gathers(it, j):
                pool.wait_ge(idx_ready, it * 2 + (j + 1))
                for s in range(TOPK):
                    sl = j * TOPK + s
                    if first_pass(it) and sl == 2:
                        pool.wait_ge(unit_done, UNITS)
                    if not (first_pass(it) and sl < RING):
                        pool.wait_ge(slot_free, it * SLOTS + (sl - RING + 1))
                        pool.nop(nofuse=True)
                    pool.indirect_dma_start(ring[sl % RING], None, a["uv"],
                                            bass.IndirectOffsetOnAxis(ap=gidx[:, j, s:s + 1], axis=0)
                                            ).then_inc(gath[sl % RING], 16)

            for j in range(2):
                pool.wait_ge(h0_out[j], 16 * DEC_B // 2)
            gathers(0, 0)
            gathers(0, 1)
            with pool.Fori(1, ITERS) as it:
                gathers(it, 0)
                gathers(it, 1)

        @block.vector
        def _(dve):
            ch = Chain(dve, dve_s)

            def normalise(count):
                gain = "norm_mix" if count == 1 else "norm_ffn"
                dve.wait_ge(root_ready, 1 if count == 1 else 3)
                ch.link(dve.reciprocal(rs, rs))
                for k in range(KT + 1):
                    if k < KT:
                        dve.scalar_tensor_tensor(out=X[:, k, :], in0=X[:, k, :], scalar=pcol(gain, k), in1=rs,
                                                 op0=ALU.mult, op1=ALU.mult).then_inc(xn_ready, 1)
                    if k:
                        dve.wait_ge(hn_hi, (count - 1) * KT + k)
                        dve.tensor_tensor(fr(X[:, k - 1, :]), X[:, k - 1, :], fr(HN[:, k - 1, :]),
                                          ALU.subtract).then_inc(hn_ready, 1)

            ch.step(dve.memset(sp1, 0.0))
            dve.wait_ge(ld_c, 32)
            dve.wait_ge(ld_s, 16 * 3)
            ch.link(dve.tensor_copy(fr(wdt_hi), wdt))
            ch.step(dve.tensor_tensor(fr(wdt), wdt, fr(wdt_hi), ALU.subtract))
            normalise(1)
            def conv(n, p, frees, freed, weights, bias, blk, guard):
                dve.wait_ge(out_free[frees], freed)
                dve.wait_ge(hist_in, n + 1)
                if guard is not None:
                    dve.wait_ge(*guard)
                row, o = cb[:, p, :], acc[:, p, 0:CONVN]
                ch.link(dve.tensor_scalar(o, row[:, PAD:CBW], pcol(weights, blk, PAD), pcol(bias, blk), ALU.mult, ALU.add))
                for k in range(PAD - 1, -1, -1):
                    ch.link(dve.scalar_tensor_tensor(out=o, in0=row[:, k:k + CONVN], scalar=pcol(weights, blk, k), in1=o,
                                                     op0=ALU.mult, op1=ALU.add))
                dve.tensor_copy(acc[:, p, SEQ:TOK].rearrange("p (b l) -> p b l", l=DEC_L),
                                seqs(acc[:, p, :])[:, :, 0:DEC_L]).then_inc(conv_done, 1)

            conv(0, 0, 0, 1, "conv_w", "conv_b", 0, None)
            conv(1, 1, 1, 1, "conv_w", "conv_b", 1, None)
            dve.wait_ge(dt_mm, 1)
            ch.wait()
            nt = NCH * NH
            ch.step(dve.tensor_tensor(sp1[:, 0:nt].rearrange("p (t h) -> p t h", h=NH),
                                      ps[:, 5, 0:nt].rearrange("p (t h) -> p t h", h=NH), bc1(pc("dt_bias"), NCH), ALU.add))
            ch.step(dve.tensor_tensor(sp1[0:DEC, nt:nt + NH], ps[0:DEC, 5, nt:nt + NH], pc("dt_bias")[0:DEC, :], ALU.add))
            ch.link(dve.tensor_scalar(sp1[:, nt + NH:168], pc("rg_lam"), -1.0, None, ALU.mult))
            ch.link(dve.tensor_scalar(sp3, sp1, -1.0, None, ALU.mult))
            dve.tensor_tensor(sp3, sp3, sp1, ALU.min).then_inc(sp_in, 1)
            dve.wait_ge(sp_in, 1)
            dve.wait_ge(sp_exp, 2)
            ch.step(dve.tensor_scalar(sp1, sp1, 0.0, None, ALU.max))
            ch.link(dve.tensor_scalar(sp3, sp2, 2.0, None, ALU.add))
            ch.link(dve.reciprocal(sp3, sp3))
            ch.link(dve.tensor_tensor(sp2, sp2, sp3, ALU.mult))
            ch.link(dve.tensor_tensor(sp3, sp2, sp2, ALU.mult))
            ch.link(dve.tensor_scalar(sp4, sp3, 1.0 / 21, None, ALU.mult))
            for d in range(19, 1, -2):
                ch.link(dve.scalar_tensor_tensor(out=sp4, in0=sp4, scalar=1.0 / d, in1=sp3, op0=ALU.add, op1=ALU.mult))
            ch.link(dve.scalar_tensor_tensor(out=sp4, in0=sp4, scalar=1.0, in1=sp2, op0=ALU.add, op1=ALU.mult))
            ch.link(dve.scalar_tensor_tensor(out=sp4, in0=sp4, scalar=2.0, in1=sp1, op0=ALU.mult, op1=ALU.add))
            spt = sp4[:, 0:TILES * NH].rearrange("p (t h) -> p t h", h=NH)
            ch.step(dve.tensor_copy(DT[:], spt))
            ch.step(dve.scalar_tensor_tensor(out=DA[:], in0=spt, scalar=-1.0, in1=bc1(ea_log[:], TILES),
                                             op0=ALU.mult, op1=ALU.mult))
            ch.step(dve.tensor_scalar(ca[:], sp4[:, TILES * NH:168], -4.0, None, ALU.mult))
            ch.step(dve.tensor_scalar(half_b[:, 0:RGB], pc("rg_ba"), 0.5, None, ALU.mult))
            dve.tensor_scalar(half_b[:, RGB:2 * RGB], pc("rg_bx"), 0.5, None, ALU.mult).then_inc(dt_ready, 1)

            with dve.Fori(1, CONVB // 2) as i:
                ch.enter(i - 1, 8)
                for j in range(2):
                    n = i * 2 + j
                    conv(n, j, j, i + 1, "conv_w", "conv_b", n, (xbc_ready, i * 2 + (j - 1)))
                ch.leave(CONVB // 2 - 1)

            def ssd_chunk(c, first):
                dve.wait_ge(small_mm, c + 1)
                if not first:
                    dve.wait_ge(dec_ready, c * 8)
                    dve.wait_ge(ed_ready, c)
                ch.link(dve.tensor_scalar(nac[:], ps[:, 5, 0:NH], -1.0, None, ALU.mult))
                dve.tensor_tensor(el[:], ps[:, 5, NH:2 * NH], nac[:], ALU.add).then_inc(small_sb, 1)

                def segments(hb):
                    dve.wait_ge(ab_mm, c * 8 + (hb + 1))
                    if not (first and hb < 2):
                        dve.wait_ge(dec_ready, c * 8 + (hb - 1))
                    dve.tensor_tensor(seg[:, hb % 2, :].rearrange("p (k t) -> p k t", t=CH),
                                      ps[:, hb % 2, :].rearrange("p (k t) -> p k t", t=CH), bc1(cc("mneg"), 4),
                                      ALU.add).then_inc(seg_ready, 1)

                def weights(hb):
                    if hb == 0:
                        dve.wait_ge(cb_sb, c + 1)
                    dve.wait_ge(dec_ready, c * 8 + (hb + 1))
                    if not (first and hb < 2):
                        dve.wait_ge(intra_mm, c * 8 + (hb - 1))
                    dve.tensor_tensor(wgt[:, hb % 2, :].rearrange("p (k t) -> p k t", t=CH),
                                      dec[:, hb % 2, :].rearrange("p (k t) -> p k t", t=CH), bc1(cbs[:, hb // 2, :], 4),
                                      ALU.mult).then_inc(wgt_ready, 1)

                def scaled_x(b):
                    dve.wait_ge(tr_mm, c * 5 + (b + 1))
                    if b == 0 and not first:
                        dve.wait_ge(intra_mm, c * 8)
                        dve.wait_ge(xs2_ready, c)
                    dve.tensor_tensor(xdt[:, b * 512:(b + 1) * 512].rearrange("p (h d) -> p h d", d=HD),
                                      ps[:, 6 if b % 2 == 0 else 3, :].rearrange("p (h d) -> p h d", d=HD),
                                      bc(DT[:, c, 8 * b:8 * b + 8], HD), ALU.mult).then_inc(tr_free_x, 1)

                segments(0)
                scaled_x(0)
                scaled_x(1)
                segments(1)
                scaled_x(2)
                scaled_x(3)
                for g in range(NG):
                    weights(2 * g)
                    if g + 1 < NG:
                        segments(2 * g + 2)
                    weights(2 * g + 1)
                    if g + 1 < NG:
                        segments(2 * g + 3)
                    dve.wait_ge(eas_ready, c * NG + (g + 1))
                    dve.wait_ge(inter_mm, c * NG + (g + 1))
                    if not (first and g == 0):
                        dve.wait_ge(y_done, c * NG + g)
                    dve.tensor_tensor(yt, ps[:, 3, :], eas, ALU.mult).then_inc(inter_read, 1)
                    dve.wait_ge(inter_read, c * NG + (g + 1))
                    dve.wait_ge(intra_mm, c * 8 + (2 * g + 2))
                    dve.tensor_tensor(yt, ps[:, 2, :], yt, ALU.add).then_inc(intra_read, 1)
                    dve.wait_ge(intra_read, c * NG + (g + 1))
                    dve.wait_ge(xd_ready, c + 1)
                    dve.tensor_tensor(XBC[:, 4 * g:4 * g + 4, c * CH:(c + 1) * CH],
                                      yt.rearrange("p (k t) -> p k t", t=CH),
                                      xd[:, c % 2, 512 * g:512 * (g + 1)].rearrange("p (k t) -> p k t", t=CH),
                                      ALU.add).then_inc(y_done, 1)
                    dve.wait_ge(s_mm, c * NG + (g + 1))
                    hg = hT[:, g * 512:(g + 1) * 512]
                    ch.link(dve.tensor_tensor(hg.rearrange("p (h d) -> p h d", d=HD), hg.rearrange("p (h d) -> p h d", d=HD),
                                              bc(cdec[:, 0, 8 * g:8 * g + 8], HD), ALU.mult))
                    dve.tensor_tensor(hg, ps[:, 7, :], hg, ALU.add).then_inc(h_done, 1)

            dve.wait_ge(state_kept, CONVB)
            dve.wait_ge(xbc_ready, CONVB)
            dve.wait_ge(set_ready, 2)
            for c in range(NCH):
                ssd_chunk(c, c == 0)
            n = DEC
            dve.wait_ge(small_mm, NCH + 1)
            dve.wait_ge(dec_ready, NCH * 8)
            ch.link(dve.tensor_scalar(nac[0:n, :], ps[0:n, 5, 0:NH], -1.0, None, ALU.mult))
            dve.tensor_tensor(el[0:n, :], ps[0:n, 5, NH:2 * NH], nac[0:n, :], ALU.add).then_inc(small_sb, 1)
            for hb in range(2):
                sv = seg[0:n, hb, :].rearrange("p (k t) -> p k t", t=n)
                dve.wait_ge(ab_mm, NCH * 8 + hb + 1)
                ch.link(dve.tensor_tensor(sv, ps[0:n, hb, :].rearrange("p (k t) -> p k t", t=n), bc1(cc("mneg_s", n), 16),
                                          ALU.add))
                dve.tensor_tensor(sv, sv, bc(nac[0:n, 16 * hb:16 * hb + 16], n), ALU.add).then_inc(seg_ready, 1)
            for b in range(4):
                dve.wait_ge(tr_mm, NCH * 5 + b + 1)
                if b == 0:
                    dve.wait_ge(intra_mm, NCH * 8)
                    dve.wait_ge(xs2_ready, NCH)
                dve.tensor_tensor(xdt[0:n, b * 512:(b + 1) * 512].rearrange("p (h d) -> p h d", d=HD),
                                  ps[0:n, 6 if b % 2 == 0 else 3, :].rearrange("p (h d) -> p h d", d=HD),
                                  bc(DT[0:n, NCH, 8 * b:8 * b + 8], HD), ALU.mult).then_inc(tr_free_x, 1)
            dve.wait_ge(cb_sb, NCH + 1)
            for hb in range(2):
                dve.wait_ge(dec_ready, NCH * 8 + hb + 1)
                for k in range(2):
                    g = 2 * hb + k
                    last = dve.tensor_tensor(wgt[0:n, hb, k * 256:(k + 1) * 256].rearrange("p (k t) -> p k t", t=n),
                                             dec[0:n, hb, k * 256:(k + 1) * 256].rearrange("p (k t) -> p k t", t=n),
                                             bc1(cbs[0:n, 0, g * n:(g + 1) * n], 8), ALU.mult)
                    if k == 0:
                        ch.step(last)
                last.then_inc(wgt_ready, 1)

            def new_state(b, j):
                dve.wait_ge(h0_dec, b + 1)
                dve.wait_ge(s_mm, b + (NCH * NG + 1))
                hv = h0[:, j, :].rearrange("p (g d) -> p g d", d=512)
                dve.tensor_tensor(hv, ps[:, 4:8, :], hv, ALU.add).then_inc(h_done, 1)

            with dve.Fori(0, DEC_B // 2) as i:
                for j in range(2):
                    new_state(i * 2 + j, j)
            dve.wait_ge(inter_mm, NCH * NG + DEC_B)
            dve.wait_ge(eas_ready, NCH * NG + 1)
            dve.wait_ge(intra_mm, NCH * 8 + 2)
            dve.wait_ge(xd_ready, NCH + 1)
            ch.link(dve.tensor_tensor(yt, ps[:, 3, :], eas, ALU.mult))
            ch.link(dve.tensor_tensor(yt, ps[:, 2, :], yt, ALU.add))
            dve.tensor_tensor(XBC[:, 0:XB, SEQ:TOK], yt.rearrange("p (k t) -> p k t", t=n),
                              xd[:, NCH % 2, 0:XB * n].rearrange("p (k t) -> p k t", t=n),
                              ALU.add).then_inc(y_done, 1)
            dve.wait_ge(y_done, NCH * NG + 1)
            dve.wait_ge(hT_out, 16)

            ch.link(dve.memset(ssq, 0.0))

            def gated(i, j, first=False):
                b = i * 2 + j
                dve.wait_ge(out_free[j], i + (O_Z // 2 + 1))
                if not first:
                    dve.wait_ge(yg_sq, b - 1)
                    dve.wait_ge(y_gated, b - 1)
                dve.tensor_tensor(tt[:, j, :], gate[:, j, :], XBC[:, b, :], ALU.mult).then_inc(yg_ready, 1)
                dve.wait_ge(yg_ready, b + 1)
                dve.tensor_scalar(yf[:, j, :], tt[:, j, :], pcol("ssd_norm", b), None, ALU.mult).then_inc(yf_ready, 1)

            def square_sum(b, j):
                dve.wait_ge(yg_sq, b + 1)
                dve.tensor_tensor(ssq, ssq, acc[:, j, 0:TOK], ALU.add).then_inc(ssq_ready, 1)
                dve.wait_ge(ssq_ready, b + 1)

            gated(0, 0, True)
            gated(0, 1, True)
            square_sum(0, 0)
            with dve.Fori(1, XB // 2) as i:
                for j in range(2):
                    gated(i, j)
                    square_sum(i * 2 + (j - 1), (j - 1) % 2)
            square_sum(XB - 1, 1)
            dve.wait_ge(root_ready, 2)
            ch.link(dve.reciprocal(rs, rs))
            dve.wait_ge(gb_read, KT)
            with dve.Fori(0, KT // 2) as i:
                for j in range(2):
                    b = i * 2 + j
                    dve.wait_ge(unit_done, i * 4 + (U_SO + 2 * j + 2))
                    dve.scalar_tensor_tensor(out=halves(M[:, b, :]), in0=halves(M[:, b, :]), scalar=1.0, in1=outb(j),
                                             op0=ALU.add, op1=ALU.mult).then_inc(out_free[j], 1)
                    dve.wait_ge(out_free[j], i + (O_SO // 2 + 1))
                    dve.tensor_tensor(M[:, b, :], M[:, b, :], rs, ALU.mult).then_inc(m_ready, 1)

            def rg_conv(b, j, guard):
                conv(b + CONVB, j, 0, b + (O_RG // 2 + 1), "rg_conv_w", "rg_conv_b", b, guard)

            def rg_arguments(b, j):
                dve.wait_ge(g_in, b + 1)
                ch.link(dve.tensor_scalar(rg_g3, rg_g2[:, j, :], GELU_C, 1.0, ALU.mult, ALU.add))
                dve.tensor_tensor(rg_g3, rg_g3, rg_g[:, j, :], ALU.mult).then_inc(g_u, 1)
                dve.wait_ge(rg_at, b + 1)
                ch.link(dve.tensor_tensor(tt[:, 0, :], rg_a, rg_a, ALU.mult))
                dve.scalar_tensor_tensor(out=tt[:, 0, :], in0=tt[:, 0, :], scalar=1.0, in1=rg_q,
                                         op0=ALU.add, op1=ALU.mult).then_inc(rg_arg, 1)

            def rg_states(b, j):
                dve.wait_ge(conv_done, b + (CONVB + 1))
                ch.link(dve.scalar_tensor_tensor(out=tt[:, 1, :], in0=rg_ti, scalar=1.0, in1=acc[:, j, 0:TOK],
                                                 op0=ALU.add, op1=ALU.mult))
                dve.wait_ge(rg_root, b + 1)
                ch.link(dve.tensor_tensor(tt[:, 1, :], tt[:, 1, :], rg_q, ALU.mult))
                a0 = rg_a[:, SEQ:TOK].rearrange("p (b l) -> p b l", l=DEC_L)[:, :, 0]
                b0 = tt[:, 1, SEQ:TOK].rearrange("p (b l) -> p b l", l=DEC_L)[:, :, 0]
                ch.link(dve.tensor_tensor(tt[:, 0, 0:DEC_B], a0, rgh0[:, b, :], ALU.mult))
                ch.link(dve.tensor_tensor(b0, b0, tt[:, 0, 0:DEC_B], ALU.add))
                ch.link(dve.memset(a0, 0.0))
                dve.tensor_tensor_scan(rg_h, rg_a, tt[:, 1, :], 0.0, ALU.mult, ALU.add).then_inc(rg_scanned, 1)
                dve.wait_ge(rg_scanned, b + 1)
                ch.step(dve.tensor_copy(rgho[:, b, 0:1], rg_h[:, SEQ - 1:SEQ]))
                ch.step(dve.tensor_copy(rgho[:, b, 1:1 + DEC_B],
                                        rg_h[:, SEQ:TOK].rearrange("p (b l) -> p b l", l=DEC_L)[:, :, DEC_L - 1]))
                dve.wait_ge(g_th, b + 1)
                ch.link(dve.scalar_tensor_tensor(out=tt[:, 0, :], in0=rg_g2[:, j, :], scalar=1.0, in1=rg_g[:, j, :],
                                                 op0=ALU.add, op1=ALU.mult))
                ch.link(dve.tensor_tensor(tt[:, 0, :], tt[:, 0, :], rg_h, ALU.mult))
                ch.link(dve.tensor_scalar(fr(R[:, b, :]), tt[:, 0, :], 1.0, None, ALU.mult))
                dve.tensor_tensor(fr(r_low[:, b, :]), tt[:, 0, :], fr(R[:, b, :]), ALU.subtract).then_inc(r_ready, 1)

            def rg_block(b, j, guard):
                rg_arguments(b, j)
                rg_conv(b + 1, 1 - j, guard)
                rg_states(b, j)

            dve.wait_ge(m_ready, KT)
            rg_conv(0, 0, None)
            rg_block(0, 0, None)
            rg_block(1, 1, (ax_mm, 1))
            with dve.Fori(1, RGB // 2 - 1) as i:
                ch.enter(i - 1, 2 * 16)
                for j in range(2):
                    rg_block(i * 2 + j, j, (ax_mm, i * 2 + j))
                ch.leave(RGB // 2 - 2)
            rg_block(RGB - 2, 0, (ax_mm, RGB - 2))
            rg_arguments(RGB - 1, 1)
            rg_states(RGB - 1, 1)
            dve.wait_ge(r_ready, RGB)
            with dve.Fori(0, KT) as b:
                ch.enter(b, 2)
                dve.wait_ge(out_free[0], b + (O_GA // 2 + 1))
                dve.wait_ge(unit_done, b * 2 + (U_GA + 2))
                dve.scalar_tensor_tensor(out=halves(tt[:, 0, :]), in0=halves(gate[:, 0, :]), scalar=1.0, in1=outb(1),
                                         op0=ALU.add, op1=ALU.mult).then_inc(out_free[1], 1)
                dve.wait_ge(out_free[1], b + (O_GA // 2 + 1))
                ch.link(dve.scalar_tensor_tensor(out=tt[:, 1, :], in0=tt[:, 0, :], scalar=0.5, in1=M[:, b, :],
                                                 op0=ALU.mult, op1=ALU.add))
                ch.link(dve.tensor_scalar(fr(M[:, b, :]), tt[:, 1, :], 1.0, None, ALU.mult))
                dve.tensor_tensor(fr(m_low[:, b, :]), tt[:, 1, :], fr(M[:, b, :]), ALU.subtract).then_inc(m_ready, 1)
                dve.wait_ge(m_ready, b + (KT + 1))
                ch.leave(KT)
            dve.wait_ge(ld_x, 16)
            for b in range(KT):
                p = b % 2
                dve.wait_ge(unit_done, U_WO + b + 1)
                if b >= 2:
                    dve.wait_ge(out_free[p], (O_WO + b) // 2)
                    dve.wait_ge(sq_ready, 4 + b - 1)
                    dve.wait_ge(x2t_mm, b - 1)
                dve.scalar_tensor_tensor(out=halves(x2b[:, p, :]), in0=outb(p), scalar=0.5, in1=halves(X[:, b, :]),
                                         op0=ALU.mult, op1=ALU.add).then_inc(x2_ready, 1)
            normalise(2)
            dve.wait_ge(ss_root, 1)
            dve.wait_ge(ld_rows, 16)
            ch.link(dve.reciprocal(fss[:, TILES:2 * TILES], fss[:, TILES:2 * TILES]))
            for i in range(TILES):
                m = CH if i < NCH else DEC
                last = dve.scalar_tensor_tensor(out=H2T[:, i, :] if i < NCH else h2s[0:m, :], in0=X2T[0:m, i, :],
                                                scalar=fss[0:m, TILES + i:TILES + i + 1], in1=rows[0:m, 0, :],
                                                op0=ALU.mult, op1=ALU.mult)
                if i < NCH:
                    ch.step(last)
            last.then_inc(h2t_ready, 1)

            SCh = SC.rearrange("p t (j s n) -> p t j s n", j=2, n=NKEYS)

            def apart():
                dve.nop(nofuse=True)

            def top16(vals, idxs, src, src2):
                apart()
                ch.link(dve.max(vals[:, 0:8], src))
                apart()
                ch.step(dve.max_index(idxs[:, 0:8], vals[:, 0:8], src))
                ch.link(dve.match_replace(src2, vals[:, 0:8], src, LOWEST))
                apart()
                ch.link(dve.max(vals[:, 8:16], src2))
                apart()
                ch.link(dve.max_index(idxs[:, 8:16], vals[:, 8:16], src2))

            def route(it, j, h):
                ch.link(dve.tensor_copy(tk_s, SCh[:, it, j]))
                for s in range(2):
                    top16(tk_v[:, s, :], tk_i[:, s, :], tk_s[:, s, :], tk_s2[:, s, :])
                ch.step(dve.tensor_copy(tk_if[:], tk_i[:]))
                ch.link(dve.tensor_tensor(tk_c.rearrange("p (a b) -> p a b", b=TOPK), bc(tk_v[:, 0, :], TOPK),
                                          bc1(tk_v[:, 1, :], TOPK), ALU.add))
                top16(tk_fv[:], tk_fi[:], tk_c, tk_c2[:])
                dve.tensor_scalar(tk_nm[:], tk_fv[:, 0:1], -1.0, None, ALU.mult).then_inc(fv_ready, 1)
                ch.step(dve.tensor_scalar(tk_ab[:, 0, :], tk_fi[:], 4, None, ALU.logical_shift_right))
                ch.link(dve.tensor_scalar(tk_ab[:, 1, :], tk_fi[:], 15, None, ALU.bitwise_and))
                ch.link(dve.tensor_copy(tk_abf[:], tk_ab[:]))
                ch.link(dve.tensor_tensor(tk_eq, bc(tk_abf[:].rearrange("p s k -> p (s k)"), TOPK),
                                          bc1(cc("iota"), 2 * TOPK), ALU.is_equal))
                for s in range(2):
                    ev = tk_eq[:, s * TOPK:(s + 1) * TOPK, :]
                    ch.step(dve.tensor_tensor(ev, ev, bc1(tk_if[:, s, :], TOPK), ALU.mult))
                ch.wait()
                ch.link(dve.tensor_reduce(tk_sel[:].rearrange("p s k -> p (s k)"), tk_eq, AX_X, ALU.add))
                dve.scalar_tensor_tensor(out=gidx[:, j, :], in0=tk_sel[:, 0, :], scalar=float(NKEYS), in1=tk_sel[:, 1, :],
                                         op0=ALU.mult, op1=ALU.add).then_inc(idx_ready, 1)
                dve.wait_ge(ex_ready, h + 1)
                ch.link(dve.reciprocal(tk_r[:], tk_sum[:]))
                ch.link(dve.tensor_scalar(gw[:, j, :], tk_e[:], tk_r[:, 0:1], 0.5, ALU.mult, ALU.mult))

            ROUTE = 27

            def slots(it, j, half):
                for q in halfway(half):
                    gi = it * (SLOTS // GROUP) + (j * (TOPK // GROUP) + q + 1)
                    for s in range(GROUP):
                        k = q * GROUP + s
                        sl = j * TOPK + k
                        dve.wait_ge(gath[sl % RING], it * 64 + (sl // RING + 1) * 16)
                        u = ring[sl % RING][:, 0:D_MODEL]
                        ch.step(dve.tensor_tensor_reduce(out=u, in0=u, in1=tb, scale=1.0, scalar=0.0, op0=ALU.mult,
                                                         op1=ALU.add, accum_out=act_z[:, j, k:k + 1]))
                    ch.wait()
                    z = act_z[:, j, q * GROUP:(q + 1) * GROUP]
                    ch.link(dve.tensor_tensor(g1[:], z, z, ALU.mult))
                    ch.link(dve.tensor_scalar(g1[:], g1[:], GELU_C, 1.0, ALU.mult, ALU.add))
                    dve.tensor_tensor(g3[:], g1[:], z, ALU.mult).then_inc(gl_in, 1)
                    dve.wait_ge(gl_th, gi)
                    ch.link(dve.scalar_tensor_tensor(out=g1[:], in0=gth[:], scalar=1.0, in1=z, op0=ALU.add, op1=ALU.mult))
                    dve.tensor_tensor(slot_w[:, j, q * GROUP:(q + 1) * GROUP], g1[:], gw[:, j, q * GROUP:(q + 1) * GROUP],
                                      ALU.mult).then_inc(w_ready, 1)

            SLOTC = (TOPK // GROUP) * (GROUP + 3)

            def flush(it, tile):
                dve.wait_ge(slot_free, it * SLOTS)
                y = X2T[:, tile, :].rearrange("p (h d) -> p h d", h=2)
                dve.tensor_tensor(y, ps[:, 0:2, :], y, ALU.add).then_inc(flushed, 1)

            dve.wait_ge(sc_ready, 2)
            route(0, 0, 0)
            dve.wait_ge(sc_ready, 4)
            route(0, 1, 1)
            dve.wait_ge(h2s_moved, 64)

            def iteration(it, tile, prev_tile, last=False):
                ch.link(dve.tensor_copy(tb, H2T[:, tile, :]))
                if prev_tile is not None:
                    flush(it, prev_tile)
                slots(it, 0, 0)
                if prev_tile is not None:
                    route(it, 1, it * 2 + 1)
                slots(it, 0, 1)
                slots(it, 1, 0)
                if last:
                    final_norm(0, NCH, 2)
                else:
                    route(it + 1, 0, it * 2 + 2)
                slots(it, 1, 1)

            def final_norm(i0, i1, roots):
                m = CH if i0 < NCH else DEC
                dve.wait_ge(ss_root, roots)
                ch.link(dve.reciprocal(fss[:, TILES + i0:TILES + i1], fss[:, TILES + i0:TILES + i1]))
                for i in range(i0, i1):
                    dve.scalar_tensor_tensor(out=X2T[0:m, i, :], in0=X2T[0:m, i, :],
                                             scalar=fss[0:m, TILES + i:TILES + i + 1],
                                             in1=rows[0:m, 1, :], op0=ALU.mult, op1=ALU.mult).then_inc(fin_ready, 1)

            dve.wait_ge(sc_ready, HS)
            iteration(0, 0, None)
            dve.wait_ge(sc_moved, 64)
            with dve.Fori(1, ITERS - 1) as it:
                ch.enter(it - 1, 1 + 2 * (ROUTE + SLOTC))
                iteration(it, it // 4, (it - 1) // 4)
                ch.leave(ITERS - 2)
            iteration(ITERS - 1, NCH, NCH - 1, True)
            flush(ITERS, NCH)
            dve.wait_ge(fin_mm, 1)
            dve.tensor_copy(X2T[0:DEC, NCH, :].rearrange("p (h d) -> p h d", h=2), ps[0:DEC, 2:4, :]).then_inc(flushed, 1)
            final_norm(NCH, TILES, 3)


def _blocks(w, kb):
    i, o = w.shape
    return w.reshape(i // P // kb, kb, P, o // P, P).transpose(3, 0, 2, 1, 4)


def _chan(v):
    v = np.asarray(v)
    r = v.reshape(v.shape[:-1] + (v.shape[-1] // P, P))
    return np.moveaxis(np.moveaxis(r, -1, 0), -1, 1)


def _constants():
    c = np.zeros((P, NCON), np.float32)

    def put(name, v):
        o, w = CCOL[name]
        c[:v.shape[0], o:o + w] = v

    i, s = np.arange(P), np.arange(DEC)
    same = s[:, None] // DEC_L == s[None, :] // DEC_L
    put("ident", np.eye(P))
    put("tri", i[:, None] <= i[None, :])
    put("mneg", np.where(i[:, None] <= i[None, :], 0.0, NEG))
    put("ones", np.ones((P, P)))
    put("tri_s", same & (s[:, None] <= s[None, :]))
    put("mneg_s", np.where(same & (s[:, None] <= s[None, :]), 0.0, NEG))
    put("blk_s", same)
    put("bcol", s[:, None] // DEC_L == np.arange(DEC_B)[None, :])
    put("sel", i[:, None] % DEC == s[None, :])
    put("iota", np.broadcast_to(np.arange(TOPK), (P, TOPK)))
    return c


def kernel(**inputs):
    import concourse.bacc as bacc
    from concourse.bass_utils import run_bass_kernel_spmd

    g = {k: np.asarray(v) for k, v in inputs.items()}
    x = np.concatenate([g["x_prompt"][0], g["x_sample"].reshape(DEC, D_MODEL)], 0)
    w_in = g["w_in"][0]
    cuts = np.cumsum([0, RGB * P, RGB * P, INNER, CONVB * P, NH, D_MODEL, D_MODEL])
    rgx, rgg, z, xbc, dt, ga, gb = (w_in[:, cuts[i]:cuts[i + 1]] for i in range(7))
    b1 = {k: _blocks(v, KT)[:, 0] for k, v in dict(
        rgx=rgx, rgg=rgg, z=z, xbc=xbc, ga=ga, gb=gb, rgo=g["w_rg_out"][0], wo=g["w_out"][0], wq=g["peer_wq"][0]).items()}
    so = _blocks(g["w_ssd_out"][0], KT).reshape(2 * KT, P, KT, P)
    rg = np.stack([b1["rgx"], b1["rgg"]], 1).reshape(2 * KT, P, KT, P)
    gr = np.stack([b1["ga"], b1["rgo"]], 1).reshape(2 * KT, P, KT, P)
    arrays = {
        "wstream": np.concatenate([b1["xbc"], b1["gb"], b1["z"], so, rg, gr, b1["wo"], b1["wq"]], 0),
        "x": _chan(x),
        "consts": _constants(),
        "wdt": dt.reshape(KT, P, NH).transpose(1, 0, 2),
        "wax": np.stack([g["rg_wa"][0], g["rg_wx"][0]], 1).transpose(2, 0, 1, 3),
        "keys": g["peer_keys"][0].reshape(HS, NKEYS, P).transpose(2, 0, 1),
        "hist": np.concatenate([_chan(g["state_ssd_conv"][0]), _chan(g["state_rg_conv"][0])], 1),
        "rgh0": _chan(g["state_rg_h"][0]),
        "sample_h_in": g["state_ssd_h"][0].reshape(DEC_B, INNER, NST).transpose(0, 2, 1),
        "rows": np.broadcast_to(np.stack([g["norm_ffn"][0], g["norm_final"]]), (P, 2, D_MODEL)),
        "uv": np.concatenate([g["peer_u"][0], g["peer_v"][0]], 1),
    }
    par = {
        "norm_mix": _chan(g["norm_mix"][0]), "norm_ffn": _chan(g["norm_ffn"][0]), "ssd_norm": _chan(g["ssd_norm"][0]),
        "ssd_d": _chan(np.repeat(g["ssd_d"][0], HD)),
        "conv_w": _chan(g["ssd_conv_w"][0]), "conv_b": _chan(g["ssd_conv_b"][0]),
        "rg_conv_w": _chan(g["rg_conv_w"][0]), "rg_conv_b": _chan(g["rg_conv_b"][0]),
        "rg_ba": _chan(g["rg_ba"][0]), "rg_bx": _chan(g["rg_bx"][0]), "rg_lam": _chan(g["rg_lam"][0]),
        "dt_bias": np.broadcast_to(g["ssd_dt_bias"][0], (P, NH)), "a_log": np.broadcast_to(g["ssd_a_log"][0], (P, NH)),
    }
    arrays["params"] = np.concatenate([par[n].reshape(P, -1) for n, _ in _PARAMS], 1)

    outs = {"y_prompt": (SEQ, D_MODEL), "y_sample": (DEC, D_MODEL), "hist_s": (P, CONVB + RGB, DEC_B * PAD),
            "hist_p": (P, CONVB + RGB, PAD),
            "rgho": (P, RGB, 1 + DEC_B), "prompt_h": (P, INNER), "sample_h_out": (DEC_B, P, INNER)}
    nc = bacc.Bacc("TRN2", target_bir_lowering=False, num_devices=1)
    aps = {}
    for k, v in arrays.items():
        arrays[k] = np.ascontiguousarray(v)
        aps[k] = nc.dram_tensor("in_" + k, v.shape, F32, kind="ExternalInput").ap()
    for k, s in outs.items():
        aps[k] = nc.dram_tensor("out_" + k, s, F32, kind="ExternalOutput").ap()
    hybrid_layer(nc, aps)
    r = run_bass_kernel_spmd(nc, [{"in_" + k: v for k, v in arrays.items()}], core_ids=[0]).results[0]
    o = {k: np.asarray(r["out_" + k]) for k in outs}

    def unchan(v):
        return np.moveaxis(np.moveaxis(v, 0, -1), 0, -2).reshape(v.shape[2:] + (-1,))

    hists, rgh = np.concatenate([unchan(o["hist_p"]), unchan(o["hist_s"])], 0), unchan(o["rgho"])
    ssd_c, rg_c = hists[:, :CONVB * P], hists[:, CONVB * P:]
    return (
        o["y_prompt"][None], o["y_sample"].reshape(DEC_B, DEC_L, D_MODEL),
        rgh[None, 0:1], rg_c[None, None, 0:PAD],
        o["prompt_h"].T.reshape(1, 1, NH, HD, NST), ssd_c[None, None, 0:PAD],
        rgh[None, 1:], rg_c[PAD:].reshape(1, DEC_B, PAD, -1),
        o["sample_h_out"].transpose(0, 2, 1).reshape(1, DEC_B, NH, HD, NST), ssd_c[PAD:].reshape(1, DEC_B, PAD, -1),
    )
```
